# Optimizing a Trainium2 kernel written in Bass

```python
import math
import jax
import jax.numpy as jnp
from jax import lax
import numpy as np

D_MODEL = 1024
BATCH = 1
SEQ = 512
DEPTH = 1

N_MIXERS = 4
N_SSD_LAYERS = (DEPTH + N_MIXERS - 1) // N_MIXERS
N_GLA_LAYERS = (DEPTH + N_MIXERS - 2) // N_MIXERS
N_RWKV_LAYERS = (DEPTH + N_MIXERS - 3) // N_MIXERS
N_S5_LAYERS = (DEPTH + N_MIXERS - 4) // N_MIXERS

DEEPNORM_ALPHA = (2 * DEPTH) ** 0.25
DEEPNORM_BETA = (8 * DEPTH) ** -0.25
LN_EPS = 1e-5
RMS_EPS = 1e-5

SSD_D_INNER = 2 * D_MODEL
SSD_HEAD_DIM = 64
SSD_N_HEADS = SSD_D_INNER // SSD_HEAD_DIM
SSD_N_GROUPS = 4
SSD_D_STATE = 128
SSD_CONV = 4
SSD_CHUNK = 64
SSD_CONV_DIM = SSD_D_INNER + 2 * SSD_N_GROUPS * SSD_D_STATE
SSD_IN_DIM = SSD_D_INNER + SSD_CONV_DIM + SSD_N_HEADS

GLA_N_HEADS = 4
GLA_D_K = D_MODEL // 2
GLA_D_V = D_MODEL
GLA_GATE_RANK = 16
GLA_TAU = 16.0
GLA_CHUNK = 64
GLA_IN_DIM = 2 * GLA_D_K + 2 * GLA_D_V + GLA_GATE_RANK

RWKV_HEAD_DIM = 64
RWKV_N_HEADS = D_MODEL // RWKV_HEAD_DIM
RWKV_DECAY_LORA = 64
RWKV_A_LORA = 64
RWKV_GATE_LORA = 160
RWKV_GN_EPS = 64e-5

S5_GROUP = 16
S5_N_GROUPS = D_MODEL // S5_GROUP
S5_STATE = 64

N_EXPERTS = 16
N_EXPERT_GROUPS = 4
EXPERTS_PER_GROUP = N_EXPERTS // N_EXPERT_GROUPS
TOP_K = 2
D_EXPERT = D_MODEL
MOE_BLOCK = 128

kernel_name = 'hybrid_ssd_gla_rwkv7_s5_moe_deepnorm'

def layer_norm(x, g, b):
    xf = x.astype(jnp.float32)
    mu = jnp.mean(xf, -1, keepdims=True)
    var = jnp.mean(jnp.square(xf - mu), -1, keepdims=True)
    return ((xf - mu) * lax.rsqrt(var + LN_EPS) * g + b).astype(x.dtype)

def rms_norm_f32(y, eps):
    return y * lax.rsqrt(jnp.mean(jnp.square(y), -1, keepdims=True) + eps)

def token_shift(h):
    return jnp.pad(h, ((0, 0), (1, 0), (0, 0)))[:, :-1]

def causal_depthwise_conv(x, w, b):
    k = w.shape[0]
    y = lax.conv_general_dilated(x, w[:, None, :], window_strides=(1,), padding=[(k - 1, 0)],
                                 dimension_numbers=('NWC', 'WIO', 'NWC'),
                                 feature_group_count=x.shape[-1])
    return y + b

def to_chunks(t, chunk):
    b, s = t.shape[:2]
    return jnp.moveaxis(t.reshape((b, s // chunk, chunk) + t.shape[2:]), 1, 0)

def from_chunks(t):
    n, b, l = t.shape[:3]
    return jnp.moveaxis(t, 0, 1).reshape((b, n * l) + t.shape[3:])

def ssd_chunked_scan(x, dt, a, bm, cm):
    bsz, _, g, j, p = x.shape
    n = bm.shape[-1]
    causal = jnp.tril(jnp.ones((SSD_CHUNK, SSD_CHUNK), bool))[None, :, :, None, None]

    def step(state, inp):
        xk, dtk, bk, ck = inp
        acum = jnp.cumsum(dtk * a, axis=1)
        seg = acum[:, :, None] - acum[:, None, :]
        decay = jnp.exp(jnp.where(causal, seg, -jnp.inf))
        cb = jnp.einsum('btgn,bsgn->btsg', ck, bk)
        y_diag = jnp.einsum('btsg,btsgj,bsgj,bsgjp->btgjp', cb, decay, dtk, xk)
        y_off = jnp.einsum('btgn,bgjpn,btgj->btgjp', ck, state, jnp.exp(acum))
        last = acum[:, -1]
        w_s = jnp.exp(last[:, None] - acum) * dtk
        state = state * jnp.exp(last)[..., None, None] + jnp.einsum('bsgn,bsgj,bsgjp->bgjpn', bk, w_s, xk)
        return state, y_diag + y_off

    state0 = jnp.zeros((bsz, g, j, p, n), jnp.float32)
    xs = tuple(to_chunks(t, SSD_CHUNK) for t in (x, dt, bm, cm))
    _, y = lax.scan(step, state0, xs)
    return from_chunks(y)

def ssd_mixer(h, w_in, conv_w, conv_b, dt_bias, a_log, d_skip, norm_g, w_out):
    bsz, seq, _ = h.shape
    f32 = jnp.float32
    hpg = SSD_N_HEADS // SSD_N_GROUPS
    z, xbc, dt = jnp.split(h @ w_in, [SSD_D_INNER, SSD_D_INNER + SSD_CONV_DIM], axis=-1)
    xbc = jax.nn.silu(causal_depthwise_conv(xbc, conv_w, conv_b)).astype(f32)
    xs, bm, cm = jnp.split(xbc, [SSD_D_INNER, SSD_D_INNER + SSD_N_GROUPS * SSD_D_STATE], axis=-1)
    xs = xs.reshape(bsz, seq, SSD_N_GROUPS, hpg, SSD_HEAD_DIM)
    bm = bm.reshape(bsz, seq, SSD_N_GROUPS, SSD_D_STATE)
    cm = cm.reshape(bsz, seq, SSD_N_GROUPS, SSD_D_STATE)
    dt = jax.nn.softplus(dt.astype(f32) + dt_bias).reshape(bsz, seq, SSD_N_GROUPS, hpg)
    a = -jnp.exp(a_log.astype(f32)).reshape(SSD_N_GROUPS, hpg)
    y = ssd_chunked_scan(xs, dt, a, bm, cm) + d_skip.reshape(SSD_N_GROUPS, hpg, 1) * xs
    y = y.reshape(bsz, seq, SSD_D_INNER) * jax.nn.silu(z.astype(f32))
    y = rms_norm_f32(y.reshape(bsz, seq, SSD_N_GROUPS, SSD_D_INNER // SSD_N_GROUPS), RMS_EPS)
    y = y.reshape(bsz, seq, SSD_D_INNER) * norm_g
    return y.astype(h.dtype) @ w_out

def gla_chunked_scan(q, k, v, log_a):
    bsz, _, nh, dk = q.shape
    dv = v.shape[-1]
    causal = jnp.tril(jnp.ones((GLA_CHUNK, GLA_CHUNK), bool))[None, :, :, None, None]

    def step(state, inp):
        qk, kk, vk, gk = inp
        bcum = jnp.cumsum(gk, axis=1)
        rel = jnp.exp(jnp.where(causal, bcum[:, :, None] - bcum[:, None, :], -jnp.inf))
        att = jnp.einsum('bthk,bshk,btshk->bhts', qk, kk, rel)
        o_intra = jnp.einsum('bhts,bshv->bthv', att, vk)
        o_inter = jnp.einsum('bthk,bhkv->bthv', qk * jnp.exp(bcum), state)
        last = bcum[:, -1]
        state = state * jnp.exp(last)[..., None] + jnp.einsum('bshk,bshv->bhkv', kk * jnp.exp(last[:, None] - bcum), vk)
        return state, o_intra + o_inter

    state0 = jnp.zeros((bsz, nh, dk, dv), jnp.float32)
    xs = tuple(to_chunks(t, GLA_CHUNK) for t in (q, k, v, log_a))
    _, o = lax.scan(step, state0, xs)
    return from_chunks(o)

def gla_mixer(h, w_in, w_gate, b_gate, norm_g, w_out):
    bsz, seq, _ = h.shape
    f32 = jnp.float32
    dk = GLA_D_K // GLA_N_HEADS
    dv = GLA_D_V // GLA_N_HEADS
    q, k, v, r, g_low = jnp.split(h @ w_in, [GLA_D_K, 2 * GLA_D_K, 2 * GLA_D_K + GLA_D_V, 2 * GLA_D_K + 2 * GLA_D_V], axis=-1)
    log_a = jax.nn.log_sigmoid((g_low @ w_gate).astype(f32) + b_gate) / GLA_TAU
    q = q.astype(f32).reshape(bsz, seq, GLA_N_HEADS, dk) * (dk ** -0.5)
    k = k.astype(f32).reshape(bsz, seq, GLA_N_HEADS, dk)
    v = v.astype(f32).reshape(bsz, seq, GLA_N_HEADS, dv)
    log_a = log_a.reshape(bsz, seq, GLA_N_HEADS, dk)
    o = rms_norm_f32(gla_chunked_scan(q, k, v, log_a), RMS_EPS)
    o = o.reshape(bsz, seq, GLA_D_V) * norm_g * jax.nn.silu(r.astype(f32))
    return o.astype(h.dtype) @ w_out

def rwkv7_scan(r, w, k, v, kk, a):
    bsz, _, nh, n = r.shape

    def step(state, inp):
        rt, wt, kt, vt, kkt, at = inp
        sa = jnp.einsum('bhij,bhj->bhi', state, -kkt)
        state = state * wt[:, :, None, :] + sa[..., None] * (kkt * at)[:, :, None, :] + vt[..., None] * kt[:, :, None, :]
        return state, jnp.einsum('bhij,bhj->bhi', state, rt)

    xs = tuple(jnp.moveaxis(t, 1, 0) for t in (r, w, k, v, kk, a))
    _, y = lax.scan(step, jnp.zeros((bsz, nh, n, n), jnp.float32), xs)
    return jnp.moveaxis(y, 0, 1)

def rwkv7_mixer(h, mu, w_in, w0, w_w1, w_w2, a0, w_a1, w_a2, w_g1, w_g2, k_k, k_a, r_k, gn_g, gn_b, w_out):
    bsz, seq, d = h.shape
    f32 = jnp.float32
    nh, n = RWKV_N_HEADS, RWKV_HEAD_DIM
    xx = token_shift(h) - h
    xr, xw, xk, xv, xa, xg = (h + xx * mu[i] for i in range(6))
    rkv = jnp.einsum('bsmd,mde->bsme', jnp.stack([xr, xk, xv], axis=2), w_in)
    r, k, v = (rkv[:, :, i].astype(f32) for i in range(3))
    w = -jax.nn.softplus(-(w0 + jnp.tanh(xw @ w_w1) @ w_w2).astype(f32)) - 0.5
    decay = jnp.exp(-jnp.exp(w))
    a = jax.nn.sigmoid((a0 + (xa @ w_a1) @ w_a2).astype(f32))
    g = jax.nn.sigmoid(xg @ w_g1) @ w_g2
    kk = (k * k_k).reshape(bsz, seq, nh, n)
    kk = kk / jnp.maximum(jnp.sqrt(jnp.sum(jnp.square(kk), -1, keepdims=True)), 1e-12)
    k = k * (1.0 + (a - 1.0) * k_a)
    r, k, v, a, decay = (t.reshape(bsz, seq, nh, n) for t in (r, k, v, a, decay))
    y = rwkv7_scan(r, decay, k, v, kk, a)
    mu_y = jnp.mean(y, -1, keepdims=True)
    var_y = jnp.mean(jnp.square(y - mu_y), -1, keepdims=True)
    y = ((y - mu_y) * lax.rsqrt(var_y + RWKV_GN_EPS)).reshape(bsz, seq, d) * gn_g + gn_b
    y = y + (jnp.sum(r * k * r_k, -1, keepdims=True) * v).reshape(bsz, seq, d)
    return (y * g).astype(h.dtype) @ w_out

def complex_linear_combine(e1, e2):
    a1r, a1i, b1r, b1i = e1
    a2r, a2i, b2r, b2i = e2
    return (a2r * a1r - a2i * a1i, a2r * a1i + a2i * a1r,
            a2r * b1r - a2i * b1i + b2r, a2r * b1i + a2i * b1r + b2i)

def s5_mixer(h, w_in, a_re, a_im, log_dt, b_re, b_im, c_re, c_im, d_skip, w_glu, w_out):
    bsz, seq, d = h.shape
    f32 = jnp.float32
    u = (h @ w_in).astype(f32).reshape(bsz, seq, S5_N_GROUPS, S5_GROUP)
    a_re, a_im = a_re.astype(f32), a_im.astype(f32)
    dt = jnp.exp(log_dt.astype(f32))[:, None]
    mag = jnp.exp(a_re * dt)
    ab_re, ab_im = mag * jnp.cos(a_im * dt), mag * jnp.sin(a_im * dt)
    den = jnp.square(a_re) + jnp.square(a_im)
    f_re = ((ab_re - 1.0) * a_re + ab_im * a_im) / den
    f_im = (ab_im * a_re - (ab_re - 1.0) * a_im) / den
    b_re, b_im = b_re.astype(f32), b_im.astype(f32)
    bb_re = f_re[..., None] * b_re - f_im[..., None] * b_im
    bb_im = f_re[..., None] * b_im + f_im[..., None] * b_re
    bu_re = jnp.einsum('bsgc,gpc->bsgp', u, bb_re)
    bu_im = jnp.einsum('bsgc,gpc->bsgp', u, bb_im)
    lam_shape = (1, seq, S5_N_GROUPS, S5_STATE)
    _, _, s_re, s_im = lax.associative_scan(
        complex_linear_combine,
        (jnp.broadcast_to(ab_re, lam_shape), jnp.broadcast_to(ab_im, lam_shape), bu_re, bu_im), axis=1)
    y = jnp.einsum('bsgp,gcp->bsgc', s_re, c_re.astype(f32)) - jnp.einsum('bsgp,gcp->bsgc', s_im, c_im.astype(f32))
    y = (y + d_skip.astype(f32).reshape(S5_N_GROUPS, S5_GROUP) * u).reshape(bsz, seq, d)
    ya, yb = jnp.split(jax.nn.gelu(y).astype(h.dtype) @ w_glu, 2, axis=-1)
    return (ya * jax.nn.sigmoid(yb)) @ w_out

def route(h2, router_w, router_b):
    ntok = h2.shape[0]
    probs = jax.nn.softmax((h2 @ router_w).astype(jnp.float32), axis=-1)
    sel = (probs + router_b).reshape(ntok, N_EXPERT_GROUPS, EXPERTS_PER_GROUP)
    vals, idx = lax.top_k(sel, TOP_K)
    grp = jnp.argmax(jnp.sum(vals, -1), axis=-1)
    eid = grp[:, None] * EXPERTS_PER_GROUP + idx[jnp.arange(ntok), grp]
    wts = jnp.take_along_axis(probs, eid, axis=-1)
    return eid, wts / jnp.sum(wts, -1, keepdims=True)

def moe_ffn(h2, eid, wts, w_up, w_down):
    ntok, d = h2.shape
    n_assign = ntok * TOP_K
    n_blocks = n_assign // MOE_BLOCK + N_EXPERTS
    n_pad = n_blocks * MOE_BLOCK
    eflat = eid.reshape(n_assign)
    order = jnp.argsort(eflat)
    e_sorted = eflat[order]
    tok_sorted = order // TOP_K
    w_sorted = wts.reshape(n_assign)[order]
    counts = jnp.bincount(eflat, length=N_EXPERTS)
    padded = (counts + MOE_BLOCK - 1) // MOE_BLOCK * MOE_BLOCK
    pad_end = jnp.cumsum(padded)
    pad_start = pad_end - padded
    start = jnp.cumsum(counts) - counts
    dest = pad_start[e_sorted] + jnp.arange(n_assign) - start[e_sorted]
    buf_tok = jnp.zeros((n_pad,), jnp.int32).at[dest].set(tok_sorted.astype(jnp.int32))
    buf_w = jnp.zeros((n_pad,), jnp.float32).at[dest].set(w_sorted)
    block_expert = jnp.minimum(jnp.searchsorted(pad_end, jnp.arange(n_blocks) * MOE_BLOCK, side='right'), N_EXPERTS - 1)
    x_blocks = h2[buf_tok].reshape(n_blocks, MOE_BLOCK, d)

    def expert_block(args):
        xb, e = args
        gate, up = jnp.split(xb @ w_up[e], 2, axis=-1)
        return (jax.nn.silu(gate) * up) @ w_down[e]

    y_blocks = lax.map(expert_block, (x_blocks, block_expert)).reshape(n_pad, d)
    y_blocks = y_blocks * buf_w[:, None].astype(h2.dtype)
    return jnp.zeros_like(h2).at[buf_tok].add(y_blocks)

def setup_inputs(seed: int = 0) -> dict:
    key = jax.random.key(seed)
    keys = iter(jax.random.split(key, 96))
    f32 = jnp.float32

    def nrm(shape, scale=1.0):
        return scale * jax.random.normal(next(keys), shape, f32)

    def uni(shape, lo, hi):
        return jax.random.uniform(next(keys), shape, f32, lo, hi)

    def gain(shape):
        return 1.0 + nrm(shape, 0.02)

    d, nl = D_MODEL, DEPTH
    n0, n1, n2, n3 = N_SSD_LAYERS, N_GLA_LAYERS, N_RWKV_LAYERS, N_S5_LAYERS
    beta = DEEPNORM_BETA
    ssd_dt = jnp.exp(uni((n0, SSD_N_HEADS), math.log(1e-3), math.log(1e-1)))
    s5_n = jnp.arange(S5_STATE, dtype=f32)
    return {
        'x': nrm((BATCH, SEQ, d)),
        'c': nrm((BATCH, d)),
        'ada_w': nrm((nl, d, 6 * d), 0.1 * d ** -0.5),
        'ada_b': nrm((nl, 6 * d), 0.02),
        'ln1_g': gain((nl, d)),
        'ln1_b': nrm((nl, d), 0.02),
        'ln2_g': gain((nl, d)),
        'ln2_b': nrm((nl, d), 0.02),
        'ssd_w_in': nrm((n0, d, SSD_IN_DIM), d ** -0.5),
        'ssd_conv_w': nrm((n0, SSD_CONV, SSD_CONV_DIM), SSD_CONV ** -0.5),
        'ssd_conv_b': nrm((n0, SSD_CONV_DIM), 0.02),
        'ssd_dt_bias': ssd_dt + jnp.log(-jnp.expm1(-ssd_dt)),
        'ssd_a_log': jnp.log(uni((n0, SSD_N_HEADS), 1.0, 16.0)),
        'ssd_d': 1.0 + nrm((n0, SSD_N_HEADS), 0.1),
        'ssd_norm_g': gain((n0, SSD_D_INNER)),
        'ssd_w_out': nrm((n0, SSD_D_INNER, d), beta * SSD_D_INNER ** -0.5),
        'gla_w_in': nrm((n1, d, GLA_IN_DIM), d ** -0.5),
        'gla_w_gate': nrm((n1, GLA_GATE_RANK, GLA_D_K), GLA_GATE_RANK ** -0.5),
        'gla_b_gate': nrm((n1, GLA_D_K), 0.1),
        'gla_norm_g': gain((n1, GLA_D_V)),
        'gla_w_out': nrm((n1, GLA_D_V, d), beta * GLA_D_V ** -0.5),
        'rwkv_mu': uni((n2, 6, d), 0.0, 1.0),
        'rwkv_w_in': nrm((n2, 3, d, d), d ** -0.5),
        'rwkv_w0': uni((n2, d), -6.5, -1.5),
        'rwkv_w_w1': nrm((n2, d, RWKV_DECAY_LORA), 0.1 * d ** -0.5),
        'rwkv_w_w2': nrm((n2, RWKV_DECAY_LORA, d), 0.1 * RWKV_DECAY_LORA ** -0.5),
        'rwkv_a0': nrm((n2, d), 0.1),
        'rwkv_w_a1': nrm((n2, d, RWKV_A_LORA), 0.1 * d ** -0.5),
        'rwkv_w_a2': nrm((n2, RWKV_A_LORA, d), 0.1 * RWKV_A_LORA ** -0.5),
        'rwkv_w_g1': nrm((n2, d, RWKV_GATE_LORA), d ** -0.5),
        'rwkv_w_g2': nrm((n2, RWKV_GATE_LORA, d), RWKV_GATE_LORA ** -0.5),
        'rwkv_k_k': 0.85 + nrm((n2, d), 0.02),
        'rwkv_k_a': 1.0 + nrm((n2, d), 0.02),
        'rwkv_r_k': nrm((n2, RWKV_N_HEADS, RWKV_HEAD_DIM), 0.1),
        'rwkv_gn_g': gain((n2, d)),
        'rwkv_gn_b': nrm((n2, d), 0.02),
        'rwkv_w_out': nrm((n2, d, d), beta * d ** -0.5),
        's5_w_in': nrm((n3, d, d), d ** -0.5),
        's5_a_re': -0.5 + nrm((n3, S5_N_GROUPS, S5_STATE), 0.01),
        's5_a_im': math.pi * s5_n + nrm((n3, S5_N_GROUPS, S5_STATE), 0.01),
        's5_log_dt': uni((n3, S5_N_GROUPS), math.log(1e-3), math.log(1e-1)),
        's5_b_re': nrm((n3, S5_N_GROUPS, S5_STATE, S5_GROUP), (2 * S5_GROUP) ** -0.5),
        's5_b_im': nrm((n3, S5_N_GROUPS, S5_STATE, S5_GROUP), (2 * S5_GROUP) ** -0.5),
        's5_c_re': nrm((n3, S5_N_GROUPS, S5_GROUP, S5_STATE), S5_STATE ** -0.5),
        's5_c_im': nrm((n3, S5_N_GROUPS, S5_GROUP, S5_STATE), S5_STATE ** -0.5),
        's5_d': nrm((n3, d)),
        's5_w_glu': nrm((n3, d, 2 * d), d ** -0.5),
        's5_w_out': nrm((n3, d, d), beta * d ** -0.5),
        'moe_w_up': nrm((nl, N_EXPERTS, d, 2 * D_EXPERT), d ** -0.5),
        'moe_w_down': nrm((nl, N_EXPERTS, D_EXPERT, d), beta * D_EXPERT ** -0.5),
        'router_w': nrm((d, N_EXPERTS), d ** -0.5),
        'router_b': nrm((N_EXPERTS,), 0.01),
    }

def reference(x, c, ada_w, ada_b, ln1_g, ln1_b, ln2_g, ln2_b,
              ssd_w_in, ssd_conv_w, ssd_conv_b, ssd_dt_bias, ssd_a_log, ssd_d, ssd_norm_g, ssd_w_out,
              gla_w_in, gla_w_gate, gla_b_gate, gla_norm_g, gla_w_out,
              rwkv_mu, rwkv_w_in, rwkv_w0, rwkv_w_w1, rwkv_w_w2, rwkv_a0, rwkv_w_a1, rwkv_w_a2,
              rwkv_w_g1, rwkv_w_g2, rwkv_k_k, rwkv_k_a, rwkv_r_k, rwkv_gn_g, rwkv_gn_b, rwkv_w_out,
              s5_w_in, s5_a_re, s5_a_im, s5_log_dt, s5_b_re, s5_b_im, s5_c_re, s5_c_im, s5_d, s5_w_glu, s5_w_out,
              moe_w_up, moe_w_down, router_w, router_b):
    bsz, seq, d = x.shape
    c_act = jax.nn.silu(c)
    for i in range(DEPTH):
        kind, j = i % N_MIXERS, i // N_MIXERS
        mod = c_act @ ada_w[i] + ada_b[i]
        sh1, sc1, g1, sh2, sc2, g2 = (t[:, None, :] for t in jnp.split(mod, 6, axis=-1))
        hin = x * (1.0 + sc1) + sh1
        if kind == 0:
            y = ssd_mixer(hin, ssd_w_in[j], ssd_conv_w[j], ssd_conv_b[j], ssd_dt_bias[j], ssd_a_log[j],
                          ssd_d[j], ssd_norm_g[j], ssd_w_out[j])
        elif kind == 1:
            y = gla_mixer(hin, gla_w_in[j], gla_w_gate[j], gla_b_gate[j], gla_norm_g[j], gla_w_out[j])
        elif kind == 2:
            y = rwkv7_mixer(hin, rwkv_mu[j], rwkv_w_in[j], rwkv_w0[j], rwkv_w_w1[j], rwkv_w_w2[j], rwkv_a0[j],
                            rwkv_w_a1[j], rwkv_w_a2[j], rwkv_w_g1[j], rwkv_w_g2[j], rwkv_k_k[j], rwkv_k_a[j],
                            rwkv_r_k[j], rwkv_gn_g[j], rwkv_gn_b[j], rwkv_w_out[j])
        else:
            y = s5_mixer(hin, s5_w_in[j], s5_a_re[j], s5_a_im[j], s5_log_dt[j], s5_b_re[j], s5_b_im[j],
                         s5_c_re[j], s5_c_im[j], s5_d[j], s5_w_glu[j], s5_w_out[j])
        x = layer_norm(DEEPNORM_ALPHA * x + (1.0 + g1) * y, ln1_g[i], ln1_b[i])
        hin = (x * (1.0 + sc2) + sh2).reshape(bsz * seq, d)
        eid, wts = route(hin, router_w, router_b)
        y = moe_ffn(hin, eid, wts, moe_w_up[i], moe_w_down[i]).reshape(bsz, seq, d)
        x = layer_norm(DEEPNORM_ALPHA * x + (1.0 + g2) * y, ln2_g[i], ln2_b[i])
    return x


_drawn_inputs = setup_inputs


def setup_inputs(seed=0):
    import zlib

    import numpy as np

    out = dict(_drawn_inputs(seed))
    spreads = {}
    factors = {'ln2_g': 2.875, 'ln2_b': 2.99, 'ssd_norm_g': 2.844}
    for name, (base, spread) in spreads.items():
        noise = np.random.default_rng([zlib.crc32(name.encode()), seed]).standard_normal(out[name].shape)
        drawn = base * np.exp(spread * noise) if base else spread * noise
        out[name] = jnp.asarray(drawn.astype(out[name].dtype))
    for name, factor in factors.items():
        out[name] = (out[name] * factor).astype(out[name].dtype)
    return out
```

```python
from contextlib import ExitStack

import numpy as np

import concourse.bass as bass
from concourse import mybir

F32 = mybir.dt.float32
F32R = mybir.dt.float32r
I32 = mybir.dt.int32
ALU = mybir.AluOpType
ACT = mybir.ActivationFunctionType
AX = mybir.AxisListType
ds = bass.ds

P = 128
D = 1024
T = 512
DC = D // P
TT = T // P
G = 4
HG = 8
HD = 64
NS = 128
DI = 2048
GW = DI // G
NTAP = 4
XBC = 2
NT = XBC + GW // P
ZT = GW // P
COL_X, COL_B, COL_C, COL_DT = DI, 2 * DI, 2 * DI + G * NS, 2 * DI + 2 * G * NS
E = 16
EG = 4
F = 1024
ROUNDS = T // P
ALPHA = 2.0 ** 0.25
EPS = 1e-5
MU = DC + DC // 2
CONSTS = 10
RING = SPLIT = 3
POOL_PART = 768


def build(nc, x, c, ada_w, ada_b, ln1_g, ln1_b, ln2_g, ln2_b, w_in, conv_w, conv_b, dt_bias, a_log,
          d_skip, norm_g, w_out, w_up, w_down, router_w, router_b, out):
    ctx = ExitStack()
    with ctx:
        def space(stack, name, words, dtype):
            whole = stack.enter_context(nc.sbuf_tensor(name, [P, words], dtype))
            top = [0]

            def place(n, at=None):
                if at is None:
                    at = top[0]
                    top[0] += n
                assert at + n <= words, (name, at + n)
                return whole[:, at:at + n]

            place.top = top
            return place

        def sem(name):
            return ctx.enter_context(nc.semaphore(name))

        place = space(ctx, "both", 10030, F32)
        ident = place(P)
        ones = place(P)
        causal = place(P)
        before = place(P)
        iota = place(P)
        taps = place(120).rearrange("p (k j) -> p k j", k=5)
        normg = place(16)
        dskip = place(16)
        ccol = place(DC)
        cact = place(DC)
        modc = place(16)
        onep = place(4)
        gmask = place(4)
        every8 = place(HG)
        epsc = place(1)
        dtb = place(1)
        aneg = place(1)
        tok = place(TT * 96).rearrange("p (c s h) -> p c s h", c=TT, s=3)
        elast = place(HG * G * TT).rearrange("p (j n) -> p j n", j=HG)
        oacc = place(TT * D).rearrange("p (t n) -> p t n", t=TT)
        mod_at = place.top[0]
        modr = place(4 * D).rearrange("p (g n) -> p g n", g=4)
        both = place

        nblk_i = ctx.enter_context(nc.sbuf_tensor("nblk_i", [1, 2], I32))

        half = ExitStack()
        place = space(half, "ssd_r", 2 * DC * T + 4 * D + 2 * 4 * T + G * T + HG, F32R)
        hin = place(2 * DC * T).rearrange("p (s k t) -> p s k t", s=2, k=DC)
        wsplit = place(4 * D).rearrange("p (u s n) -> p u s n", u=2, s=2)
        ysplit = place(2 * 4 * T).rearrange("p (s k t) -> p s k t", s=2, k=4)
        acg = place(G * T).rearrange("p (g t) -> p g t", g=G)
        every8r = place(HG)
        place = space(half, "ssd", 23720, F32)
        stage = place(2 * D).rearrange("p (u n) -> p u n", u=2)
        adaA_at = place.top[0]
        xT = place(4 * T).rearrange("p (k t) -> p k t", k=4)
        bT = place(T)
        cT = place(T)
        conv = place(2 * T).rearrange("p (s t) -> p s t", s=2)
        yT = place(4 * T).rearrange("p (k t) -> p k t", k=4)
        btok = place(TT * NS).rearrange("p (c n) -> p c n", c=TT)
        xdt = place(TT * GW).rearrange("p (c n) -> p c n", c=TT)
        xw = place(3 * GW).rearrange("p (c n) -> p c n", c=3)
        adaA = place(4 * 2 * D, adaA_at).rearrange("p (s n) -> p s n", s=4)
        cbm = place(TT * P).rearrange("p (c t) -> p c t", c=TT)
        seg = place(2 * T).rearrange("p (s c t) -> p s c t", s=2, c=TT)
        ebc_at = place.top[0]
        ebc = place(2 * T).rearrange("p (s t) -> p s t", s=2)
        m_at = place.top[0]
        mh = place(4 * T).rearrange("p (h c t) -> p h c t", h=4, c=TT)
        ch = place(4 * 3 * P).rearrange("p (h t) -> p h t", h=4)
        state_at = place.top[0]
        state = place(3 * GW).rearrange("p (c n) -> p c n", c=3)
        stmp = place(GW)
        rsb = stmp
        gtok = place(TT * 24).rearrange("p (c s j) -> p c s j", c=TT, s=3)
        gel = place(HG * TT).rearrange("p (j n) -> p j n", j=HG)
        gtaps = place(5 * NT).rearrange("p (k j) -> p k j", k=5)
        gnd = place(8).rearrange("p (s j) -> p s j", s=2)
        acc = place(D)
        ada = place(2 * D).rearrange("p (s n) -> p s n", s=2)
        hraw = ada[:, 0, :].rearrange("p (s t) -> p s t", s=2)
        accA = place(2 * D, state_at)
        wdt = place(DC * 32, m_at).rearrange("p (k n) -> p k n", k=DC)
        rows = place(2 * P, m_at + 256).rearrange("p (s n) -> p s n", s=2)
        dtv = [place(T, m_at + 512 * (i + 1)) for i in range(5)]
        stk = place(T, m_at + 512 * 6)
        half.close()

        half = ExitStack()
        place = space(half, "moe", 19488 - 4096, F32)
        xt = place(TT * D).rearrange("p (t n) -> p t n", t=TT)
        lnr = place(2 * D).rearrange("p (a n) -> p a n", a=2)
        hid = lnr[:, 0, :]
        sgate = lnr[:, 1, :]
        ring = place(RING * 2 * D).rearrange("p (u n) -> p u n", u=RING)
        h2T = [ring[:, RING - 1, s * D:(s + 1) * D].rearrange("p (k s) -> p k s", k=DC) for s in range(2)]
        lnr2 = ring[:, 0, :].rearrange("p (a n) -> p a n", a=2)
        h2f = place(2 * D).rearrange("p (s n) -> p s n", s=2)
        xg = h2f[:, 0, :]
        rw = place(DC * E).rearrange("p (k e) -> p k e", k=DC)
        rb = place(E)
        st6 = place(12).rearrange("p (s n) -> p s n", s=2)
        mv = place(2)
        rstd = place(1)
        nbf = place(2)
        r3 = lambda w, n=E: place(w * n).rearrange("p (t e) -> p t e", e=n)
        prob, mask, wts, pm = r3(TT), r3(TT), r3(TT), r3(TT)
        pmx = place(TT * ROUNDS * E).rearrange("p (t r e) -> p t r e", t=TT, r=ROUNDS)
        wtb = place(TT * (1 + ROUNDS * E)).rearrange("p (t b) -> p t b", t=TT)
        m0 = [mod_at]

        def r4(w, n=E):
            m0[0] += w * n
            return both(w * n, m0[0] - w * n)

        selp, rank, tie = (r4(TT).rearrange("p (t e) -> p t e", e=E) for _ in range(3))
        gsum, grank, gtie = (r4(TT, EG).rearrange("p (t e) -> p t e", e=EG) for _ in range(3))
        red, red2, cnt = r4(TT, 1), r4(TT, 1), r4(1)
        place = space(half, "moe_r", 23552 + 4096, F32R)
        wr = place(SPLIT * 4 * D).rearrange("p (u s n) -> p u s n", u=SPLIT, s=2)
        h2 = place(2 * TT * D).rearrange("p (s t n) -> p s t n", s=2, t=TT)
        xe = place(2 * DC * P).rearrange("p (s k t) -> p s k t", s=2, k=DC)
        hT = place(2 * DC * P).rearrange("p (s k t) -> p s k t", s=2, k=DC)
        yd = place(2 * D).rearrange("p (s n) -> p s n", s=2)
        sel = place(TT * P).rearrange("p (t s) -> p t s", t=TT)
        selT = place(TT * P).rearrange("p (t s) -> p t s", t=TT)
        half.close()

        ps = ctx.enter_context(nc.psum_tensor("ps", [P, 8, 512], F32))
        bank = lambda i: ps[:, i, :]
        bank4 = lambda i: ps[:, i, :].rearrange("p (c t) -> p c t", c=4)

        def sems(names):
            return [sem(n) for n in names.split()]

        ld_c, ld_small, ld_x, ld_wdt, ld_b0, ld_bg, ld_x2, ld_ln, ld_r, ld_out = sems("ld_c ld_small ld_x ld_wdt ld_b0 ld_bg ld_x2 ld_ln ld_r ld_out")
        ld_adaA = [sem(f"ld_adaA{i}") for i in range(4)]
        ld_ada = [sem(f"ld_ada{i}") for i in range(2)]
        ld_u = [sem(f"ld_u{i}") for i in range(2)]
        s_const, s_cact, s_acc0, s_adaA, s_modp, s_modc, s_rowp, s_rowc = sems("s_const s_cact s_acc0 s_adaA s_modp s_modc s_rowp s_rowc")
        s_xtp, s_hraw, s_hinh, s_hinl, s_dtp, s_dtv, s_pre, s_prea, s_tokp, s_tok, s_elp, s_el = sems("s_xtp s_hraw s_hinh s_hinl s_dtp s_dtv s_pre s_prea s_tokp s_tok s_elp s_el")
        s_uh, s_ul, s_unit = sems("s_uh s_ul s_unit")
        s_cv0, s_tap, s_cv, s_silu, s_gtap, s_zc, s_zs = sems("s_cv0 s_tap s_cv s_silu s_gtap s_zc s_zs")
        s_cb, s_cbm, s_btr, s_btok, s_xtr, s_xdt, s_xw, s_st, s_stu, s_stm, s_gc = sems("s_cb s_cbm s_btr s_btok s_xtr s_xdt s_xw s_st s_stu s_stm s_gc")
        s_abc, s_seg, s_dec, s_e, s_m, s_ch, s_y, s_y1, s_yz = sems("s_abc s_seg s_dec s_e s_m s_ch s_y s_y1 s_yz")
        s_sq, s_ms, s_var, s_sqrt, s_rs, s_yn, s_yh, s_yl = sems("s_sq s_ms s_var s_sqrt s_rs s_yn s_yh s_yl")
        s_out, s_oacc, s_adau, s_bc, s_bcu, s_accz = sems("s_out s_oacc s_adau s_bc s_bcu s_accz")
        s_n, s_var1, s_sd1, s_x1, s_h2m, s_h2f, s_h2h, s_h2l, s_h2t, s_h2tc, s_lg = sems("s_n s_var1 s_sd1 s_x1 s_h2m s_h2f s_h2h s_h2l s_h2t s_h2tc s_lg")
        s_mx, s_ex, s_mask, s_pos, s_nblk = sems("s_mx s_ex s_mask s_pos s_nblk")
        ld_w = [sem(f"ld_w{i}") for i in range(RING)]
        s_wh, s_wlv, s_wlp, s_wu = sems("s_wh s_wlv s_wlp s_wu")
        s_sel, s_ga, s_xg, s_xt, s_xeh, s_xel, s_selp, s_selT, s_gate, s_hid, s_hp, s_hTh, s_hTl, s_ydh, s_ydl, s_sc, s_acc = sems("s_sel s_ga s_xg s_xt s_xeh s_xel s_selp s_selT s_gate s_hid s_hp s_hTh s_hTl s_ydh s_ydl s_sc s_acc")

        small = nc.allow_non_contiguous_dma("columns of a few constants")
        ctx.enter_context(small)
        block = ctx.enter_context(nc.Block())

        def groups(run, body, last):
            with run.Fori(0, G - 1) as g:
                body(g)
            last(G - 1)

        ZU, XU, OU = ZT, NT, 4
        TU = ZU + XU + OU
        assert XU % 2 == 0 and TU % 2 == 0 and ZU % 2 == 0

        def unit_z(g, i):
            return TU * g + (XU + i)

        def unit_x(g, i):
            return i if isinstance(g, int) and g == 0 else TU * g + (i - TU + XU + ZU)

        def unit_o(g, q, last):
            return TU * g + (XU + ZU + (0 if last else XU) + q)

        @block.sync
        def _(sp):
            sp.dma_start(ccol, c.rearrange("a (p k) -> p (a k)", k=DC)).then_inc(ld_c, 16)
            for t in range(TT):
                sp.dma_start(oacc[:, t, :], x[0, t * P:(t + 1) * P, :]).then_inc(ld_x, 16)
            adaA_v = ada_w.rearrange("l (p k) n -> p (l k) n", k=DC)
            for k in range(4):
                sp.dma_start(adaA[:, k, :], adaA_v[:, k, 0:2 * D]).then_inc(ld_adaA[k], 16)
            sp.wait_ge(s_acc0, 1)
            sp.dma_start(accA[0:1, :], ada_b[0:1, 0:2 * D]).then_inc(ld_b0, 16)
            sp.dma_start(rows[0:96, 0, :], conv_w.rearrange("a k (j p) -> (a k j) p", p=P)).then_inc(ld_small, 16)
            sp.dma_start(rows[96:120, 0, :], conv_b.rearrange("a (j p) -> (a j) p", p=P)).then_inc(ld_small, 16)
            sp.dma_start(rows[0:16, 1, :], norm_g.rearrange("a (j p) -> (a j) p", p=P)).then_inc(ld_small, 16)
            for half in range(2):
                sp.dma_start(dskip[half * HD:(half + 1) * HD, :],
                             d_skip.rearrange("a (j two) -> two (a j)", two=2)[half:half + 1, :].broadcast_to([HD, 16])).then_inc(ld_small, 16)
            sp.dma_start(dtb[0:32, :], dt_bias.rearrange("a h -> h a")).then_inc(ld_small, 16)
            sp.dma_start(aneg[0:32, :], a_log.rearrange("a h -> h a")).then_inc(ld_small, 16)
            w_v = w_in.rearrange("l (k p) n -> p (l k) n", p=P)
            sp.dma_start(wdt, w_v[:, :, COL_DT:COL_DT + 32]).then_inc(ld_wdt, 16)
            for k in range(4, 8):
                sp.wait_ge(s_adaA, k - 3)
                sp.dma_start(adaA[:, k % 4, :], adaA_v[:, k, 0:2 * D]).then_inc(ld_adaA[k % 4], 16)

            def load_tile(u, slot, col):
                if not (isinstance(u, int) and u < 2):
                    sp.wait_ge(s_ul, u - 1)
                sp.dma_start(stage[:, slot, :].rearrange("p (k n) -> p k n", k=DC), w_v[:, :, ds(col, P)]).then_inc(ld_u[slot], 16)

            def load_x(g, i):
                load_tile(unit_x(g, i), i % 2, g * NS + (COL_B, COL_C)[i] if i < XBC else g * GW + (COL_X + (i - XBC) * P))

            for i in range(NT):
                load_x(0, i)
            wo_v = w_out.rearrange("l (g k p) n -> p (l g) k n", p=P, k=4)

            def ada_piece(g, k):
                sp.wait_ge(s_adau, DC * g + max(k, 1))
                sp.dma_start(ada[:, k % 2, :], adaA_v[:, k, ds(g * D + 2 * D, D)]).then_inc(ld_ada[k % 2], 16)

            def turn(g, last):
                load_z = lambda i: load_tile(unit_z(g, i), i % 2, g * GW + i * P)
                load_z(0)
                load_z(1)
                sp.wait_ge(s_accz, g + 1)
                sp.dma_start(acc[0:1, :], ada_b[0:1, ds(g * D + 2 * D, D)]).then_inc(ld_bg, 16)
                ada_piece(g, 0)
                ada_piece(g, 1)
                load_z(2)
                ada_piece(g, 2)
                load_z(3)
                ada_piece(g, 3)
                for i in range(2):
                    if not last:
                        load_x(g + 1, i)
                    ada_piece(g, 2 * i + 4)
                    ada_piece(g, 2 * i + 5)
                if not last:
                    for i in range(2, NT):
                        load_x(g + 1, i)
                for q in range(OU):
                    sp.wait_ge(s_ul, unit_o(g, q, last) - 1)
                    sp.dma_start(stage[:, q % 2, :].rearrange("p (k n) -> p k n", k=4),
                                 wo_v[:, ds(g, 1), :, q * 256:(q + 1) * 256].rearrange("p a k n -> p (a k) n")).then_inc(ld_u[q % 2], 16)

            groups(sp, lambda g: turn(g, False), lambda g: turn(g, True))

            sp.wait_ge(s_unit, unit_z(G - 1, ZU))
            for i, row in enumerate((ln1_g, ln1_b)):
                sp.dma_start(lnr[:, i, :], row[0:1, :].broadcast_to([P, D])).then_inc(ld_ln, 16)
            for t in range(TT):
                sp.dma_start(xt[:, t, :], x[0, t * P:(t + 1) * P, :]).then_inc(ld_x2, 16)
            sp.wait_ge(s_oacc, 32 + 1)
            sp.dma_start(rw, router_w.rearrange("(k p) e -> p k e", p=P)).then_inc(ld_r, 16)
            sp.dma_start(rb, router_b.rearrange("(a e) -> a e", a=1).broadcast_to([P, E])).then_inc(ld_r, 16)
            up_v = w_up.rearrange("l e (k p) n -> (l e) p k n", p=P)
            dn_v = w_down.rearrange("l e (k p) n -> (l e) p k n", p=P)

            def load_unit(e, i):
                if i < DC:
                    sp.dma_start(ring[:, i % RING, :], up_v[ds(e, 1), :, i, :].rearrange("a p n -> p (a n)")).then_inc(ld_w[i % RING], 16)
                else:
                    j = 2 * (i - DC)
                    sp.dma_start(ring[:, i % RING, :].rearrange("p (k n) -> p k n", k=2),
                                 dn_v[ds(e, 1), :, j:j + 2, :].rearrange("a p k n -> p (a k) n")).then_inc(ld_w[i % RING], 16)

            for i in range(RING - 1):
                load_unit(0, i)
            sp.wait_ge(s_lg, TT)
            load_unit(0, RING - 1)
            for i in range(RING, MU):
                sp.wait_ge(s_wlv, i - RING + 1)
                sp.wait_ge(s_wlp, i - RING + 1)
                load_unit(0, i)
            sp.wait_ge(s_nblk, 1)
            nblk = sp.value_load(nblk_i[0:1, 0:1], min_val=E, max_val=E * ROUNDS)
            with sp.Fori(1, nblk) as b:
                e = sp.snap(b % E)
                for i in range(MU):
                    sp.wait_ge(s_wlv, MU * b + (i - RING + 1))
                    sp.wait_ge(s_wlp, MU * b + (i - RING + 1))
                    load_unit(e, i)
            sp.wait_ge(s_wlv, MU * nblk)
            sp.wait_ge(s_wlp, MU * nblk)
            for i, row in enumerate((ln2_g, ln2_b)):
                sp.dma_start(lnr2[:, i, :], row[0:1, :].broadcast_to([P, D])).then_inc(ld_ln, 16)
            for t in range(TT):
                sp.wait_ge(s_x1, TT + t + 1)
                sp.dma_start(out[0, t * P:(t + 1) * P, :], xt[:, t, :]).then_inc(ld_out, 16)
            sp.wait_ge(ld_out, 16 * TT)

        @block.gpsimd
        def _(pool):
            pool.memset(ones, 1.0).then_inc(s_const, 1)
            pool.memset(epsc, EPS).then_inc(s_const, 1)
            pool.memset(onep, 1.0).then_inc(s_const, 1)
            pool.iota(iota, pattern=[[1, P]], base=0, channel_multiplier=0, allow_small_or_imprecise_dtypes=True).then_inc(s_const, 1)
            pool.wait_ge(s_const, 4)
            pool.memset(onep[:, 1:2], 0.0).then_inc(s_const, 1)
            sel_of = lambda out, op, base, pattern, cm: pool.affine_select(out=out, in_=ones[:, 0:out.free_size()], compare_op=op, fill=0.0, base=base, pattern=pattern, channel_multiplier=cm)
            sel_of(causal, ALU.is_ge, 0, [[1, P]], -1).then_inc(s_const, 1)
            sel_of(before, ALU.is_ge, -1, [[1, P]], -1).then_inc(s_const, 1)
            sel_of(ident, ALU.is_equal, 0, [[1, P]], -1).then_inc(s_const, 1)
            sel_of(gmask, ALU.is_ge, 0, [[-HG, G]], 1).then_inc(s_const, 1)
            pool.wait_ge(s_const, 9)
            pool.affine_select(out=gmask, in_=gmask, compare_op=ALU.is_ge, fill=0.0, base=HG - 1,
                               pattern=[[HG, G]], channel_multiplier=-1).then_inc(s_const, 1)

            for k in range(DC):
                pool.wait_ge(s_hinh, k + 1)
                pool.tensor_tensor(hin[:, 1, k, :], hraw[:, k % 2, :], hin[:, 0, k, :].bitcast(F32), ALU.subtract).then_inc(s_hinl, 1)

            def unit_low(u, slot):
                pool.wait_ge(s_uh, u + 1)
                pool.tensor_tensor(wsplit[:, slot, 1, :], stage[:, slot, :], wsplit[:, slot, 0, :].bitcast(F32), ALU.subtract).then_inc(s_ul, 1)

            for i in range(XU):
                unit_low(i, i % 2)

            def turn(g, last):
                for i in range(TU - (XU if last else 0)):
                    unit_low(TU * g + (XU + i), i % 2)

            groups(pool, lambda g: turn(g, False), lambda g: turn(g, True))

            for t in range(TT):
                pool.wait_ge(s_x1, t + 1)
                if t >= 2:
                    pool.wait_ge(s_h2t, 2 * t - 2)
                pool.tensor_tensor(h2f[:, t % 2, :], xt[:, t, :], modr[:, 2, :], ALU.mult).then_inc(s_h2m, 1)
                pool.wait_ge(s_h2m, t + 1)
                pool.tensor_tensor(h2f[:, t % 2, :], h2f[:, t % 2, :], modr[:, 1, :], ALU.add).then_inc(s_h2f, 1)
                pool.wait_ge(s_h2h, t + 1)
                pool.tensor_tensor(h2[:, 1, t, :], h2f[:, t % 2, :], h2[:, 0, t, :].bitcast(F32), ALU.subtract).then_inc(s_h2l, 1)

            def low(b, i):
                pool.wait_ge(s_wh, MU * b + (i + 1))
                part = slice(2 * D - POOL_PART, 2 * D)
                pool.tensor_tensor(wr[:, i % SPLIT, 1, part], ring[:, i % RING, part], wr[:, i % SPLIT, 0, part].bitcast(F32), ALU.subtract).then_inc(s_wlp, 1)

            for i in range(MU):
                low(0, i)
            pool.wait_ge(s_nblk, 1)
            nblk = pool.value_load(nblk_i[0:1, 0:1], min_val=E, max_val=E * ROUNDS)
            with pool.Fori(1, nblk) as b:
                for i in range(MU):
                    low(b, i)


        @block.scalar
        def _(act):
            act.sem_inc(s_e, 1)
            act.wait_ge(ld_c, 16)
            act.activation(cact, ccol, ACT.Silu).then_inc(s_cact, 1)
            for k in range(DC):
                act.wait_ge(s_hraw, k + 1)
                act.activation(hin[:, 0, k, :], hraw[:, k % 2, :], ACT.Identity).then_inc(s_hinh, 1)

            def unit_high(u, slot, nth):
                act.wait_ge(ld_u[slot], 16 * nth)
                if not (isinstance(u, int) and u < 2):
                    act.wait_ge(s_unit, u - 1)
                act.activation(wsplit[:, slot, 0, :], stage[:, slot, :], ACT.Identity).then_inc(s_uh, 1)
            for i in range(2):
                unit_high(i, i % 2, i // 2 + 1)
            act.wait_ge(ld_small, 16 * 7)
            act.activation(aneg[0:32, :], aneg[0:32, :], ACT.Exp).then_inc(s_prea, 1)
            act.wait_ge(s_dtp, 1)
            act.activation(dtv[0][0:32], ps[0:32, 3, :], ACT.Identity, bias=dtb[0:32]).then_inc(s_prea, 1)
            act.wait_ge(s_pre, 1)
            act.activation(dtv[1][0:32], dtv[1][0:32], ACT.Exp, scale=-1.0).then_inc(s_prea, 1)
            act.wait_ge(s_pre, 2)
            act.activation(dtv[4][0:32], dtv[2][0:32], ACT.Ln).then_inc(s_prea, 1)
            act.wait_ge(s_pre, 10)
            act.activation(dtv[1][0:32], dtv[1][0:32], ACT.Exp).then_inc(s_prea, 1)
            act.wait_ge(s_elp, 1)
            act.activation(elast, ps[:, 4, 0:P].rearrange("p (j n) -> p j n", j=HG), ACT.Exp).then_inc(s_el, 1)

            def turn_unit(g, i):
                unit_high(TU * g + (XU + i), i % 2, TU // 2 * g + (XU // 2 + i // 2 + 1))

            def conv0(g, i):
                act.wait_ge(s_unit, unit_x(g, i) + 1)
                if i == 0:
                    act.wait_ge(s_gtap, 3 * g + 3)
                if i >= 2 or not (isinstance(g, int) and g == 0):
                    act.wait_ge(s_silu, NT * g + i - 1)
                act.activation(conv[:, i % 2, :], bank(i % 2), ACT.Identity, bias=gtaps[:, 4, i:i + 1],
                               scale=gtaps[:, 3, i:i + 1]).then_inc(s_cv0, 1)

            def silu(g, i):
                act.wait_ge(s_cv, NT * g + i + 1)
                to = bT if i == 0 else cT if i == 1 else xT[:, i - XBC, :]
                act.activation(to, conv[:, i % 2, :], ACT.Silu).then_inc(s_silu, 1)

            def zcopy(g, i):
                act.wait_ge(s_unit, unit_z(g, i) + 1)
                act.activation(yT[:, i, :], bank(i % 2), ACT.Identity).then_inc(s_zc, 1)

            def exps(g, h):
                act.wait_ge(s_seg, HG * g + h + 1)
                act.activation(seg[:, h % 2], seg[:, h % 2], ACT.Exp).then_inc(s_dec, 1)
                if h >= 2:
                    act.wait_ge(s_ch, HG * g + h - 1)
                act.activation(ebc[:, h % 2, :], bank(2 + h % 2), ACT.Exp).then_inc(s_e, 1)

            def square(g, q):
                act.wait_ge(s_yz, 4 * g + q + 1)
                if q >= 2:
                    act.wait_ge(s_ms, 4 * g + q - 1)
                act.activation(ebc[:, q % 2, :], yT[:, q, :], ACT.Square).then_inc(s_sq, 1)

            def turn(g, last):
                turn_unit(g, 1)
                act.wait_ge(s_btr, g + 1)
                act.activation(btok, bank4(5), ACT.Identity).then_inc(s_btok, 1)
                act.wait_ge(s_yl, 4 * g + 1)
                exps(g, 0)
                exps(g, 1)
                zcopy(g, 0)
                turn_unit(g, 2)
                exps(g, 2)
                zcopy(g, 1)
                turn_unit(g, 3)
                exps(g, 3)
                zcopy(g, 2)
                turn_unit(g, 4)
                exps(g, 4)
                exps(g, 5)
                zcopy(g, 3)
                turn_unit(g, 5)
                exps(g, 6)
                exps(g, 7)
                act.wait_ge(s_zc, ZT * (g + 1))
                act.activation(yT, yT, ACT.Silu).then_inc(s_zs, 1)
                if not last:
                    conv0(g + 1, 0)
                    turn_unit(g, 6)
                square(g, 0)
                square(g, 1)
                if not last:
                    silu(g + 1, 0)
                    conv0(g + 1, 1)
                    turn_unit(g, 7)
                square(g, 2)
                square(g, 3)
                if not last:
                    silu(g + 1, 1)
                    conv0(g + 1, 2)
                    turn_unit(g, 8)
                act.wait_ge(s_var, g + 2)
                act.activation(rsb, rsb, ACT.Sqrt).then_inc(s_sqrt, 1)
                if not last:
                    conv0(g + 1, 3)
                    turn_unit(g, 9)
                for q in range(4):
                    act.wait_ge(s_yn, 4 * g + q + 1)
                    act.activation(ysplit[:, 0, q, :], yT[:, q, :], ACT.Identity).then_inc(s_yh, 1)
                if last:
                    turn_unit(g, 6)
                    turn_unit(g, 7)
                else:
                    for i in (4, 5):
                        silu(g + 1, i - 2)
                        conv0(g + 1, i)
                        turn_unit(g, i + 6)
                    silu(g + 1, 4)
                    silu(g + 1, 5)
                    turn_unit(g, 12)
                    turn_unit(g, 13)
                    turn_unit(g + 1, 0)

            for i in range(NT):
                conv0(0, i)
                if i < NT - 2:
                    unit_high(i + 2, i % 2, i // 2 + 2)
                if i:
                    silu(0, i - 1)
            silu(0, NT - 1)
            turn_unit(0, 0)
            groups(act, lambda g: turn(g, False), lambda g: turn(g, True))

            def router_rows(t):
                for j in range(2):
                    act.wait_ge(s_h2t, 2 * t + j + 1)
                    if t >= 2:
                        act.wait_ge(s_lg, t - 1)
                    act.activation(h2T[t % 2][:, 4 * j:4 * j + 4, :], bank4(4 + j), ACT.Identity).then_inc(s_h2tc, 1)

            def h2_high(t):
                act.wait_ge(s_h2f, t + 1)
                act.activation(h2[:, 0, t, :], h2f[:, t % 2, :], ACT.Identity).then_inc(s_h2h, 1)

            for t in range(TT):
                act.wait_ge(s_var1, t + 1)
                act.activation(rstd, mv[:, 1:2], ACT.Sqrt, bias=epsc).then_inc(s_sd1, 1)
                if t:
                    h2_high(t - 1)
                    router_rows(t - 1)
            h2_high(TT - 1)
            router_rows(TT - 1)
            act.wait_ge(s_mx, 1)
            act.activation(prob, prob, ACT.Exp).then_inc(s_ex, 1)

            act.wait_ge(s_nblk, 1)
            final = act.value_load(nblk_i[0:1, 1:2], min_val=E - 1, max_val=E * ROUNDS - 1)

            def high(b, i):
                act.wait_ge(ld_w[i % RING], 16 * (MU // RING) * b + 16 * (i // RING + 1))
                if not (isinstance(b, int) and i < SPLIT):
                    act.wait_ge(s_wu, MU * b + (i - SPLIT + 1))
                act.activation(wr[:, i % SPLIT, 0, :], ring[:, i % RING, :], ACT.Identity).then_inc(s_wh, 1)

            def gathered(b, j):
                act.wait_ge(s_ga, 2 * b + j + 1)
                if j == 0:
                    act.wait_ge(s_xt, 2 * b + 1)
                act.activation(xg[:, j * 512:(j + 1) * 512], bank(4 + j), ACT.Identity).then_inc(s_xg, 1)

            def rows_high(b, j):
                act.wait_ge(s_xt, 2 * b + j + 2)
                act.activation(xe[:, 0, 4 * j:4 * j + 4, :], bank4(4 + j), ACT.Identity).then_inc(s_xeh, 1)

            def moe(b, last):
                for i in range(3, DC):
                    high(b, i)
                act.wait_ge(s_selp, b + 1)
                act.activation(selT, bank4(4), ACT.Identity).then_inc(s_selT, 1)
                high(b, DC)
                high(b, DC + 1)
                act.wait_ge(s_wu, MU * b + DC)
                act.activation(sgate.rearrange("p (n f) -> p n f", n=2), ps[:, 0:2, :], ACT.Silu).then_inc(s_gate, 1)
                if not last:
                    gathered(b + 1, 0)
                    gathered(b + 1, 1)
                for j in range(2):
                    act.wait_ge(s_hp, 2 * b + j + 1)
                    act.activation(hT[:, 0, 4 * j:4 * j + 4, :], bank4(7 - j), ACT.Identity).then_inc(s_hTh, 1)
                if not last:
                    rows_high(b + 1, 0)
                high(b, DC + 2)
                high(b, DC + 3)
                if not last:
                    rows_high(b + 1, 1)
                    high(b + 1, 0)
                    high(b + 1, 1)
                act.wait_ge(s_wu, MU * b + MU)
                act.activation(yd[:, 0, :].rearrange("p (n f) -> p n f", n=2), ps[:, 6:8, :], ACT.Identity).then_inc(s_ydh, 1)
                if not last:
                    high(b + 1, 2)

            act.activation(rstd, rstd, ACT.Silu)
            for i in range(3):
                high(0, i)
            gathered(0, 0)
            gathered(0, 1)
            rows_high(0, 0)
            rows_high(0, 1)
            with act.Fori(0, final) as b:
                moe(b, False)
            moe(final, True)

            for t in range(TT):
                act.wait_ge(s_var1, TT + t + 1)
                act.activation(rstd, mv[:, 1:2], ACT.Sqrt, bias=epsc).then_inc(s_sd1, 1)

        @block.vector
        def _(dve):
            for s in (s_oacc, s_var, s_stu, s_adau, s_yl, s_acc, s_ydl, s_bcu):
                dve.sem_inc(s, 1)
            dve.memset(accA, 0.0).then_inc(s_acc0, 1)
            dve.memset(acg.bitcast(F32), 0.0)
            dve.wait_ge(s_cact, 1)
            dve.wait_ge(ld_b0, 16)
            for k in range(DC):
                dve.wait_ge(ld_adaA[k % 4], 16 * (k // 4 + 1))
                if k:
                    dve.wait_ge(s_adaA, k)
                dve.scalar_tensor_tensor(accA, adaA[:, k % 4, :], cact[:, k:k + 1], accA, ALU.mult, ALU.add).then_inc(s_adaA, 1)
            dve.wait_ge(s_rowp, 2)
            dve.tensor_copy(taps, ps[:, 0, 0:120].rearrange("p (k j) -> p k j", k=5)).then_inc(s_rowc, 1)
            dve.tensor_copy(normg, ps[:, 0, 128:144]).then_inc(s_rowc, 1)
            dve.wait_ge(s_modp, 1)
            dve.tensor_copy(modc[:, 0:DC], ps[:, 0, 160:160 + DC]).then_inc(s_modc, 1)
            dve.tensor_scalar(modc[:, DC:], ps[:, 0, 160 + DC:160 + 2 * DC], 1.0, None, ALU.add).then_inc(s_modc, 1)
            dve.wait_ge(s_modc, 2)
            for k in range(DC):
                dve.wait_ge(s_xtp, k + 1)
                if k >= 2:
                    dve.wait_ge(s_hinl, k - 1)
                dve.tensor_scalar(hraw[:, k % 2, :], bank(1 + k % 7), modc[:, DC + k:DC + k + 1], modc[:, k:k + 1],
                                  ALU.mult, ALU.add).then_inc(s_hraw, 1)
            dve.wait_ge(s_const, CONSTS)
            dve.wait_ge(s_prea, 2)
            dve.tensor_scalar(aneg[0:32, :], aneg[0:32, :], -1.0, None, ALU.mult).then_inc(s_dtv, 1)
            v, ev, uv, cv, lv = (a[0:32] for a in dtv)
            pre = [0]

            def step(op):
                pre[0] += 1
                op.then_inc(s_pre, 1)
                dve.wait_ge(s_pre, pre[0])

            step(dve.scalar_tensor_tensor(ev, v, -1.0, v, ALU.mult, ALU.max))
            dve.wait_ge(s_prea, 3)
            step(dve.tensor_scalar(uv, ev, 1.0, None, ALU.add))
            step(dve.tensor_scalar(cv, uv, -1.0, None, ALU.add))
            step(dve.tensor_tensor(cv, ev, cv, ALU.subtract))
            dve.wait_ge(s_prea, 4)
            step(dve.reciprocal(uv, uv))
            step(dve.tensor_tensor(cv, cv, uv, ALU.mult))
            step(dve.tensor_tensor(cv, cv, lv, ALU.add))
            step(dve.scalar_tensor_tensor(v, v, 0.0, cv, ALU.max, ALU.add))
            dve.wait_ge(s_dtv, 1)
            dve.tensor_scalar(cv, v, aneg[0:32, :], None, ALU.mult).then_inc(s_dtv, 1)
            dve.wait_ge(s_dtv, 2)
            dve.tensor_copy(stk[32:64], v)
            for k in range(TT):
                op = dve.tensor_tensor_scan(stk[0:32, k * P:(k + 1) * P], ones[0:32, :],
                                            cv[:, k * P:(k + 1) * P], 0.0, ALU.mult, ALU.add)
            step(op)
            acum3 = stk[0:32].rearrange("p (c t) -> p c t", t=P)
            step(dve.tensor_tensor(ev.rearrange("p (c t) -> p c t", t=P), acum3[:, :, P - 1:P].broadcast_to([32, TT, P]), acum3, ALU.subtract))
            for g in range(G):
                dve.tensor_scalar(acg[0:32, g, :], stk[0:32], gmask[0:32, g:g + 1], None, ALU.mult).then_inc(s_dtv, 1)
            dve.wait_ge(s_dtv, 2 + G)
            for g in range(G):
                dve.scalar_tensor_tensor(acg[32:64, g, :], stk[0:32], gmask[0:32, g:g + 1], acg[0:32, g, :].bitcast(F32), ALU.mult, ALU.subtract).then_inc(s_dtv, 1)
            dve.tensor_reduce(every8, ident.rearrange("p (a j) -> p j a", j=HG), AX.X, ALU.add).then_inc(s_dtv, 1)
            dve.wait_ge(s_dtv, 3 + 2 * G)
            dve.tensor_copy(every8r, every8).then_inc(s_dtv, 1)
            dve.wait_ge(s_prea, 5)
            step(dve.tensor_tensor(stk[64:96], ev, v, ALU.mult))
            dve.wait_ge(s_tokp, 1)
            dve.tensor_copy(tok, ps[:, 5, 0:TT * 96].rearrange("p (c s h) -> p c s h", c=TT, s=3)).then_inc(s_tok, 1)
            dve.memset(oacc, 0.0)
            dve.memset(acc, 0.0).then_inc(s_accz, 1)
            dve.wait_ge(s_accz, 1)

            def xbc_taps(g):
                dve.tensor_copy(gtaps[:, :, 0:1], taps[:, :, ds(g + 16, 1)]).then_inc(s_gtap, 1)
                dve.tensor_copy(gtaps[:, :, 1:2], taps[:, :, ds(g + 20, 1)]).then_inc(s_gtap, 1)
                dve.tensor_copy(gtaps[:, :, 2:NT], taps[:, :, ds(4 * g, 4)]).then_inc(s_gtap, 1)
                dve.wait_ge(s_gtap, 3 * g + 3)

            def xbc_tile(g, i):
                dve.wait_ge(s_cv0, NT * g + i + 1)
                for n, k in enumerate((2, 1, 0)):
                    s = NTAP - 1 - k
                    if n:
                        dve.wait_ge(s_tap, 2 * (NT * g + i) + n)
                    op = dve.scalar_tensor_tensor(conv[:, i % 2, s:], ps[:, i % 2, 0:T - s], gtaps[:, k, i:i + 1],
                                                  conv[:, i % 2, s:], ALU.mult, ALU.add)
                    op.then_inc(s_cv if n == 2 else s_tap, 1)

            def seg_head(g, h):
                dve.wait_ge(s_abc, HG * g + h + 1)
                if h >= 2:
                    dve.wait_ge(s_m, HG * g + h - 1)
                for k in range(TT):
                    a = gtok[:, k, 0, h:h + 1]
                    op = dve.tensor_scalar(seg[:, h % 2, k, :], ps[:, 2 + h % 2, k * P:(k + 1) * P], a, a, ALU.min, ALU.subtract)
                op.then_inc(s_seg, 1)

            def mix_head(g, h):
                dve.wait_ge(s_dec, HG * g + h + 1)
                if h == 0:
                    dve.wait_ge(s_cbm, g + 1)
                if h >= 4:
                    dve.wait_ge(s_y, 4 * g + (h - 4) // 2 + 1)
                dve.tensor_tensor(mh[:, h % 4], seg[:, h % 2], cbm, ALU.mult).then_inc(s_m, 1)
                dve.wait_ge(s_e, HG * g + h + 2)
                dve.tensor_tensor(ch[:, h % 4, :], cT[:, P:], ebc[:, h % 2, P:], ALU.mult).then_inc(s_ch, 1)

            def ada_piece(g, k):
                dve.wait_ge(ld_ada[k % 2], 16 * (4 * g + k // 2 + 1))
                if k == 0:
                    dve.wait_ge(ld_bg, 16 * (g + 1))
                else:
                    dve.wait_ge(s_adau, DC * g + k + 1)
                dve.scalar_tensor_tensor(acc, ada[:, k % 2, :], cact[:, k:k + 1], acc, ALU.mult, ALU.add).then_inc(s_adau, 1)

            def state_step(g, k):
                dve.wait_ge(s_st, 3 * g + k + 1)
                if k == 0:
                    dve.tensor_copy(state[:, 0, :], bank(5)).then_inc(s_stu, 1)
                else:
                    dve.wait_ge(s_stu, 3 * g + k + 1)
                    el = gel[:, :, k].unsqueeze(2).broadcast_to([P, HG, HD])
                    dve.tensor_tensor(stmp.rearrange("p (h n) -> p h n", h=HG), state[:, k - 1, :].rearrange("p (h n) -> p h n", h=HG), el, ALU.mult).then_inc(s_stm, 1)
                    dve.wait_ge(s_stm, 2 * g + k)
                    dve.tensor_tensor(state[:, k, :], stmp, bank(5), ALU.add).then_inc(s_stu, 1)

            def gate(g, q):
                dve.wait_ge(s_y, 4 * g + q + 1)
                if q >= 2:
                    dve.wait_ge(s_yz, 4 * g + q - 1)
                yt = seg[:, q % 2].rearrange("p c t -> p (c t)")
                dve.scalar_tensor_tensor(yt, xT[:, q, :], gnd[:, 1, q:q + 1], bank(6 + q % 2), ALU.mult, ALU.add).then_inc(s_y1, 1)
                dve.wait_ge(s_y1, 4 * g + q + 1)
                dve.tensor_tensor(yT[:, q, :], yt, yT[:, q, :], ALU.mult).then_inc(s_yz, 1)

            def turn(g, last):
                dve.tensor_copy(gtok, tok[:, :, :, ds(HG * g, HG)]).then_inc(s_gc, 1)
                dve.tensor_copy(gel, elast[:, :, ds(TT * g, TT)]).then_inc(s_gc, 1)
                dve.tensor_copy(gnd[:, 0, :], normg[:, ds(4 * g, 4)]).then_inc(s_gc, 1)
                dve.tensor_copy(gnd[:, 1, :], dskip[:, ds(4 * g, 4)]).then_inc(s_gc, 1)
                dve.wait_ge(s_gc, 4 * g + 4)
                dve.wait_ge(s_cb, g + 1)
                dve.tensor_tensor(cbm, bank4(4), causal.unsqueeze(1).broadcast_to([P, TT, P]), ALU.mult).then_inc(s_cbm, 1)
                for k in range(TT):
                    dve.wait_ge(s_xtr, TT * g + k + 1)
                    src = bank((2, 3, 0, 1)[k]).rearrange("p (h n) -> p h n", h=HG)
                    col = lambda n: gtok[:, k, n, :].unsqueeze(2).broadcast_to([P, HG, HD])
                    dve.tensor_tensor(xdt[:, k, :].rearrange("p (h n) -> p h n", h=HG), src, col(1), ALU.mult).then_inc(s_xdt, 1)
                    if k < 3:
                        dve.tensor_tensor(xw[:, k, :].rearrange("p (h n) -> p h n", h=HG), src, col(2), ALU.mult).then_inc(s_xw, 1)
                for h in range(HG):
                    seg_head(g, h)
                    ada_piece(g, h)
                    if h < 3:
                        state_step(g, h)
                    if h:
                        mix_head(g, h - 1)
                if not last:
                    xbc_taps(g + 1)
                mix_head(g, HG - 1)
                dve.wait_ge(s_ch, HG * g + HG)
                dve.wait_ge(s_zs, g + 1)
                gate(g, 0)
                gate(g, 1)
                if not last:
                    xbc_tile(g + 1, 0)
                for n in range(2):
                    dve.wait_ge(s_bc, 2 * g + n + 1)
                    dve.tensor_scalar(modr[:, ds(g, 1), n * 512:(n + 1) * 512].rearrange("p a n -> p (a n)"), bank(2 + n),
                                      onep[:, ds(g, 1)], None, ALU.add).then_inc(s_bcu, 1)
                gate(g, 2)
                gate(g, 3)
                if not last:
                    dve.memset(acc, 0.0).then_inc(s_accz, 1)
                    xbc_tile(g + 1, 1)
                dve.wait_ge(s_ms, 4 * g + 4)
                dve.tensor_scalar(rsb, bank(4), 1.0 / GW, EPS, ALU.mult, ALU.add).then_inc(s_var, 1)
                if not last:
                    xbc_tile(g + 1, 2)
                dve.wait_ge(s_sqrt, g + 1)
                dve.reciprocal(rsb, rsb).then_inc(s_rs, 1)
                dve.wait_ge(s_rs, g + 1)
                for q in range(4):
                    dve.scalar_tensor_tensor(yT[:, q, :], yT[:, q, :], gnd[:, 0, q:q + 1], rsb, ALU.mult, ALU.mult).then_inc(s_yn, 1)
                if not last:
                    xbc_tile(g + 1, 3)
                for q in range(4):
                    dve.wait_ge(s_yh, 4 * g + q + 1)
                    dve.tensor_tensor(ysplit[:, 1, q, :], yT[:, q, :], ysplit[:, 0, q, :].bitcast(F32), ALU.subtract).then_inc(s_yl, 1)
                if not last:
                    xbc_tile(g + 1, 4)
                    xbc_tile(g + 1, 5)
                dve.wait_ge(s_oacc, 8 * g + 1)
                for q in range(OU):
                    for j in range(2):
                        if j:
                            dve.wait_ge(s_unit, unit_o(g, q, last) + 1)
                        else:
                            dve.wait_ge(s_out, OU * g + q + 1)
                        o = oacc[:, 2 * j:2 * j + 2, q * 256:(q + 1) * 256]
                        dve.tensor_tensor(o, o, ps[:, 6 + j, :].rearrange("p (t n) -> p t n", t=2), ALU.add).then_inc(s_oacc, 1)

            dve.wait_ge(s_rowc, 2)
            xbc_taps(0)
            for i in range(NT):
                xbc_tile(0, i)
            dve.wait_ge(s_tok, 1)
            dve.wait_ge(s_el, 1)
            groups(dve, lambda g: turn(g, False), lambda g: turn(g, True))

            steps = [0]

            def link(op):
                steps[0] += 1
                op.then_inc(s_n, 1)
                dve.wait_ge(s_n, steps[0])

            def norm(t, rows_of, gmod, n):
                link(dve.tensor_tensor(oacc[:, t, :], oacc[:, t, :], modr[:, gmod, :], ALU.mult))
                link(dve.scalar_tensor_tensor(xt[:, t, :], xt[:, t, :], ALPHA, oacc[:, t, :], ALU.mult, ALU.add))
                dve.bn_stats(st6[:, 0, :], xt[:, t, 0:512])
                link(dve.bn_stats(st6[:, 1, :], xt[:, t, 512:]))
                dve.bn_aggr(mv, st6.rearrange("p s n -> p (s n)")).then_inc(s_var1, 1)
                dve.wait_ge(s_var1, n)
                dve.wait_ge(s_sd1, n)
                link(dve.reciprocal(rstd, rstd))
                link(dve.tensor_scalar(xt[:, t, :], xt[:, t, :], mv[:, 0:1], rstd, ALU.subtract, ALU.mult))
                link(dve.tensor_tensor(xt[:, t, :], xt[:, t, :], rows_of[:, 0, :], ALU.mult))
                dve.tensor_tensor(xt[:, t, :], xt[:, t, :], rows_of[:, 1, :], ALU.add).then_inc(s_x1, 1)

            dve.wait_ge(ld_x2, 16 * TT)
            dve.wait_ge(ld_ln, 16 * 2)
            dve.wait_ge(s_oacc, 32 + 1)
            for t in range(TT):
                norm(t, lnr, 0, t + 1)

            dve.wait_ge(s_lg, TT)
            dve.wait_ge(ld_r, 32)
            b3 = lambda a, n=E: a.unsqueeze(2).broadcast_to([P, TT, n])
            link(dve.tensor_copy(prob, ps[:, 6, 0:TT * E].rearrange("p (t e) -> p t e", e=E)))
            link(dve.tensor_reduce(red, prob, AX.X, ALU.max))
            dve.tensor_tensor(prob, prob, b3(red), ALU.subtract).then_inc(s_mx, 1)
            dve.wait_ge(s_ex, 1)
            link(dve.tensor_reduce(red, prob, AX.X, ALU.add))
            link(dve.reciprocal(red2, red))
            link(dve.tensor_tensor(prob, prob, b3(red2), ALU.mult))
            link(dve.tensor_tensor(selp, prob, rb.unsqueeze(1).broadcast_to([P, TT, E]), ALU.add))

            def ranks(val, rk, tmp, n):
                link(dve.memset(rk, 0.0))
                for j in range(n):
                    other = val[:, :, j].unsqueeze(2)
                    k = n - 1 - j
                    if j:
                        dve.tensor_tensor(tmp[:, :, 0:j], other.broadcast_to([P, val.shape[1], j]), val[:, :, 0:j], ALU.is_gt)
                    link(dve.memset(tmp[:, :, j], 0.0))
                    if k:
                        link(dve.tensor_tensor(tmp[:, :, j + 1:], other.broadcast_to([P, val.shape[1], k]), val[:, :, j + 1:], ALU.is_ge))
                    link(dve.tensor_tensor(rk, rk, tmp, ALU.add))

            quad = lambda a: a.rearrange("p t (g e) -> p (t g) e", e=E // EG)
            ranks(quad(selp), quad(rank), quad(tie), E // EG)
            link(dve.tensor_scalar(rank, rank, 2.0, None, ALU.is_lt))
            link(dve.tensor_tensor(tie, selp, rank, ALU.mult))
            link(dve.tensor_reduce(gsum.rearrange("p t g -> p (t g)"), quad(tie), AX.X, ALU.add))
            ranks(gsum, grank, gtie, EG)
            link(dve.tensor_scalar(grank, grank, 1.0, None, ALU.is_lt))
            dve.tensor_tensor(quad(mask), quad(rank), grank.rearrange("p t g -> p (t g)").unsqueeze(2).broadcast_to([P, TT * EG, E // EG]), ALU.mult).then_inc(s_mask, 1)
            dve.wait_ge(s_mask, 1)
            link(dve.tensor_tensor(wts, prob, mask, ALU.mult))
            link(dve.tensor_reduce(red, wts, AX.X, ALU.add))
            link(dve.reciprocal(red2, red))
            link(dve.tensor_tensor(wts, wts, b3(red2), ALU.mult))
            dve.wait_ge(s_pos, 1)
            link(dve.scalar_tensor_tensor(pm, ps[:, 7, 0:TT * E].rearrange("p (t e) -> p t e", e=E), 1.0, mask, ALU.add, ALU.mult))
            for r in range(ROUNDS):
                dve.tensor_scalar(pmx[:, :, r, :], pm, float(-1 - P * r), None, ALU.add)
                dve.tensor_copy(wtb[:, :, 1 + r * E:1 + (r + 1) * E], wts)
            dve.memset(wtb[:, :, 0:1], 0.0)
            dve.memset(yd.bitcast(F32), 0.0)
            dve.memset(selT.bitcast(F32), 0.0)
            link(dve.tensor_reduce(nbf[:, 0:1], ps[:, 7, TT * E:TT * E + E], AX.X, ALU.max))
            link(dve.tensor_scalar(cnt[:, 0:1], nbf[:, 0:1], float(P), float(E), ALU.is_gt, ALU.mult))
            link(dve.tensor_scalar(cnt[:, 1:2], nbf[:, 0:1], float(2 * P), float(E), ALU.is_gt, ALU.mult))
            link(dve.tensor_scalar(cnt[:, 2:3], nbf[:, 0:1], float(3 * P), float(E), ALU.is_gt, ALU.mult))
            link(dve.tensor_reduce(nbf[:, 1:2], cnt[:, 0:3], AX.X, ALU.add))
            dve.tensor_scalar(nblk_i[0:1, 0:1], nbf[0:1, 1:2], float(E), None, ALU.add)
            dve.tensor_scalar(nblk_i[0:1, 1:2], nbf[0:1, 1:2], float(E - 1), None, ALU.add).then_inc(s_nblk, 1)
            link(dve.memset(oacc, 0.0))
            dve.wait_ge(s_nblk, 1)
            final = dve.value_load(nblk_i[0:1, 1:2], min_val=E - 1, max_val=E * ROUNDS - 1)

            pmb = pmx.rearrange("p t r e -> p t (r e)")

            def select(b):
                for t in range(TT):
                    op = dve.tensor_scalar(sel[:, t, :], iota, pmb[:, t, ds(b, 1)], None, ALU.is_equal)
                op.then_inc(s_sel, 1)

            def low(b, i):
                dve.wait_ge(s_wh, MU * b + (i + 1))
                part = slice(0, 2 * D - POOL_PART)
                dve.tensor_tensor(wr[:, i % SPLIT, 1, part], ring[:, i % RING, part], wr[:, i % SPLIT, 0, part].bitcast(F32), ALU.subtract).then_inc(s_wlv, 1)

            def add(b, js):
                for j in js:
                    dve.wait_ge(s_sc, 8 * b + j + 1)
                    t = j // 2
                    o = oacc[:, t, (j % 2) * 512:(j % 2 + 1) * 512]
                    dve.scalar_tensor_tensor(o, bank(4 + j % 2), wtb[:, t, ds(b, 1)], o, ALU.mult, ALU.add).then_inc(s_acc, 1)

            def rows_low(b, j):
                dve.wait_ge(s_xeh, 2 * b + j + 1)
                h = slice(4 * j, 4 * j + 4)
                dve.tensor_tensor(xe[:, 1, h, :], bank4(4 + j), xe[:, 0, h, :].bitcast(F32), ALU.subtract).then_inc(s_xel, 1)

            def moe(b, last):
                dve.wait_ge(s_acc, 8 * b + 1)
                for i in range(3, 7):
                    add(b, (2 * i - 6, 2 * i - 5))
                    low(b, i)
                low(b, 7)
                if not last:
                    dve.wait_ge(s_selp, b + 1)
                    select(b + 1)
                low(b, DC)
                low(b, DC + 1)
                dve.wait_ge(s_gate, b + 1)
                dve.tensor_tensor(hid.rearrange("p (n f) -> p n f", n=2), sgate.rearrange("p (n f) -> p n f", n=2), ps[:, 2:4, :], ALU.mult).then_inc(s_hid, 1)
                for j in range(2):
                    dve.wait_ge(s_hTh, 2 * b + j + 1)
                    h = slice(4 * j, 4 * j + 4)
                    dve.tensor_tensor(hT[:, 1, h, :], bank4(7 - j), hT[:, 0, h, :].bitcast(F32), ALU.subtract).then_inc(s_hTl, 1)
                if not last:
                    rows_low(b + 1, 0)
                low(b, DC + 2)
                low(b, DC + 3)
                if not last:
                    rows_low(b + 1, 1)
                    low(b + 1, 0)
                    low(b + 1, 1)
                dve.wait_ge(s_ydh, b + 1)
                two = lambda a: a.rearrange("p (n f) -> p n f", n=2)
                dve.tensor_tensor(two(yd[:, 1, :]), ps[:, 6:8, :], two(yd[:, 0, :].bitcast(F32)), ALU.subtract).then_inc(s_ydl, 1)
                if not last:
                    low(b + 1, 2)

            select(0)
            for i in range(3):
                low(0, i)
            rows_low(0, 0)
            rows_low(0, 1)
            with dve.Fori(0, final) as b:
                moe(b, False)
            moe(final, True)

            add(final + 1, range(8))
            dve.wait_ge(s_acc, 8 * final + 17)
            dve.wait_ge(ld_ln, 16 * 4)
            for t in range(TT):
                norm(t, lnr2, 3, TT + t + 1)

        @block.tensor
        def _(pe):
            mm = nc.tensor.matmul
            pe.wait_ge(s_const, CONSTS)
            pe.wait_ge(ld_x, 16 * TT)

            def x_chunk(k):
                for t in range(TT):
                    op = nc.tensor.transpose(ps[:, 1 + k % 7, t * P:(t + 1) * P], oacc[:, t, k * P:(k + 1) * P], ident)
                op.then_inc(s_xtp, 1)

            for k in range(7):
                x_chunk(k)
            pe.wait_ge(ld_small, 16 * 7)
            nc.tensor.transpose(ps[:, 0, 0:120], rows[0:120, 0, :], ident[0:120, 0:120]).then_inc(s_rowp, 1)
            nc.tensor.transpose(ps[:, 0, 128:144], rows[0:16, 1, :], ident[0:16, 0:16]).then_inc(s_rowp, 1)
            pe.wait_ge(s_rowc, 2)
            pe.wait_ge(s_adaA, DC)
            for j in range(16):
                op = mm(ps[:, 0, 160 + j:161 + j], accA[:, j * P:(j + 1) * P], ones[:, 0:1], start=True, stop=True)
            op.then_inc(s_modp, 1)
            pe.wait_ge(s_hraw, 1)
            x_chunk(7)

            def parts(u, slot, k, n):
                return wsplit[:, slot, 0, :].rearrange("p (k n) -> p k n", k=k), wsplit[:, slot, 1, :].rearrange("p (k n) -> p k n", k=k)

            def tile(u, slot, to):
                pe.wait_ge(s_ul, u + 1)
                wh, wl = parts(u, slot, DC, P)
                for k in range(DC):
                    mm(to, wh[:, k, :], hin[:, 0, k, :], start=(k == 0), stop=False)
                    mm(to, wh[:, k, :], hin[:, 1, k, :], start=False, stop=False)
                    op = mm(to, wl[:, k, :], hin[:, 0, k, :], start=False, stop=(k == DC - 1))
                op.then_inc(s_unit, 1)

            def xbc_tile(g, i):
                if i >= 2:
                    pe.wait_ge(s_cv, NT * g + i - 1)
                elif not isinstance(g, int):
                    pe.wait_ge(s_zc, ZT * (g - 1) + i + 3)
                tile(unit_x(g, i), i % 2, bank(i % 2))

            def z_tile(g, i):
                if i >= 2:
                    pe.wait_ge(s_zc, ZT * g + i - 1)
                elif i == 0:
                    pe.wait_ge(s_xw, 3 * g + 3)
                else:
                    pe.wait_ge(s_xdt, TT * g + 4)
                tile(unit_z(g, i), i % 2, bank(i % 2))

            pe.wait_ge(s_hinl, DC)
            pe.wait_ge(ld_wdt, 16)
            for k in range(DC):
                mm(ps[0:32, 3, :], wdt[:, k, :], hin[:, 0, k, :].bitcast(F32), start=(k == 0), stop=False)
                op = mm(ps[0:32, 3, :], wdt[:, k, :], hin[:, 1, k, :].bitcast(F32), start=False, stop=(k == DC - 1))
            op.then_inc(s_dtp, 1)
            xbc_tile(0, 0)
            xbc_tile(0, 1)
            pe.wait_ge(s_dtv, 4 + 2 * G)
            acl = acg.rearrange("p g (c t) -> p (g c) t", t=P)
            for j in range(HG):
                op = mm(ps[:, 4, j * 16:(j + 1) * 16], every8r[:, j:j + 1].broadcast_to([P, P]), acl[:, :, P - 1], start=True, stop=True)
            op.then_inc(s_elp, 1)
            pe.wait_ge(s_pre, 11)
            for k in range(TT):
                op = nc.tensor.transpose(ps[:, 5, k * 96:(k + 1) * 96], stk[0:96, k * P:(k + 1) * P], ident[0:96, 0:96])
            op.then_inc(s_tokp, 1)

            def acum_rows(g, h):
                if h < 2:
                    pe.wait_ge(s_xw, 3 * g + h + 1)
                else:
                    pe.wait_ge(s_e, HG * g + h - 1 + 1)
                mm(bank(2 + h % 2), every8r[:, h:h + 1].broadcast_to([P, P]),
                   acg[:, ds(g, 1), :].rearrange("p a t -> p (a t)"), start=True, stop=True).then_inc(s_abc, 1)

            def state_sum(g, k):
                pe.wait_ge(s_xw, 3 * g + k + 1)
                if k == 0:
                    pe.wait_ge(s_btok, g + 1)
                else:
                    pe.wait_ge(s_stu, 3 * g + k + 1)
                mm(bank(5), btok[:, k, :], xw[:, k, :], start=True, stop=True).then_inc(s_st, 1)

            def y_pair(g, q):
                pe.wait_ge(s_ch, HG * g + 2 * q + 2)
                if q == 0:
                    pe.wait_ge(s_stu, 3 * g + 4)
                    pe.wait_ge(s_oacc, 8 * g + 1)
                if q >= 2:
                    pe.wait_ge(s_y1, 4 * g + q - 1)
                for k in range(TT):
                    for hh in range(2):
                        h = 2 * q + hh
                        o = ps[hh * HD:(hh + 1) * HD, 6 + q % 2, k * P:(k + 1) * P]
                        op = mm(o, xdt[:, k, h * HD:(h + 1) * HD], mh[:, h % 4, k, :], start=True, stop=(k == 0))
                        if k:
                            op = mm(o, state[:, k - 1, h * HD:(h + 1) * HD], ch[:, h % 4, (k - 1) * P:k * P], start=False, stop=True)
                op.then_inc(s_y, 1)

            def turn(g, last):
                pe.wait_ge(s_silu, NT * (g + 1))
                pe.wait_ge(s_var, g + 1)
                for k in range(TT):
                    t = slice(k * P, (k + 1) * P)
                    op = mm(ps[:, 4, t], bT[:, t], cT[:, t], start=True, stop=True)
                op.then_inc(s_cb, 1)
                pe.wait_ge(s_stu, 3 * g + 1)
                for k in range(TT):
                    t = slice(k * P, (k + 1) * P)
                    op = nc.tensor.transpose(ps[:, 5, t], bT[:, t], ident)
                op.then_inc(s_btr, 1)
                for k in range(TT):
                    if k == 0:
                        pe.wait_ge(s_bcu, 2 * g + 1)
                    if k == 2:
                        pe.wait_ge(s_cv, NT * g + NT)
                    for j in range(4):
                        op = nc.tensor.transpose(ps[:, (2, 3, 0, 1)[k], j * P:(j + 1) * P], xT[:, j, k * P:(k + 1) * P], ident)
                    op.then_inc(s_xtr, 1)
                acum_rows(g, 0)
                acum_rows(g, 1)
                state_sum(g, 0)
                z_tile(g, 0)
                state_sum(g, 1)
                z_tile(g, 1)
                acum_rows(g, 2)
                state_sum(g, 2)
                acum_rows(g, 3)
                z_tile(g, 2)
                y_pair(g, 0)
                acum_rows(g, 4)
                acum_rows(g, 5)
                z_tile(g, 3)
                y_pair(g, 1)
                acum_rows(g, 6)
                acum_rows(g, 7)
                if not last:
                    xbc_tile(g + 1, 0)
                y_pair(g, 2)
                pe.wait_ge(s_adau, DC * g + DC + 1)
                pe.wait_ge(s_e, HG * g + HG + 1)
                for n in range(2):
                    mm(bank(2 + n), ones, acc[:, n * 512:(n + 1) * 512], start=True, stop=True).then_inc(s_bc, 1)
                if not last:
                    xbc_tile(g + 1, 1)
                y_pair(g, 3)
                for q in range(4):
                    if q == 2 and not last:
                        xbc_tile(g + 1, 2)
                    pe.wait_ge(s_sq, 4 * g + q + 1)
                    mm(bank(4), ones, ebc[:, q % 2, :], start=(q == 0), stop=(q == 3)).then_inc(s_ms, 1)
                if not last:
                    for i in range(3, NT):
                        xbc_tile(g + 1, i)
                pe.wait_ge(s_yl, 4 * g + 5)
                for q in range(OU):
                    pe.wait_ge(s_ul, unit_o(g, q, last) + 1)
                    wh, wl = parts(None, q % 2, 4, 256)
                    for j in range(2):
                        if q:
                            pe.wait_ge(s_oacc, 8 * g + 2 * q + j)
                        for t in (2 * j, 2 * j + 1):
                            to, tt = ps[:, 6 + j, (t % 2) * 256:(t % 2 + 1) * 256], slice(t * P, (t + 1) * P)
                            for k in range(4):
                                mm(to, ysplit[:, 0, k, tt], wh[:, k, :], start=(k == 0), stop=False)
                                mm(to, ysplit[:, 0, k, tt], wl[:, k, :], start=False, stop=False)
                                op = mm(to, ysplit[:, 1, k, tt], wh[:, k, :], start=False, stop=(k == 3))
                        op.then_inc(s_unit if j else s_out, 1)

            for i in range(2, NT):
                xbc_tile(0, i)
            pe.wait_ge(s_tok, 1)
            pe.wait_ge(s_el, 1)
            groups(pe, lambda g: turn(g, False), lambda g: turn(g, True))

            for t in range(TT):
                pe.wait_ge(s_h2f, t + 1)
                for j in range(2):
                    if t:
                        pe.wait_ge(s_h2tc, 2 * t - 1 + j)
                    for k in range(4):
                        op = nc.tensor.transpose(ps[:, 4 + j, k * P:(k + 1) * P], h2f[:, t % 2, (4 * j + k) * P:(4 * j + k + 1) * P], ident)
                    op.then_inc(s_h2t, 1)
                if t == 0:
                    pe.wait_ge(ld_r, 32)
                pe.wait_ge(s_h2tc, 2 * t + 2)
                for k in range(DC):
                    op = mm(ps[:, 6, t * E:(t + 1) * E], h2T[t % 2][:, k, :], rw[:, k, :], start=(k == 0), stop=(k == DC - 1))
                op.then_inc(s_lg, 1)
            pe.wait_ge(s_mask, 1)
            for t in range(TT):
                for u in range(t):
                    mm(ps[:, 7, t * E:(t + 1) * E], ones, mask[:, u, :], start=(u == 0), stop=False)
                mm(ps[:, 7, t * E:(t + 1) * E], before, mask[:, t, :], start=(t == 0), stop=True)
            for t in range(TT):
                op = mm(ps[:, 7, TT * E:TT * E + E], ones, mask[:, t, :], start=(t == 0), stop=(t == TT - 1))
            op.then_inc(s_pos, 1)

            pe.wait_ge(s_nblk, 1)
            final = pe.value_load(nblk_i[0:1, 1:2], min_val=E - 1, max_val=E * ROUNDS - 1)

            pe.sem_inc(s_xt, 1)

            def gather(b, j):
                if j == 0:
                    pe.wait_ge(s_sel, b + 1)
                for t in range(TT):
                    for part in range(2):
                        op = mm(bank(4 + j), sel[:, t, :], h2[:, part, t, j * 512:(j + 1) * 512], start=(t + part == 0), stop=(t == TT - 1 and part == 1))
                op.then_inc(s_ga, 1)

            def turn_rows(b, j):
                pe.wait_ge(s_xg, 2 * b + 2)
                for k in range(4):
                    d = 4 * j + k
                    op = nc.tensor.transpose(ps[:, 4 + j, k * P:(k + 1) * P], xg[:, d * P:(d + 1) * P], ident)
                op.then_inc(s_xt, 1)

            def scatter(b, j):
                if j == 0:
                    pe.wait_ge(s_ydl, b + 1)
                if j >= 2:
                    pe.wait_ge(s_acc, 8 * b + j - 1 + 1)
                t, n = j // 2, slice((j % 2) * 512, (j % 2 + 1) * 512)
                mm(bank(4 + j % 2), selT[:, t, :], yd[:, 0, n], start=True, stop=False)
                mm(bank(4 + j % 2), selT[:, t, :], yd[:, 1, n], start=False, stop=True).then_inc(s_sc, 1)

            def products(to, xh, xl, wh, wl, start, stop):
                n = range(len(to))
                for i in n:
                    mm(to[i], xh, wh[i], start=start, stop=False)
                for i in n:
                    mm(to[i], xh, wl[i], start=False, stop=False)
                for i in n:
                    op = mm(to[i], xl, wh[i], start=False, stop=stop)
                return op

            def moe(b, last):
                for i in range(DC):
                    if i % 4 == 0:
                        pe.wait_ge(s_xel, 2 * b + i // 4 + 1)
                    pe.wait_ge(s_wlv, MU * b + (i + 1))
                    pe.wait_ge(s_wlp, MU * b + (i + 1))
                    cols = [[wr[:, i % SPLIT, s, n * 512:(n + 1) * 512] for n in range(4)] for s in range(2)]
                    products([bank(n) for n in range(4)], xe[:, 0, i, :], xe[:, 1, i, :], cols[0], cols[1], i == 0, i == DC - 1).then_inc(s_wu, 1)
                    if i < 4:
                        if i == 0:
                            pe.wait_ge(s_xel, 2 * b + 2)
                        scatter(b, 2 * i)
                        scatter(b, 2 * i + 1)
                    if i == 4:
                        pe.wait_ge(s_acc, 8 * b + 7 + 1)
                        for t in range(TT):
                            op = nc.tensor.transpose(ps[:, 4, t * P:(t + 1) * P], sel[:, t, :].bitcast(F32), ident)
                        op.then_inc(s_selp, 1)
                pe.wait_ge(s_selT, b + 1)
                pe.wait_ge(s_acc, 8 * b + 8 + 1)
                if not last:
                    gather(b + 1, 0)
                    gather(b + 1, 1)
                pe.wait_ge(s_hid, b + 1)
                for j in range(2):
                    for k in range(4):
                        d = 4 * j + k
                        op = nc.tensor.transpose(ps[:, 7 - j, k * P:(k + 1) * P], hid[:, d * P:(d + 1) * P], ident)
                    op.then_inc(s_hp, 1)
                if not last:
                    turn_rows(b + 1, 0)
                pe.wait_ge(s_hTl, 2 * b + 2)
                for i in range(DC, MU):
                    pe.wait_ge(s_wlv, MU * b + (i + 1))
                    pe.wait_ge(s_wlp, MU * b + (i + 1))
                    for kk in range(2):
                        k = 2 * (i - DC) + kk
                        cols = [[wr[:, i % SPLIT, s, kk * D + n * 512:kk * D + (n + 1) * 512] for n in range(2)] for s in range(2)]
                        op = products([bank(6), bank(7)], hT[:, 0, k, :], hT[:, 1, k, :], cols[0], cols[1], k == 0, k == DC - 1)
                    op.then_inc(s_wu, 1)
                    if i == DC and not last:
                        turn_rows(b + 1, 1)

            pe.wait_ge(s_h2tc, 2 * TT)
            pe.wait_ge(s_h2l, TT)
            gather(0, 0)
            gather(0, 1)
            turn_rows(0, 0)
            turn_rows(0, 1)
            with pe.Fori(0, final) as b:
                moe(b, False)
            moe(final, True)
            for j in range(8):
                scatter(final + 1, j)


NAMES = ["x", "c", "ada_w", "ada_b", "ln1_g", "ln1_b", "ln2_g", "ln2_b", "ssd_w_in", "ssd_conv_w", "ssd_conv_b",
         "ssd_dt_bias", "ssd_a_log", "ssd_d", "ssd_norm_g", "ssd_w_out", "moe_w_up", "moe_w_down", "router_w", "router_b"]


def kernel(**inputs):
    import concourse.bacc as bacc
    from concourse.bass_utils import run_bass_kernel_spmd

    nc = bacc.Bacc("TRN2", target_bir_lowering=False, num_devices=1)
    arrays, args = {}, []
    for name in NAMES:
        a = np.ascontiguousarray(inputs[name])
        arrays[f"in_{name}"] = a
        args.append(nc.dram_tensor(f"in_{name}", a.shape, mybir.dt.from_np(a.dtype), kind="ExternalInput").ap())
    args.append(nc.dram_tensor("out_y", (1, T, D), F32, kind="ExternalOutput").ap())
    build(nc, *args)
    r = run_bass_kernel_spmd(nc, [arrays], core_ids=[0])
    return r.results[0]["out_y"]
```

```python
from contextlib import ExitStack

import numpy as np

import concourse.bass as bass
from concourse import mybir

F32 = mybir.dt.float32
F32R = mybir.dt.float32r
I32 = mybir.dt.int32
ALU = mybir.AluOpType
ACT = mybir.ActivationFunctionType
AX = mybir.AxisListType
ds = bass.ds

P = 128
D = 1024
T = 512
DC = D // P
TT = T // P
G = 4
HG = 8
HD = 64
NS = 128
DI = 2048
GW = DI // G
NTAP = 4
XBC = 2
NT = XBC + GW // P
ZT = GW // P
COL_X, COL_B, COL_C, COL_DT = DI, 2 * DI, 2 * DI + G * NS, 2 * DI + 2 * G * NS
E = 16
EG = 4
F = 1024
ROUNDS = T // P
ALPHA = 2.0 ** 0.25
EPS = 1e-5
MU = DC + DC // 2
CONSTS = 10
RING = SPLIT = 3
POOL_PART = 768


def build(nc, x, c, ada_w, ada_b, ln1_g, ln1_b, ln2_g, ln2_b, w_in, conv_w, conv_b, dt_bias, a_log,
          d_skip, norm_g, w_out, w_up, w_down, router_w, router_b, out):
    ctx = ExitStack()
    with ctx:
        def space(stack, name, words, dtype):
            whole = stack.enter_context(nc.sbuf_tensor(name, [P, words], dtype))
            top = [0]

            def place(n, at=None):
                if at is None:
                    at = top[0]
                    top[0] += n
                assert at + n <= words, (name, at + n)
                return whole[:, at:at + n]

            place.top = top
            return place

        def sem(name):
            return ctx.enter_context(nc.semaphore(name))

        place = space(ctx, "both", 10094, F32)
        ident = place(P)
        ones = place(P)
        causal = place(P)
        before = place(P)
        iota = place(P)
        taps = place(120).rearrange("p (k j) -> p k j", k=5)
        normg = place(16)
        dskip = place(16)
        ccol = place(DC)
        cact = place(DC)
        modc = place(16)
        onep = place(4)
        gmask = place(4)
        every8 = place(HG)
        epsc = place(1)
        dtb = place(1)
        aneg = place(1)
        tok = place(TT * 96).rearrange("p (c s h) -> p c s h", c=TT, s=3)
        elast = place(HG * G * TT).rearrange("p (j n) -> p j n", j=HG)
        oacc = place(TT * D).rearrange("p (t n) -> p t n", t=TT)
        st6 = place(12 * TT).rearrange("p (t s n) -> p t s n", t=TT, s=2)
        mv = place(2 * TT).rearrange("p (t n) -> p t n", t=TT)
        rstd = place(TT)
        shift = place(TT)
        mod_at = place.top[0]
        modr = place(4 * D).rearrange("p (g n) -> p g n", g=4)
        both = place

        nblk_i = ctx.enter_context(nc.sbuf_tensor("nblk_i", [1, 2], I32))

        half = ExitStack()
        place = space(half, "ssd_r", 2 * DC * T + 4 * D + 2 * 4 * T + G * T + HG, F32R)
        hin = place(2 * DC * T).rearrange("p (s k t) -> p s k t", s=2, k=DC)
        wsplit = place(4 * D).rearrange("p (u s n) -> p u s n", u=2, s=2)
        ysplit = place(2 * 4 * T).rearrange("p (s k t) -> p s k t", s=2, k=4)
        acg = place(G * T).rearrange("p (g t) -> p g t", g=G)
        every8r = place(HG)
        place = space(half, "ssd", 23724, F32)
        stage = place(2 * D).rearrange("p (u n) -> p u n", u=2)
        adaA_at = place.top[0]
        xT = place(4 * T).rearrange("p (k t) -> p k t", k=4)
        bT = place(T)
        cT = place(T)
        conv = place(2 * T).rearrange("p (s t) -> p s t", s=2)
        yT = place(4 * T).rearrange("p (k t) -> p k t", k=4)
        btok = place(TT * NS).rearrange("p (c n) -> p c n", c=TT)
        xdt = place(TT * GW).rearrange("p (c n) -> p c n", c=TT)
        xw = place(3 * GW).rearrange("p (c n) -> p c n", c=3)
        adaA = place(4 * 2 * D, adaA_at).rearrange("p (s n) -> p s n", s=4)
        cbm = place(TT * P).rearrange("p (c t) -> p c t", c=TT)
        seg = place(2 * T).rearrange("p (s c t) -> p s c t", s=2, c=TT)
        ebc_at = place.top[0]
        ebc = place(2 * T).rearrange("p (s t) -> p s t", s=2)
        m_at = place.top[0]
        mh = place(4 * T).rearrange("p (h c t) -> p h c t", h=4, c=TT)
        ch = place(4 * 3 * P).rearrange("p (h t) -> p h t", h=4)
        state_at = place.top[0]
        state = place(3 * GW).rearrange("p (c n) -> p c n", c=3)
        stmp = place(GW)
        rstd4 = place(TT)
        gtok = place(TT * 24).rearrange("p (c s j) -> p c s j", c=TT, s=3)
        gel = place(HG * TT).rearrange("p (j n) -> p j n", j=HG)
        gtaps = place(5 * NT).rearrange("p (k j) -> p k j", k=5)
        gnd = place(8).rearrange("p (s j) -> p s j", s=2)
        acc = place(D)
        ada = place(2 * D).rearrange("p (s n) -> p s n", s=2)
        hraw = ada.rearrange("p s (h t) -> p (s h) t", h=2)
        squares = [ebc[:, 0, :], ebc[:, 1, :]] + [mh[:, i].rearrange("p c t -> p (c t)") for i in range(2)]
        accA = place(2 * D, state_at)
        wdt = place(DC * 32, m_at).rearrange("p (k n) -> p k n", k=DC)
        dtsplit = [ysplit[:, part, 0, 0:DC * 32].rearrange("p (k n) -> p k n", k=DC) for part in range(2)]
        rows = place(2 * P, m_at + 256).rearrange("p (s n) -> p s n", s=2)
        dtv = [place(T, m_at + 512 * (i + 1)) for i in range(5)]
        stk = place(T, m_at + 512 * 6)
        half.close()

        half = ExitStack()
        place = space(half, "moe", 19488 - 4096, F32)
        xt = place(TT * D).rearrange("p (t n) -> p t n", t=TT)
        lnr = place(2 * D).rearrange("p (a n) -> p a n", a=2)
        hid = lnr[:, 0, :]
        sgate = lnr[:, 1, :]
        ring = place(RING * 2 * D).rearrange("p (u n) -> p u n", u=RING)
        h2T = [ring[:, RING - 1, s * D:(s + 1) * D].rearrange("p (k s) -> p k s", k=DC) for s in range(2)]
        lnr2 = ring[:, 0, :].rearrange("p (a n) -> p a n", a=2)
        rowtmp = ring[:, 0, 0:D]
        h2f = [place(D), place(D), modr[:, 0, :]]
        h2f.append(h2f[0])
        xg = h2f[0]
        rw = place(DC * E).rearrange("p (k e) -> p k e", k=DC)
        rb = place(E)
        nbf = place(2)
        r3 = lambda w, n=E: place(w * n).rearrange("p (t e) -> p t e", e=n)
        prob, mask, wts, pm = r3(TT), r3(TT), r3(TT), r3(TT)
        pmx = place(TT * ROUNDS * E).rearrange("p (t r e) -> p t r e", t=TT, r=ROUNDS)
        wtb = place(TT * (1 + ROUNDS * E)).rearrange("p (t b) -> p t b", t=TT)
        m0 = [mod_at]

        def r4(w, n=E):
            m0[0] += w * n
            return both(w * n, m0[0] - w * n)

        selp, rank, tie = (r4(TT).rearrange("p (t e) -> p t e", e=E) for _ in range(3))
        gsum, grank, gtie = (r4(TT, EG).rearrange("p (t e) -> p t e", e=EG) for _ in range(3))
        red, red2, cnt = r4(TT, 1), r4(TT, 1), r4(1)
        cum = r4(TT + 1).rearrange("p (t e) -> p t e", e=E)
        place = space(half, "moe_r", 23552 + 4096, F32R)
        wr = place(SPLIT * 4 * D).rearrange("p (u s n) -> p u s n", u=SPLIT, s=2)
        h2 = place(2 * TT * D).rearrange("p (s t n) -> p s t n", s=2, t=TT)
        xe = place(2 * DC * P).rearrange("p (s k t) -> p s k t", s=2, k=DC)
        hT = place(2 * DC * P).rearrange("p (s k t) -> p s k t", s=2, k=DC)
        yd = place(2 * D).rearrange("p (s n) -> p s n", s=2)
        sel = place(TT * P).rearrange("p (t s) -> p t s", t=TT)
        selT = place(TT * P).rearrange("p (t s) -> p t s", t=TT)
        half.close()

        ps = ctx.enter_context(nc.psum_tensor("ps", [P, 8, 512], F32))
        bank = lambda i: ps[:, i, :]
        bank4 = lambda i: ps[:, i, :].rearrange("p (c t) -> p c t", c=4)

        def sems(names):
            return [sem(n) for n in names.split()]

        ld_c, ld_small, ld_x, ld_wdt, ld_b0, ld_bg, ld_x2, ld_ln, ld_r, ld_out = sems("ld_c ld_small ld_x ld_wdt ld_b0 ld_bg ld_x2 ld_ln ld_r ld_out")
        ld_adaA = [sem(f"ld_adaA{i}") for i in range(4)]
        ld_ada = [sem(f"ld_ada{i}") for i in range(2)]
        ld_u = [sem(f"ld_u{i}") for i in range(2)]
        s_const, s_cact, s_acc0, s_adaA, s_modp, s_modc, s_rowp, s_rowc = sems("s_const s_cact s_acc0 s_adaA s_modp s_modc s_rowp s_rowc")
        s_xtp, s_hraw, s_hinh, s_hinl, s_hinv, s_dth, s_dtl, s_dtp, s_dtv, s_pre, s_prea, s_tokp, s_tok, s_elp, s_el = sems("s_xtp s_hraw s_hinh s_hinl s_hinv s_dth s_dtl s_dtp s_dtv s_pre s_prea s_tokp s_tok s_elp s_el")
        s_uh, s_ul, s_unit = sems("s_uh s_ul s_unit")
        s_cv0, s_tap, s_cv, s_silu, s_gtap, s_zc, s_zs = sems("s_cv0 s_tap s_cv s_silu s_gtap s_zc s_zs")
        s_cb, s_cbm, s_btr, s_btok, s_xtr, s_xdt, s_xw, s_st, s_stu, s_stm, s_gc = sems("s_cb s_cbm s_btr s_btok s_xtr s_xdt s_xw s_st s_stu s_stm s_gc")
        s_abc, s_seg, s_dec, s_e, s_m, s_ch, s_y, s_y1, s_yz = sems("s_abc s_seg s_dec s_e s_m s_ch s_y s_y1 s_yz")
        s_sq, s_ms, s_var, s_sqrt, s_rs, s_yh, s_yl = sems("s_sq s_ms s_var s_sqrt s_rs s_yh s_yl")
        s_out, s_oacc, s_adau, s_bc, s_bcu, s_accz = sems("s_out s_oacc s_adau s_bc s_bcu s_accz")
        s_n, s_fold, s_var1, s_sd1, s_shift, s_nrm, s_h2m, s_h2f, s_h2h, s_h2l, s_x1v, s_x1p, s_zero = sems("s_n s_fold s_var1 s_sd1 s_shift s_nrm s_h2m s_h2f s_h2h s_h2l s_x1v s_x1p s_zero")
        s_h2t, s_h2tc, s_lg, s_om, s_gain, s_done = sems("s_h2t s_h2tc s_lg s_om s_gain s_done")
        s_mx, s_ex, s_mask, s_pos, s_nblk = sems("s_mx s_ex s_mask s_pos s_nblk")
        ld_w = [sem(f"ld_w{i}") for i in range(RING)]
        s_wh, s_wlv, s_wlp, s_wu = sems("s_wh s_wlv s_wlp s_wu")
        s_sel, s_ga, s_xg, s_xt, s_xeh, s_xel, s_selp, s_selT, s_gate, s_hid, s_hp, s_hTh, s_hTl, s_ydh, s_ydl, s_sc, s_acc = sems("s_sel s_ga s_xg s_xt s_xeh s_xel s_selp s_selT s_gate s_hid s_hp s_hTh s_hTl s_ydh s_ydl s_sc s_acc")

        small = nc.allow_non_contiguous_dma("columns of a few constants")
        ctx.enter_context(small)
        block = ctx.enter_context(nc.Block())

        def groups(run, body, last):
            with run.Fori(0, G - 1) as g:
                body(g)
            last(G - 1)

        ZU, XU, OU = ZT, NT, 4
        TU = ZU + XU + OU
        assert XU % 2 == 0 and TU % 2 == 0 and ZU % 2 == 0

        def unit_z(g, i):
            return TU * g + (XU + i)

        def unit_x(g, i):
            return i if isinstance(g, int) and g == 0 else TU * g + (i - TU + XU + ZU)

        def unit_o(g, q, last):
            return TU * g + (XU + ZU + (0 if last else XU) + q)

        @block.sync
        def _(sp):
            sp.dma_start(ccol, c.rearrange("a (p k) -> p (a k)", k=DC)).then_inc(ld_c, 16)
            adaA_v = ada_w.rearrange("l (p k) n -> p (l k) n", k=DC)
            for k in range(4):
                if k == 2:
                    sp.wait_ge(s_acc0, 1)
                    sp.dma_start(accA[0:1, :], ada_b[0:1, 0:2 * D]).then_inc(ld_b0, 16)
                sp.dma_start(adaA[:, k, :], adaA_v[:, k, 0:2 * D]).then_inc(ld_adaA[k], 16)
            for t in range(TT):
                sp.dma_start(oacc[:, t, :], x[0, t * P:(t + 1) * P, :]).then_inc(ld_x, 16)
            sp.dma_start(rows[0:96, 0, :], conv_w.rearrange("a k (j p) -> (a k j) p", p=P)).then_inc(ld_small, 16)
            sp.dma_start(rows[96:120, 0, :], conv_b.rearrange("a (j p) -> (a j) p", p=P)).then_inc(ld_small, 16)
            sp.dma_start(rows[0:16, 1, :], norm_g.rearrange("a (j p) -> (a j) p", p=P)).then_inc(ld_small, 16)
            for half in range(2):
                sp.dma_start(dskip[half * HD:(half + 1) * HD, :],
                             d_skip.rearrange("a (j two) -> two (a j)", two=2)[half:half + 1, :].broadcast_to([HD, 16])).then_inc(ld_small, 16)
            sp.dma_start(dtb[0:32, :], dt_bias.rearrange("a h -> h a")).then_inc(ld_small, 16)
            sp.dma_start(aneg[0:32, :], a_log.rearrange("a h -> h a")).then_inc(ld_small, 16)
            w_v = w_in.rearrange("l (k p) n -> p (l k) n", p=P)

            def load_tile(u, slot, col):
                if not (isinstance(u, int) and u < 2):
                    sp.wait_ge(s_ul, u - 1)
                sp.dma_start(stage[:, slot, :].rearrange("p (k n) -> p k n", k=DC), w_v[:, :, ds(col, P)]).then_inc(ld_u[slot], 16)

            def load_x(g, i):
                load_tile(unit_x(g, i), i % 2, g * NS + (COL_B, COL_C)[i] if i < XBC else g * GW + (COL_X + (i - XBC) * P))

            sp.dma_start(wdt, w_v[:, :, COL_DT:COL_DT + 32]).then_inc(ld_wdt, 16)
            load_x(0, 0)
            load_x(0, 1)
            for k in range(4, 8):
                sp.wait_ge(s_adaA, k - 3)
                sp.dma_start(adaA[:, k % 4, :], adaA_v[:, k, 0:2 * D]).then_inc(ld_adaA[k % 4], 16)
            for i in range(2, NT):
                load_x(0, i)
            wo_v = w_out.rearrange("l (g k p) n -> p (l g) k n", p=P, k=4)

            def ada_piece(g, k):
                sp.wait_ge(s_adau, DC * g + max(k, 1))
                sp.dma_start(ada[:, k % 2, :], adaA_v[:, k, ds(g * D + 2 * D, D)]).then_inc(ld_ada[k % 2], 16)

            def turn(g, last):
                load_z = lambda i: load_tile(unit_z(g, i), i % 2, g * GW + i * P)
                load_z(0)
                load_z(1)
                sp.wait_ge(s_accz, g + 1)
                sp.dma_start(acc[0:1, :], ada_b[0:1, ds(g * D + 2 * D, D)]).then_inc(ld_bg, 16)
                ada_piece(g, 0)
                ada_piece(g, 1)
                load_z(2)
                ada_piece(g, 2)
                load_z(3)
                ada_piece(g, 3)
                for i in range(2):
                    if not last:
                        load_x(g + 1, i)
                    ada_piece(g, 2 * i + 4)
                    ada_piece(g, 2 * i + 5)
                if not last:
                    for i in range(2, NT):
                        load_x(g + 1, i)
                for q in range(OU):
                    if last and q == 2:
                        sp.wait_ge(s_unit, unit_z(G - 1, ZU))
                        for i, row in enumerate((ln1_g, ln1_b)):
                            sp.dma_start(lnr[:, i, :], row[0:1, :].broadcast_to([P, D])).then_inc(ld_ln, 16)
                        for t in range(TT):
                            sp.dma_start(xt[:, t, :], x[0, t * P:(t + 1) * P, :]).then_inc(ld_x2, 16)
                    sp.wait_ge(s_ul, unit_o(g, q, last) - 1)
                    sp.dma_start(stage[:, q % 2, :].rearrange("p (k n) -> p k n", k=4),
                                 wo_v[:, ds(g, 1), :, q * 256:(q + 1) * 256].rearrange("p a k n -> p (a k) n")).then_inc(ld_u[q % 2], 16)

            groups(sp, lambda g: turn(g, False), lambda g: turn(g, True))

            sp.wait_ge(s_oacc, 32 + 1)
            sp.wait_ge(s_fold, 3)
            sp.dma_start(rw, router_w.rearrange("(k p) e -> p k e", p=P)).then_inc(ld_r, 16)
            sp.dma_start(rb, router_b.rearrange("(a e) -> a e", a=1).broadcast_to([P, E])).then_inc(ld_r, 16)
            up_v = w_up.rearrange("l e (k p) n -> (l e) p k n", p=P)
            dn_v = w_down.rearrange("l e (k p) n -> (l e) p k n", p=P)

            def load_unit(e, i):
                if i < DC:
                    sp.dma_start(ring[:, i % RING, :], up_v[ds(e, 1), :, i, :].rearrange("a p n -> p (a n)")).then_inc(ld_w[i % RING], 16)
                else:
                    j = 2 * (i - DC)
                    sp.dma_start(ring[:, i % RING, :].rearrange("p (k n) -> p k n", k=2),
                                 dn_v[ds(e, 1), :, j:j + 2, :].rearrange("a p k n -> p (a k) n")).then_inc(ld_w[i % RING], 16)

            for i in range(RING - 1):
                load_unit(0, i)
            sp.wait_ge(s_lg, TT)
            load_unit(0, RING - 1)
            for i in range(RING, MU):
                sp.wait_ge(s_wlv, i - RING + 1)
                sp.wait_ge(s_wlp, i - RING + 1)
                load_unit(0, i)
            sp.wait_ge(s_nblk, 1)
            nblk = sp.value_load(nblk_i[0:1, 0:1], min_val=E, max_val=E * ROUNDS)
            with sp.Fori(1, nblk) as b:
                e = sp.snap(b % E)
                for i in range(MU):
                    sp.wait_ge(s_wlv, MU * b + (i - RING + 1))
                    sp.wait_ge(s_wlp, MU * b + (i - RING + 1))
                    load_unit(e, i)
            sp.wait_ge(s_wlv, MU * nblk)
            sp.wait_ge(s_wlp, MU * nblk)
            for i, row in enumerate((ln2_g, ln2_b)):
                sp.dma_start(lnr2[:, i, :], row[0:1, :].broadcast_to([P, D])).then_inc(ld_ln, 16)
            for t in range(TT):
                sp.wait_ge(s_done, t + 1)
                sp.dma_start(out[0, t * P:(t + 1) * P, :], xt[:, t, :]).then_inc(ld_out, 16)
            sp.wait_ge(ld_out, 16 * TT)

        @block.gpsimd
        def _(pool):
            pool.memset(ones, 1.0).then_inc(s_const, 1)
            pool.memset(epsc, EPS).then_inc(s_const, 1)
            pool.memset(onep, 1.0).then_inc(s_const, 1)
            pool.iota(iota, pattern=[[1, P]], base=0, channel_multiplier=0, allow_small_or_imprecise_dtypes=True).then_inc(s_const, 1)
            pool.wait_ge(s_const, 4)
            pool.memset(onep[:, 1:2], 0.0).then_inc(s_const, 1)
            sel_of = lambda out, op, base, pattern, cm: pool.affine_select(out=out, in_=ones[:, 0:out.free_size()], compare_op=op, fill=0.0, base=base, pattern=pattern, channel_multiplier=cm)
            sel_of(causal, ALU.is_ge, 0, [[1, P]], -1).then_inc(s_const, 1)
            sel_of(before, ALU.is_ge, -1, [[1, P]], -1).then_inc(s_const, 1)
            sel_of(ident, ALU.is_equal, 0, [[1, P]], -1).then_inc(s_const, 1)
            sel_of(gmask, ALU.is_ge, 0, [[-HG, G]], 1).then_inc(s_const, 1)
            pool.wait_ge(s_const, 9)
            pool.affine_select(out=gmask, in_=gmask, compare_op=ALU.is_ge, fill=0.0, base=HG - 1,
                               pattern=[[HG, G]], channel_multiplier=-1).then_inc(s_const, 1)

            def unit_low(u, slot):
                pool.wait_ge(s_uh, u + 1)
                pool.tensor_tensor(wsplit[:, slot, 1, :], stage[:, slot, :], wsplit[:, slot, 0, :].bitcast(F32), ALU.subtract).then_inc(s_ul, 1)

            unit_low(0, 0)
            unit_low(1, 1)
            pool.wait_ge(s_dth, 1)
            pool.tensor_tensor(dtsplit[1], wdt, dtsplit[0].bitcast(F32), ALU.subtract).then_inc(s_dtl, 1)
            for k in range(0, DC, 2):
                pool.wait_ge(s_hinh, k + 1)
                pool.tensor_tensor(hin[:, 1, k, :], hraw[:, k % 4, :], hin[:, 0, k, :].bitcast(F32), ALU.subtract).then_inc(s_hinl, 1)
            pool.wait_ge(s_xtp, DC)
            pool.memset(oacc, 0.0)
            pool.memset(acc, 0.0).then_inc(s_accz, 1)
            for i in range(2, XU):
                unit_low(i, i % 2)

            def decayed_c(g, h):
                pool.wait_ge(s_e, HG * g + h + 2)
                if h >= 4:
                    pool.wait_ge(s_y, 4 * g + (h - 4) // 2 + 1)
                pool.tensor_tensor(ch[:, h % 4, :], cT[:, P:], ebc[:, h % 2, P:], ALU.mult).then_inc(s_ch, 1)

            def turn(g, last):
                heads_after = {1: (0, 1), 2: (2,), 3: (3,), 4: (4, 5), 5: (6, 7)}
                for i in range(TU - (XU if last else 0)):
                    unit_low(TU * g + (XU + i), i % 2)
                    for h in heads_after.get(i, ()):
                        decayed_c(g, h)
                    if last and i == 7:
                        fold_rows()

            def fold_rows():
                pool.wait_ge(ld_ln, 16 * 2)
                pool.wait_ge(s_bcu, 2 * 3 + 1)
                pool.tensor_tensor(rowtmp, lnr[:, 1, :], modr[:, 2, :], ALU.mult).then_inc(s_fold, 1)
                pool.wait_ge(s_fold, 1)
                pool.tensor_tensor(modr[:, 1, :], rowtmp, modr[:, 1, :], ALU.add).then_inc(s_fold, 1)
                pool.tensor_tensor(modr[:, 2, :], lnr[:, 0, :], modr[:, 2, :], ALU.mult).then_inc(s_fold, 1)

            groups(pool, lambda g: turn(g, False), lambda g: turn(g, True))

            pool.wait_ge(s_oacc, 32 + 1)
            pool.memset(yd.bitcast(F32), 0.0)
            pool.memset(selT.bitcast(F32), 0.0).then_inc(s_zero, 1)

            pool.wait_ge(s_fold, 3)
            pool.wait_ge(s_nrm, 2)
            pool.tensor_tensor(h2f[1], xt[:, 1, :], modr[:, 2, :], ALU.mult).then_inc(s_h2m, 1)
            for t in range(TT):
                pool.wait_ge(s_h2h, t + 1)
                pool.tensor_tensor(h2[:, 1, t, :], h2f[t], h2[:, 0, t, :].bitcast(F32), ALU.subtract).then_inc(s_h2l, 1)

            for i in range(3):
                pool.wait_ge(s_wh, i + 1)
                for part, done in ((slice(0, 2 * D - POOL_PART), s_wlv), (slice(2 * D - POOL_PART, 2 * D), s_wlp)):
                    pool.tensor_tensor(wr[:, i % SPLIT, 1, part], ring[:, i % RING, part], wr[:, i % SPLIT, 0, part].bitcast(F32), ALU.subtract).then_inc(done, 1)
            pool.memset(oacc, 0.0).then_inc(s_zero, 1)
            pool.wait_ge(s_h2f, TT)
            for n, t in enumerate((2, 3)):
                pool.tensor_tensor(xt[:, t, :], xt[:, t, :], lnr[:, 0, :], ALU.mult).then_inc(s_x1p, 1)
                pool.wait_ge(s_x1p, 2 * n + 1)
                pool.tensor_tensor(xt[:, t, :], xt[:, t, :], lnr[:, 1, :], ALU.add).then_inc(s_x1p, 1)

            def low(b, i):
                pool.wait_ge(s_wh, MU * b + (i + 1))
                part = slice(2 * D - POOL_PART, 2 * D)
                pool.tensor_tensor(wr[:, i % SPLIT, 1, part], ring[:, i % RING, part], wr[:, i % SPLIT, 0, part].bitcast(F32), ALU.subtract).then_inc(s_wlp, 1)

            for i in range(3, MU):
                low(0, i)
            pool.wait_ge(s_nblk, 1)
            nblk = pool.value_load(nblk_i[0:1, 0:1], min_val=E, max_val=E * ROUNDS)
            with pool.Fori(1, nblk) as b:
                for i in range(MU):
                    low(b, i)

            for t in (1, 3):
                pool.wait_ge(s_acc, 8 * nblk + (2 * t + 3))
                pool.tensor_tensor(oacc[:, t, :], oacc[:, t, :], modr[:, 3, :], ALU.mult).then_inc(s_om, 1)
            pool.wait_ge(ld_ln, 16 * 4)
            for t in range(3):
                pool.wait_ge(s_nrm, TT + t + 1)
                pool.tensor_tensor(xt[:, t, :], xt[:, t, :], lnr2[:, 0, :], ALU.mult).then_inc(s_gain, 1)

        @block.scalar
        def _(act):
            act.sem_inc(s_e, 1)
            act.wait_ge(ld_c, 16)
            act.activation(cact, ccol, ACT.Silu).then_inc(s_cact, 1)
            def unit_high(u, slot, nth):
                act.wait_ge(ld_u[slot], 16 * nth)
                if not (isinstance(u, int) and u < 2):
                    act.wait_ge(s_unit, u - 1)
                act.activation(wsplit[:, slot, 0, :], stage[:, slot, :], ACT.Identity).then_inc(s_uh, 1)
            unit_high(0, 0, 1)
            unit_high(1, 1, 1)
            act.wait_ge(ld_wdt, 16)
            act.activation(dtsplit[0], wdt, ACT.Identity).then_inc(s_dth, 1)
            act.wait_ge(ld_small, 16 * 7)
            act.activation(aneg[0:32, :], aneg[0:32, :], ACT.Exp).then_inc(s_prea, 1)
            for k in range(DC):
                act.wait_ge(s_hraw, k + 1)
                act.activation(hin[:, 0, k, :], hraw[:, k % 4, :], ACT.Identity).then_inc(s_hinh, 1)
            act.wait_ge(s_dtp, 1)
            act.activation(dtv[0][0:32], ps[0:32, 3, :], ACT.Identity, bias=dtb[0:32]).then_inc(s_prea, 1)
            act.wait_ge(s_pre, 1)
            act.activation(dtv[1][0:32], dtv[1][0:32], ACT.Exp, scale=-1.0).then_inc(s_prea, 1)
            act.wait_ge(s_pre, 2)
            act.activation(dtv[4][0:32], dtv[2][0:32], ACT.Ln).then_inc(s_prea, 1)

            def turn_unit(g, i):
                unit_high(TU * g + (XU + i), i % 2, TU // 2 * g + (XU // 2 + i // 2 + 1))

            def conv0(g, i):
                act.wait_ge(s_unit, unit_x(g, i) + 1)
                if i == 0:
                    act.wait_ge(s_gtap, 3 * g + 3)
                if i >= 2 or not (isinstance(g, int) and g == 0):
                    act.wait_ge(s_silu, NT * g + i - 1)
                act.activation(conv[:, i % 2, :], bank(i % 2), ACT.Identity, bias=gtaps[:, 4, i:i + 1],
                               scale=gtaps[:, 3, i:i + 1]).then_inc(s_cv0, 1)

            def silu(g, i):
                act.wait_ge(s_cv, NT * g + i + 1)
                to = bT if i == 0 else cT if i == 1 else xT[:, i - XBC, :]
                act.activation(to, conv[:, i % 2, :], ACT.Silu).then_inc(s_silu, 1)

            def zcopy(g, i):
                act.wait_ge(s_unit, unit_z(g, i) + 1)
                act.activation(yT[:, i, :], bank(i % 2), ACT.Identity).then_inc(s_zc, 1)

            def exps(g, h):
                act.wait_ge(s_seg, HG * g + h + 1)
                act.activation(seg[:, h % 2], seg[:, h % 2], ACT.Exp).then_inc(s_dec, 1)
                if h >= 2:
                    act.wait_ge(s_ch, HG * g + h - 1)
                act.activation(ebc[:, h % 2, :], bank(2 + h % 2), ACT.Exp).then_inc(s_e, 1)

            def square(g, q):
                act.wait_ge(s_yz, 4 * g + q + 1)
                if q == 0:
                    act.wait_ge(s_ch, HG * g + HG)
                act.activation(squares[q], yT[:, q, :], ACT.Square).then_inc(s_sq, 1)

            def turn(g, last):
                turn_unit(g, 1)
                act.wait_ge(s_btr, g + 1)
                act.activation(btok, bank4(5), ACT.Identity).then_inc(s_btok, 1)
                act.wait_ge(s_yl, 4 * g + 1)
                exps(g, 0)
                exps(g, 1)
                zcopy(g, 0)
                turn_unit(g, 2)
                exps(g, 2)
                zcopy(g, 1)
                turn_unit(g, 3)
                exps(g, 3)
                zcopy(g, 2)
                turn_unit(g, 4)
                exps(g, 4)
                exps(g, 5)
                zcopy(g, 3)
                turn_unit(g, 5)
                exps(g, 6)
                exps(g, 7)
                act.wait_ge(s_zc, ZT * (g + 1))
                act.activation(yT, yT, ACT.Silu).then_inc(s_zs, 1)
                if not last:
                    conv0(g + 1, 0)
                    turn_unit(g, 6)
                square(g, 0)
                square(g, 1)
                if not last:
                    silu(g + 1, 0)
                    conv0(g + 1, 1)
                    turn_unit(g, 7)
                    silu(g + 1, 1)
                square(g, 2)
                square(g, 3)
                for q in range(4):
                    act.activation(ysplit[:, 0, q, :], yT[:, q, :], ACT.Identity, scale=gnd[:, 0, q:q + 1]).then_inc(s_yh, 1)
                if not last:
                    conv0(g + 1, 2)
                    turn_unit(g, 8)
                act.wait_ge(s_var, g + 2)
                act.activation(rstd4, rstd4, ACT.Sqrt).then_inc(s_sqrt, 1)
                if not last:
                    conv0(g + 1, 3)
                    turn_unit(g, 9)
                if last:
                    turn_unit(g, 6)
                    turn_unit(g, 7)
                else:
                    for i in (4, 5):
                        silu(g + 1, i - 2)
                        conv0(g + 1, i)
                        turn_unit(g, i + 6)
                    silu(g + 1, 4)
                    silu(g + 1, 5)
                    turn_unit(g, 12)
                    turn_unit(g, 13)
                    turn_unit(g + 1, 0)

            for i in range(2):
                conv0(0, i)
                unit_high(i + 2, i % 2, 2)
            act.wait_ge(s_pre, 10)
            act.activation(dtv[1][0:32], dtv[1][0:32], ACT.Exp).then_inc(s_prea, 1)
            silu(0, 0)
            silu(0, 1)
            for i in range(2, 4):
                conv0(0, i)
                unit_high(i + 2, i % 2, 3)
            silu(0, 2)
            act.wait_ge(s_elp, 1)
            act.activation(elast, ps[:, 4, 0:P].rearrange("p (j n) -> p j n", j=HG), ACT.Exp).then_inc(s_el, 1)
            silu(0, 3)
            conv0(0, 4)
            conv0(0, 5)
            silu(0, 4)
            silu(0, 5)
            turn_unit(0, 0)
            groups(act, lambda g: turn(g, False), lambda g: turn(g, True))

            def router_rows(t):
                for j in range(2):
                    act.wait_ge(s_h2t, 2 * t + j + 1)
                    if t >= 2:
                        act.wait_ge(s_lg, t - 1)
                    act.activation(h2T[t % 2][:, 4 * j:4 * j + 4, :], bank4(4 + j), ACT.Identity).then_inc(s_h2tc, 1)

            def normalise(t):
                act.activation(xt[:, t, :], xt[:, t, :], ACT.Identity, bias=shift[:, t:t + 1], scale=rstd[:, t:t + 1]).then_inc(s_nrm, 1)

            act.wait_ge(s_var1, 1)
            act.activation(rstd, mv[:, :, 1], ACT.Sqrt, bias=epsc).then_inc(s_sd1, 1)
            act.wait_ge(s_shift, 1)
            for t in range(TT):
                normalise(t)
            for t in range(TT):
                act.wait_ge(s_h2f, t + 1)
                act.activation(h2[:, 0, t, :], h2f[t], ACT.Identity).then_inc(s_h2h, 1)
                router_rows(t)

            def high(b, i):
                act.wait_ge(ld_w[i % RING], 16 * (MU // RING) * b + 16 * (i // RING + 1))
                if not (isinstance(b, int) and i < SPLIT):
                    act.wait_ge(s_wu, MU * b + (i - SPLIT + 1))
                act.activation(wr[:, i % SPLIT, 0, :], ring[:, i % RING, :], ACT.Identity).then_inc(s_wh, 1)

            def gathered(b, j):
                act.wait_ge(s_ga, 2 * b + j + 1)
                if j == 0:
                    act.wait_ge(s_xt, 2 * b + 1)
                act.activation(xg[:, j * 512:(j + 1) * 512], bank(4 + j), ACT.Identity).then_inc(s_xg, 1)

            def rows_high(b, j):
                act.wait_ge(s_xt, 2 * b + j + 2)
                act.activation(xe[:, 0, 4 * j:4 * j + 4, :], bank4(4 + j), ACT.Identity).then_inc(s_xeh, 1)

            def moe(b, last):
                for i in range(3, DC):
                    high(b, i)
                act.wait_ge(s_selp, b + 1)
                act.activation(selT, bank4(4), ACT.Identity).then_inc(s_selT, 1)
                high(b, DC)
                high(b, DC + 1)
                act.wait_ge(s_wu, MU * b + DC)
                act.wait_ge(s_x1v, 4)
                act.wait_ge(s_x1p, 4)
                act.activation(sgate.rearrange("p (n f) -> p n f", n=2), ps[:, 0:2, :], ACT.Silu).then_inc(s_gate, 1)
                if not last:
                    gathered(b + 1, 0)
                    gathered(b + 1, 1)
                for j in range(2):
                    act.wait_ge(s_hp, 2 * b + j + 1)
                    act.activation(hT[:, 0, 4 * j:4 * j + 4, :], bank4(7 - j), ACT.Identity).then_inc(s_hTh, 1)
                if not last:
                    rows_high(b + 1, 0)
                high(b, DC + 2)
                high(b, DC + 3)
                if not last:
                    rows_high(b + 1, 1)
                    high(b + 1, 0)
                    high(b + 1, 1)
                act.wait_ge(s_wu, MU * b + MU)
                act.activation(yd[:, 0, :].rearrange("p (n f) -> p n f", n=2), ps[:, 6:8, :], ACT.Identity).then_inc(s_ydh, 1)
                if not last:
                    high(b + 1, 2)

            high(0, 0)
            high(0, 1)
            act.wait_ge(s_mx, 1)
            act.activation(prob, prob, ACT.Exp).then_inc(s_ex, 1)
            high(0, 2)
            act.activation(rstd, rstd, ACT.Silu)
            gathered(0, 0)
            gathered(0, 1)
            rows_high(0, 0)
            rows_high(0, 1)
            act.wait_ge(s_nblk, 1)
            final = act.value_load(nblk_i[0:1, 1:2], min_val=E - 1, max_val=E * ROUNDS - 1)
            with act.Fori(0, final) as b:
                moe(b, False)
            moe(final, True)

            for t in range(TT):
                act.wait_ge(s_var1, t + 2)
                act.activation(rstd[:, t:t + 1], mv[:, t, 1:2], ACT.Sqrt, bias=epsc).then_inc(s_sd1, 1)
                act.wait_ge(s_shift, t + 2)
                normalise(t)

        @block.vector
        def _(dve):
            for s in (s_oacc, s_var, s_stu, s_adau, s_yl, s_acc, s_ydl, s_bcu):
                dve.sem_inc(s, 1)
            dve.memset(accA, 0.0).then_inc(s_acc0, 1)
            dve.memset(acg.bitcast(F32), 0.0)
            dve.wait_ge(s_cact, 1)
            dve.wait_ge(ld_b0, 16)
            for k in range(DC):
                dve.wait_ge(ld_adaA[k % 4], 16 * (k // 4 + 1))
                if k:
                    dve.wait_ge(s_adaA, k)
                dve.scalar_tensor_tensor(accA, adaA[:, k % 4, :], cact[:, k:k + 1], accA, ALU.mult, ALU.add).then_inc(s_adaA, 1)
            dve.wait_ge(s_rowp, 2)
            dve.tensor_copy(taps, ps[:, 0, 0:120].rearrange("p (k j) -> p k j", k=5)).then_inc(s_rowc, 1)
            dve.tensor_copy(normg, ps[:, 0, 128:144]).then_inc(s_rowc, 1)
            dve.wait_ge(s_modp, 1)
            dve.tensor_copy(modc[:, 0:DC], ps[:, 0, 160:160 + DC]).then_inc(s_modc, 1)
            dve.tensor_scalar(modc[:, DC:], ps[:, 0, 160 + DC:160 + 2 * DC], 1.0, None, ALU.add).then_inc(s_modc, 1)
            dve.wait_ge(s_modc, 2)

            def hin_low(k):
                dve.wait_ge(s_hinh, k + 1)
                dve.tensor_tensor(hin[:, 1, k, :], hraw[:, k % 4, :], hin[:, 0, k, :].bitcast(F32), ALU.subtract).then_inc(s_hinv, 1)

            for k in range(DC):
                dve.wait_ge(s_xtp, k + 1)
                if k >= 4:
                    (dve.wait_ge(s_hinv, k // 2 - 1) if k % 2 else dve.wait_ge(s_hinl, k // 2 - 1))
                dve.tensor_scalar(hraw[:, k % 4, :], bank(1 + k % 7), modc[:, DC + k:DC + k + 1], modc[:, k:k + 1],
                                  ALU.mult, ALU.add).then_inc(s_hraw, 1)
                if k >= 2 and k % 2 == 0:
                    hin_low(k - 1)
            hin_low(DC - 1)
            def xbc_taps(g):
                dve.tensor_copy(gtaps[:, :, 0:1], taps[:, :, ds(g + 16, 1)]).then_inc(s_gtap, 1)
                dve.tensor_copy(gtaps[:, :, 1:2], taps[:, :, ds(g + 20, 1)]).then_inc(s_gtap, 1)
                dve.tensor_copy(gtaps[:, :, 2:NT], taps[:, :, ds(4 * g, 4)]).then_inc(s_gtap, 1)
                dve.wait_ge(s_gtap, 3 * g + 3)

            def xbc_tile(g, i):
                dve.wait_ge(s_cv0, NT * g + i + 1)
                for n, k in enumerate((2, 1, 0)):
                    s = NTAP - 1 - k
                    if n:
                        dve.wait_ge(s_tap, 2 * (NT * g + i) + n)
                    op = dve.scalar_tensor_tensor(conv[:, i % 2, s:], ps[:, i % 2, 0:T - s], gtaps[:, k, i:i + 1],
                                                  conv[:, i % 2, s:], ALU.mult, ALU.add)
                    op.then_inc(s_cv if n == 2 else s_tap, 1)

            def seg_head(g, h):
                dve.wait_ge(s_abc, HG * g + h + 1)
                if h >= 2:
                    dve.wait_ge(s_m, HG * g + h - 1)
                for k in range(TT):
                    a = gtok[:, k, 0, h:h + 1]
                    op = dve.tensor_scalar(seg[:, h % 2, k, :], ps[:, 2 + h % 2, k * P:(k + 1) * P], a, a, ALU.min, ALU.subtract)
                op.then_inc(s_seg, 1)

            def mix_head(g, h):
                dve.wait_ge(s_dec, HG * g + h + 1)
                if h == 0:
                    dve.wait_ge(s_cbm, g + 1)
                if h >= 4:
                    dve.wait_ge(s_y, 4 * g + (h - 4) // 2 + 1)
                dve.tensor_tensor(mh[:, h % 4], seg[:, h % 2], cbm, ALU.mult).then_inc(s_m, 1)

            def ada_piece(g, k):
                dve.wait_ge(ld_ada[k % 2], 16 * (4 * g + k // 2 + 1))
                if k == 0:
                    dve.wait_ge(ld_bg, 16 * (g + 1))
                else:
                    dve.wait_ge(s_adau, DC * g + k + 1)
                dve.scalar_tensor_tensor(acc, ada[:, k % 2, :], cact[:, k:k + 1], acc, ALU.mult, ALU.add).then_inc(s_adau, 1)

            def state_step(g, k):
                dve.wait_ge(s_st, 3 * g + k + 1)
                if k == 0:
                    dve.tensor_copy(state[:, 0, :], bank(5)).then_inc(s_stu, 1)
                else:
                    dve.wait_ge(s_stu, 3 * g + k + 1)
                    el = gel[:, :, k].unsqueeze(2).broadcast_to([P, HG, HD])
                    dve.tensor_tensor(stmp.rearrange("p (h n) -> p h n", h=HG), state[:, k - 1, :].rearrange("p (h n) -> p h n", h=HG), el, ALU.mult).then_inc(s_stm, 1)
                    dve.wait_ge(s_stm, 2 * g + k)
                    dve.tensor_tensor(state[:, k, :], stmp, bank(5), ALU.add).then_inc(s_stu, 1)

            steps = [0]

            def link(op):
                steps[0] += 1
                op.then_inc(s_n, 1)
                dve.wait_ge(s_n, steps[0])

            def residual(q):
                if q == 0:
                    dve.wait_ge(ld_x2, 16 * TT)
                dve.wait_ge(s_oacc, 8 * (G - 1) + 2 * q + 3)
                cols = slice(q * 256, (q + 1) * 256)
                link(dve.tensor_tensor(oacc[:, :, cols], oacc[:, :, cols], modr[:, 0, cols].unsqueeze(1).broadcast_to([P, TT, 256]), ALU.mult))
                link(dve.scalar_tensor_tensor(xt[:, :, cols], xt[:, :, cols], ALPHA, oacc[:, :, cols], ALU.mult, ALU.add))
                if q % 2:
                    for t in range(TT):
                        op = dve.bn_stats(st6[:, t, q // 2, :], xt[:, t, q // 2 * 512:(q // 2 + 1) * 512])
                    link(op)

            def gate(g, q):
                dve.wait_ge(s_y, 4 * g + q + 1)
                if q >= 2:
                    dve.wait_ge(s_yz, 4 * g + q - 1)
                yt = seg[:, q % 2].rearrange("p c t -> p (c t)")
                dve.scalar_tensor_tensor(yt, xT[:, q, :], gnd[:, 1, q:q + 1], bank(6 + q % 2), ALU.mult, ALU.add).then_inc(s_y1, 1)
                dve.wait_ge(s_y1, 4 * g + q + 1)
                dve.tensor_tensor(yT[:, q, :], yt, yT[:, q, :], ALU.mult).then_inc(s_yz, 1)

            def turn(g, last):
                dve.tensor_copy(gtok, tok[:, :, :, ds(HG * g, HG)]).then_inc(s_gc, 1)
                dve.tensor_copy(gel, elast[:, :, ds(TT * g, TT)]).then_inc(s_gc, 1)
                dve.tensor_copy(gnd[:, 0, :], normg[:, ds(4 * g, 4)]).then_inc(s_gc, 1)
                dve.tensor_copy(gnd[:, 1, :], dskip[:, ds(4 * g, 4)]).then_inc(s_gc, 1)
                dve.wait_ge(s_gc, 4 * g + 4)
                dve.wait_ge(s_cb, g + 1)
                dve.tensor_tensor(cbm, bank4(4), causal.unsqueeze(1).broadcast_to([P, TT, P]), ALU.mult).then_inc(s_cbm, 1)
                for k in range(TT):
                    dve.wait_ge(s_xtr, TT * g + k + 1)
                    src = bank((2, 3, 0, 1)[k]).rearrange("p (h n) -> p h n", h=HG)
                    col = lambda n: gtok[:, k, n, :].unsqueeze(2).broadcast_to([P, HG, HD])
                    dve.tensor_tensor(xdt[:, k, :].rearrange("p (h n) -> p h n", h=HG), src, col(1), ALU.mult).then_inc(s_xdt, 1)
                    if k < 3:
                        dve.tensor_tensor(xw[:, k, :].rearrange("p (h n) -> p h n", h=HG), src, col(2), ALU.mult).then_inc(s_xw, 1)
                for h in range(HG):
                    seg_head(g, h)
                    ada_piece(g, h)
                    if h < 3:
                        state_step(g, h)
                    if h:
                        mix_head(g, h - 1)
                if not last:
                    xbc_taps(g + 1)
                mix_head(g, HG - 1)
                dve.wait_ge(s_m, HG * g + HG)
                dve.wait_ge(s_zs, g + 1)
                gate(g, 0)
                gate(g, 1)
                if not last:
                    xbc_tile(g + 1, 0)
                for n in range(2):
                    dve.wait_ge(s_bc, 2 * g + n + 1)
                    dve.tensor_scalar(modr[:, ds(g, 1), n * 512:(n + 1) * 512].rearrange("p a n -> p (a n)"), bank(2 + n),
                                      onep[:, ds(g, 1)], None, ALU.add).then_inc(s_bcu, 1)
                if not last:
                    dve.memset(acc, 0.0).then_inc(s_accz, 1)
                    xbc_tile(g + 1, 1)
                gate(g, 2)
                gate(g, 3)
                for q in range(4):
                    dve.wait_ge(s_yh, 4 * g + q + 1)
                    dve.scalar_tensor_tensor(ysplit[:, 1, q, :], yT[:, q, :], gnd[:, 0, q:q + 1], ysplit[:, 0, q, :].bitcast(F32), ALU.mult, ALU.subtract).then_inc(s_yl, 1)
                if not last:
                    xbc_tile(g + 1, 2)
                dve.wait_ge(s_oacc, 8 * g + 1)
                dve.wait_ge(s_ms, g + 1)
                dve.tensor_scalar(rstd4, ps[:, 4, 0:TT], 1.0 / GW, EPS, ALU.mult, ALU.add).then_inc(s_var, 1)
                if not last:
                    xbc_tile(g + 1, 3)
                dve.wait_ge(s_sqrt, g + 1)
                dve.reciprocal(rstd4, rstd4).then_inc(s_rs, 1)
                if not last:
                    xbc_tile(g + 1, 4)
                    xbc_tile(g + 1, 5)
                dve.wait_ge(s_rs, g + 1)
                for q in range(OU):
                    for j in range(2):
                        if j:
                            dve.wait_ge(s_unit, unit_o(g, q, last) + 1)
                        else:
                            dve.wait_ge(s_out, OU * g + q + 1)
                        for t in (2 * j, 2 * j + 1):
                            o = oacc[:, t, q * 256:(q + 1) * 256]
                            op = dve.scalar_tensor_tensor(o, ps[:, 6 + j, (t % 2) * 256:(t % 2 + 1) * 256], rstd4[:, t:t + 1], o, ALU.mult, ALU.add)
                        op.then_inc(s_oacc, 1)
                    if last:
                        residual(q)

            dve.wait_ge(s_rowc, 2)
            xbc_taps(0)

            dve.wait_ge(s_const, CONSTS)
            dve.wait_ge(s_prea, 2)
            dve.tensor_scalar(aneg[0:32, :], aneg[0:32, :], -1.0, None, ALU.mult).then_inc(s_dtv, 1)
            v, ev, uv, cv, lv = (a[0:32] for a in dtv)
            pre = [0]

            def step(op):
                pre[0] += 1
                op.then_inc(s_pre, 1)
                dve.wait_ge(s_pre, pre[0])

            step(dve.scalar_tensor_tensor(ev, v, -1.0, v, ALU.mult, ALU.max))
            dve.wait_ge(s_prea, 3)
            step(dve.tensor_scalar(uv, ev, 1.0, None, ALU.add))
            step(dve.tensor_scalar(cv, uv, -1.0, None, ALU.add))
            step(dve.tensor_tensor(cv, ev, cv, ALU.subtract))
            dve.wait_ge(s_prea, 4)
            step(dve.reciprocal(uv, uv))
            step(dve.tensor_tensor(cv, cv, uv, ALU.mult))
            step(dve.tensor_tensor(cv, cv, lv, ALU.add))
            step(dve.scalar_tensor_tensor(v, v, 0.0, cv, ALU.max, ALU.add))
            xbc_tile(0, 0)
            dve.wait_ge(s_dtv, 1)
            dve.tensor_scalar(cv, v, aneg[0:32, :], None, ALU.mult).then_inc(s_dtv, 1)
            dve.wait_ge(s_dtv, 2)
            dve.tensor_copy(stk[32:64], v)
            for k in range(TT):
                op = dve.tensor_tensor_scan(stk[0:32, k * P:(k + 1) * P], ones[0:32, :],
                                            cv[:, k * P:(k + 1) * P], 0.0, ALU.mult, ALU.add)
            step(op)
            acum3 = stk[0:32].rearrange("p (c t) -> p c t", t=P)
            step(dve.tensor_tensor(ev.rearrange("p (c t) -> p c t", t=P), acum3[:, :, P - 1:P].broadcast_to([32, TT, P]), acum3, ALU.subtract))
            xbc_tile(0, 1)
            for g in range(G):
                dve.tensor_scalar(acg[0:32, g, :], stk[0:32], gmask[0:32, g:g + 1], None, ALU.mult).then_inc(s_dtv, 1)
            dve.wait_ge(s_dtv, 2 + G)
            for g in range(G):
                dve.scalar_tensor_tensor(acg[32:64, g, :], stk[0:32], gmask[0:32, g:g + 1], acg[0:32, g, :].bitcast(F32), ALU.mult, ALU.subtract).then_inc(s_dtv, 1)
            dve.tensor_reduce(every8, ident.rearrange("p (a j) -> p j a", j=HG), AX.X, ALU.add).then_inc(s_dtv, 1)
            dve.wait_ge(s_dtv, 3 + 2 * G)
            dve.tensor_copy(every8r, every8).then_inc(s_dtv, 1)
            dve.wait_ge(s_prea, 5)
            step(dve.tensor_tensor(stk[64:96], ev, v, ALU.mult))
            xbc_tile(0, 2)
            xbc_tile(0, 3)
            dve.wait_ge(s_tokp, 1)
            dve.tensor_copy(tok, ps[:, 5, 0:TT * 96].rearrange("p (c s h) -> p c s h", c=TT, s=3)).then_inc(s_tok, 1)
            xbc_tile(0, 4)
            xbc_tile(0, 5)
            dve.wait_ge(s_tok, 1)
            dve.wait_ge(s_el, 1)
            groups(dve, lambda g: turn(g, False), lambda g: turn(g, True))

            for t in range(TT):
                op = dve.bn_aggr(mv[:, t, :], st6[:, t].rearrange("p s n -> p (s n)"))
            op.then_inc(s_var1, 1)
            dve.wait_ge(s_var1, 1)
            dve.wait_ge(s_sd1, 1)
            link(dve.reciprocal(rstd, rstd))
            dve.scalar_tensor_tensor(shift, mv[:, :, 0], -1.0, rstd, ALU.mult, ALU.mult).then_inc(s_shift, 1)
            dve.wait_ge(s_fold, 3)
            for t in range(TT):
                if t == 1:
                    dve.wait_ge(s_h2m, 1)
                else:
                    dve.wait_ge(s_nrm, t + 1)
                    if t == 3:
                        dve.wait_ge(s_h2l, 1)
                        dve.wait_ge(s_h2t, 2)
                    link(dve.tensor_tensor(h2f[t], xt[:, t, :], modr[:, 2, :], ALU.mult))
                dve.tensor_tensor(h2f[t], h2f[t], modr[:, 1, :], ALU.add).then_inc(s_h2f, 1)
            for t in range(2):
                dve.tensor_tensor(xt[:, t, :], xt[:, t, :], lnr[:, 0, :], ALU.mult).then_inc(s_x1v, 1)
                dve.wait_ge(s_x1v, 2 * t + 1)
                dve.tensor_tensor(xt[:, t, :], xt[:, t, :], lnr[:, 1, :], ALU.add).then_inc(s_x1v, 1)

            dve.wait_ge(s_lg, TT)
            dve.wait_ge(ld_r, 32)
            dve.wait_ge(s_h2l, 3)
            b3 = lambda a, n=E: a.unsqueeze(2).broadcast_to([P, TT, n])
            link(dve.tensor_copy(prob, ps[:, 6, 0:TT * E].rearrange("p (t e) -> p t e", e=E)))
            link(dve.tensor_reduce(red, prob, AX.X, ALU.max))
            dve.tensor_tensor(prob, prob, b3(red), ALU.subtract).then_inc(s_mx, 1)
            dve.wait_ge(s_ex, 1)
            link(dve.tensor_reduce(red, prob, AX.X, ALU.add))
            link(dve.reciprocal(red2, red))
            link(dve.tensor_tensor(prob, prob, b3(red2), ALU.mult))
            link(dve.tensor_tensor(selp, prob, rb.unsqueeze(1).broadcast_to([P, TT, E]), ALU.add))

            def ranks(val, rk, tmp, n):
                link(dve.memset(rk, 0.0))
                for j in range(n):
                    other = val[:, :, j].unsqueeze(2)
                    k = n - 1 - j
                    if j:
                        dve.tensor_tensor(tmp[:, :, 0:j], other.broadcast_to([P, val.shape[1], j]), val[:, :, 0:j], ALU.is_gt)
                    link(dve.memset(tmp[:, :, j], 0.0))
                    if k:
                        link(dve.tensor_tensor(tmp[:, :, j + 1:], other.broadcast_to([P, val.shape[1], k]), val[:, :, j + 1:], ALU.is_ge))
                    link(dve.tensor_tensor(rk, rk, tmp, ALU.add))

            quad = lambda a: a.rearrange("p t (g e) -> p (t g) e", e=E // EG)
            ranks(quad(selp), quad(rank), quad(tie), E // EG)
            link(dve.tensor_scalar(rank, rank, 2.0, None, ALU.is_lt))
            link(dve.tensor_tensor(tie, selp, rank, ALU.mult))
            link(dve.tensor_reduce(gsum.rearrange("p t g -> p (t g)"), quad(tie), AX.X, ALU.add))
            ranks(gsum, grank, gtie, EG)
            link(dve.tensor_scalar(grank, grank, 1.0, None, ALU.is_lt))
            link(dve.tensor_tensor(quad(mask), quad(rank), grank.rearrange("p t g -> p (t g)").unsqueeze(2).broadcast_to([P, TT * EG, E // EG]), ALU.mult))
            dve.memset(cum[:, 0, :], 0.0)
            link(dve.tensor_copy(cum[:, 1, :], mask[:, 0, :]))
            for t in range(1, TT):
                op = dve.tensor_tensor(cum[:, t + 1, :], cum[:, t, :], mask[:, t, :], ALU.add)
                if t < TT - 1:
                    link(op)
            op.then_inc(s_mask, 1)
            link(dve.tensor_tensor(wts, prob, mask, ALU.mult))
            link(dve.tensor_reduce(red, wts, AX.X, ALU.add))
            link(dve.reciprocal(red2, red))
            link(dve.tensor_tensor(wts, wts, b3(red2), ALU.mult))
            dve.wait_ge(s_pos, 1)
            link(dve.scalar_tensor_tensor(pm, ps[:, 7, 0:TT * E].rearrange("p (t e) -> p t e", e=E), 1.0, mask, ALU.add, ALU.mult))
            link(dve.tensor_scalar(pmx[:, :, 0, :], pm, -1.0, None, ALU.add))
            pmb = pmx.rearrange("p t r e -> p t (r e)")

            def select(b):
                for t in range(TT):
                    op = dve.tensor_scalar(sel[:, t, :], iota, pmb[:, t, ds(b, 1)], None, ALU.is_equal)
                op.then_inc(s_sel, 1)

            select(0)
            link(dve.tensor_reduce(nbf[:, 0:1], ps[:, 7, TT * E:TT * E + E], AX.X, ALU.max))
            link(dve.tensor_scalar(cnt[:, 0:1], nbf[:, 0:1], float(P), float(E), ALU.is_gt, ALU.mult))
            link(dve.tensor_scalar(cnt[:, 1:2], nbf[:, 0:1], float(2 * P), float(E), ALU.is_gt, ALU.mult))
            link(dve.tensor_scalar(cnt[:, 2:3], nbf[:, 0:1], float(3 * P), float(E), ALU.is_gt, ALU.mult))
            link(dve.tensor_reduce(nbf[:, 1:2], cnt[:, 0:3], AX.X, ALU.add))
            dve.tensor_scalar(nblk_i[0:1, 0:1], nbf[0:1, 1:2], float(E), None, ALU.add)
            dve.tensor_scalar(nblk_i[0:1, 1:2], nbf[0:1, 1:2], float(E - 1), None, ALU.add).then_inc(s_nblk, 1)
            for r in range(1, ROUNDS):
                dve.tensor_scalar(pmx[:, :, r, :], pm, float(-1 - P * r), None, ALU.add)
            for r in range(ROUNDS):
                dve.tensor_copy(wtb[:, :, 1 + r * E:1 + (r + 1) * E], wts)
            link(dve.memset(wtb[:, :, 0:1], 0.0))
            dve.wait_ge(s_nblk, 1)
            final = dve.value_load(nblk_i[0:1, 1:2], min_val=E - 1, max_val=E * ROUNDS - 1)

            def low(b, i):
                dve.wait_ge(s_wh, MU * b + (i + 1))
                part = slice(0, 2 * D - POOL_PART)
                dve.tensor_tensor(wr[:, i % SPLIT, 1, part], ring[:, i % RING, part], wr[:, i % SPLIT, 0, part].bitcast(F32), ALU.subtract).then_inc(s_wlv, 1)

            def add(b, js):
                for j in js:
                    dve.wait_ge(s_sc, 8 * b + j + 1)
                    t = j // 2
                    o = oacc[:, t, (j % 2) * 512:(j % 2 + 1) * 512]
                    dve.scalar_tensor_tensor(o, bank(4 + j % 2), wtb[:, t, ds(b, 1)], o, ALU.mult, ALU.add).then_inc(s_acc, 1)

            def rows_low(b, j):
                dve.wait_ge(s_xeh, 2 * b + j + 1)
                h = slice(4 * j, 4 * j + 4)
                dve.tensor_tensor(xe[:, 1, h, :], bank4(4 + j), xe[:, 0, h, :].bitcast(F32), ALU.subtract).then_inc(s_xel, 1)

            def moe(b, last):
                dve.wait_ge(s_acc, 8 * b + 1)
                for i in range(3, 7):
                    add(b, (2 * i - 6, 2 * i - 5))
                    low(b, i)
                low(b, 7)
                if not last:
                    dve.wait_ge(s_selp, b + 1)
                    select(b + 1)
                low(b, DC)
                low(b, DC + 1)
                dve.wait_ge(s_gate, b + 1)
                dve.tensor_tensor(hid.rearrange("p (n f) -> p n f", n=2), sgate.rearrange("p (n f) -> p n f", n=2), ps[:, 2:4, :], ALU.mult).then_inc(s_hid, 1)
                for j in range(2):
                    dve.wait_ge(s_hTh, 2 * b + j + 1)
                    h = slice(4 * j, 4 * j + 4)
                    dve.tensor_tensor(hT[:, 1, h, :], bank4(7 - j), hT[:, 0, h, :].bitcast(F32), ALU.subtract).then_inc(s_hTl, 1)
                if not last:
                    rows_low(b + 1, 0)
                low(b, DC + 2)
                low(b, DC + 3)
                if not last:
                    rows_low(b + 1, 1)
                    low(b + 1, 0)
                    low(b + 1, 1)
                dve.wait_ge(s_ydh, b + 1)
                two = lambda a: a.rearrange("p (n f) -> p n f", n=2)
                dve.tensor_tensor(two(yd[:, 1, :]), ps[:, 6:8, :], two(yd[:, 0, :].bitcast(F32)), ALU.subtract).then_inc(s_ydl, 1)
                if not last:
                    low(b + 1, 2)

            rows_low(0, 0)
            rows_low(0, 1)
            dve.wait_ge(s_zero, 2)
            with dve.Fori(0, final) as b:
                moe(b, False)
            moe(final, True)

            def sums(t):
                if t % 2:
                    dve.wait_ge(s_om, t // 2 + 1)
                else:
                    link(dve.tensor_tensor(oacc[:, t, :], oacc[:, t, :], modr[:, 3, :], ALU.mult))
                link(dve.scalar_tensor_tensor(xt[:, t, :], xt[:, t, :], ALPHA, oacc[:, t, :], ALU.mult, ALU.add))
                dve.bn_stats(st6[:, t, 0, :], xt[:, t, 0:512])
                link(dve.bn_stats(st6[:, t, 1, :], xt[:, t, 512:]))
                dve.bn_aggr(mv[:, t, :], st6[:, t].rearrange("p s n -> p (s n)")).then_inc(s_var1, 1)

            def scale(t):
                dve.wait_ge(s_var1, t + 2)
                dve.wait_ge(s_sd1, t + 2)
                link(dve.reciprocal(rstd[:, t:t + 1], rstd[:, t:t + 1]))
                dve.scalar_tensor_tensor(shift[:, t:t + 1], mv[:, t, 0:1], -1.0, rstd[:, t:t + 1], ALU.mult, ALU.mult).then_inc(s_shift, 1)

            def finish(t):
                if t < 3:
                    dve.wait_ge(s_gain, t + 1)
                else:
                    dve.wait_ge(s_nrm, TT + t + 1)
                    link(dve.tensor_tensor(xt[:, t, :], xt[:, t, :], lnr2[:, 0, :], ALU.mult))
                dve.tensor_tensor(xt[:, t, :], xt[:, t, :], lnr2[:, 1, :], ALU.add).then_inc(s_done, 1)

            add(final + 1, range(8))
            dve.wait_ge(s_acc, 8 * final + 17)
            dve.wait_ge(s_x1p, 4)
            dve.wait_ge(ld_ln, 16 * 4)
            sums(0)
            sums(1)
            scale(0)
            sums(2)
            scale(1)
            sums(3)
            scale(2)
            finish(0)
            scale(3)
            finish(1)
            finish(2)
            finish(3)

        @block.tensor
        def _(pe):
            mm = nc.tensor.matmul
            pe.wait_ge(s_const, CONSTS)
            pe.wait_ge(ld_x, 16 * TT)

            def x_chunk(k):
                for t in range(TT):
                    op = nc.tensor.transpose(ps[:, 1 + k % 7, t * P:(t + 1) * P], oacc[:, t, k * P:(k + 1) * P], ident)
                op.then_inc(s_xtp, 1)

            for k in range(7):
                x_chunk(k)
            pe.wait_ge(ld_small, 16 * 7)
            nc.tensor.transpose(ps[:, 0, 0:120], rows[0:120, 0, :], ident[0:120, 0:120]).then_inc(s_rowp, 1)
            nc.tensor.transpose(ps[:, 0, 128:144], rows[0:16, 1, :], ident[0:16, 0:16]).then_inc(s_rowp, 1)
            pe.wait_ge(s_rowc, 2)
            pe.wait_ge(s_adaA, DC)
            for j in range(16):
                op = mm(ps[:, 0, 160 + j:161 + j], accA[:, j * P:(j + 1) * P], ones[:, 0:1], start=True, stop=True)
            op.then_inc(s_modp, 1)
            pe.wait_ge(s_hraw, 1)
            x_chunk(7)

            def parts(u, slot, k, n):
                return wsplit[:, slot, 0, :].rearrange("p (k n) -> p k n", k=k), wsplit[:, slot, 1, :].rearrange("p (k n) -> p k n", k=k)

            def tile(u, slot, to):
                pe.wait_ge(s_ul, u + 1)
                wh, wl = parts(u, slot, DC, P)
                for k in range(DC):
                    mm(to, wh[:, k, :], hin[:, 0, k, :], start=(k == 0), stop=False)
                    mm(to, wh[:, k, :], hin[:, 1, k, :], start=False, stop=False)
                    op = mm(to, wl[:, k, :], hin[:, 0, k, :], start=False, stop=(k == DC - 1))
                op.then_inc(s_unit, 1)

            def xbc_tile(g, i):
                if i >= 2:
                    pe.wait_ge(s_cv, NT * g + i - 1)
                elif not isinstance(g, int):
                    pe.wait_ge(s_zc, ZT * (g - 1) + i + 3)
                tile(unit_x(g, i), i % 2, bank(i % 2))

            def z_tile(g, i):
                if i >= 2:
                    pe.wait_ge(s_zc, ZT * g + i - 1)
                elif i == 0:
                    pe.wait_ge(s_xw, 3 * g + 3)
                else:
                    pe.wait_ge(s_xdt, TT * g + 4)
                tile(unit_z(g, i), i % 2, bank(i % 2))

            pe.wait_ge(s_dtl, 1)
            pe.wait_ge(s_hraw, 3)
            for k in range(DC):
                (pe.wait_ge(s_hinv, k // 2 + 1) if k % 2 else pe.wait_ge(s_hinl, k // 2 + 1))
                mm(ps[0:32, 3, :], dtsplit[0][:, k, :], hin[:, 0, k, :], start=(k == 0), stop=False)
                mm(ps[0:32, 3, :], dtsplit[0][:, k, :], hin[:, 1, k, :], start=False, stop=False)
                op = mm(ps[0:32, 3, :], dtsplit[1][:, k, :], hin[:, 0, k, :], start=False, stop=(k == DC - 1))
            op.then_inc(s_dtp, 1)
            for i in range(4):
                xbc_tile(0, i)
            pe.wait_ge(s_dtv, 4 + 2 * G)
            acl = acg.rearrange("p g (c t) -> p (g c) t", t=P)
            for j in range(HG):
                op = mm(ps[:, 4, j * 16:(j + 1) * 16], every8r[:, j:j + 1].broadcast_to([P, P]), acl[:, :, P - 1], start=True, stop=True)
            op.then_inc(s_elp, 1)
            pe.wait_ge(s_pre, 11)
            for k in range(TT):
                op = nc.tensor.transpose(ps[:, 5, k * 96:(k + 1) * 96], stk[0:96, k * P:(k + 1) * P], ident[0:96, 0:96])
            op.then_inc(s_tokp, 1)
            xbc_tile(0, 4)
            xbc_tile(0, 5)

            def acum_rows(g, h):
                if h < 2:
                    pe.wait_ge(s_xw, 3 * g + h + 1)
                else:
                    pe.wait_ge(s_e, HG * g + h - 1 + 1)
                mm(bank(2 + h % 2), every8r[:, h:h + 1].broadcast_to([P, P]),
                   acg[:, ds(g, 1), :].rearrange("p a t -> p (a t)"), start=True, stop=True).then_inc(s_abc, 1)

            def state_sum(g, k):
                pe.wait_ge(s_xw, 3 * g + k + 1)
                if k == 0:
                    pe.wait_ge(s_btok, g + 1)
                else:
                    pe.wait_ge(s_stu, 3 * g + k + 1)
                mm(bank(5), btok[:, k, :], xw[:, k, :], start=True, stop=True).then_inc(s_st, 1)

            def y_pair(g, q):
                pe.wait_ge(s_m, HG * g + 2 * q + 2)
                pe.wait_ge(s_ch, HG * g + 2 * q + 2)
                if q == 0:
                    pe.wait_ge(s_stu, 3 * g + 4)
                    pe.wait_ge(s_oacc, 8 * g + 1)
                if q >= 2:
                    pe.wait_ge(s_y1, 4 * g + q - 1)
                for k in range(TT):
                    for hh in range(2):
                        h = 2 * q + hh
                        o = ps[hh * HD:(hh + 1) * HD, 6 + q % 2, k * P:(k + 1) * P]
                        op = mm(o, xdt[:, k, h * HD:(h + 1) * HD], mh[:, h % 4, k, :], start=True, stop=(k == 0))
                        if k:
                            op = mm(o, state[:, k - 1, h * HD:(h + 1) * HD], ch[:, h % 4, (k - 1) * P:k * P], start=False, stop=True)
                op.then_inc(s_y, 1)

            def turn(g, last):
                pe.wait_ge(s_silu, NT * (g + 1))
                pe.wait_ge(s_var, g + 1)
                for k in range(TT):
                    t = slice(k * P, (k + 1) * P)
                    op = mm(ps[:, 4, t], bT[:, t], cT[:, t], start=True, stop=True)
                op.then_inc(s_cb, 1)
                pe.wait_ge(s_stu, 3 * g + 1)
                for k in range(TT):
                    t = slice(k * P, (k + 1) * P)
                    op = nc.tensor.transpose(ps[:, 5, t], bT[:, t], ident)
                op.then_inc(s_btr, 1)
                for k in range(TT):
                    if k == 0:
                        pe.wait_ge(s_bcu, 2 * g + 1)
                    if k == 2:
                        pe.wait_ge(s_cv, NT * g + NT)
                    for j in range(4):
                        op = nc.tensor.transpose(ps[:, (2, 3, 0, 1)[k], j * P:(j + 1) * P], xT[:, j, k * P:(k + 1) * P], ident)
                    op.then_inc(s_xtr, 1)
                acum_rows(g, 0)
                acum_rows(g, 1)
                state_sum(g, 0)
                z_tile(g, 0)
                state_sum(g, 1)
                acum_rows(g, 2)
                z_tile(g, 1)
                state_sum(g, 2)
                acum_rows(g, 3)
                acum_rows(g, 4)
                z_tile(g, 2)
                acum_rows(g, 5)
                y_pair(g, 0)
                acum_rows(g, 6)
                z_tile(g, 3)
                acum_rows(g, 7)
                y_pair(g, 1)
                if not last:
                    xbc_tile(g + 1, 0)
                pe.wait_ge(s_adau, DC * g + DC + 1)
                pe.wait_ge(s_e, HG * g + HG + 1)
                for n in range(2):
                    mm(bank(2 + n), ones, acc[:, n * 512:(n + 1) * 512], start=True, stop=True).then_inc(s_bc, 1)
                if not last:
                    xbc_tile(g + 1, 1)
                y_pair(g, 2)
                y_pair(g, 3)
                if not last:
                    xbc_tile(g + 1, 2)
                pe.wait_ge(s_cbm, g + 1)
                pe.wait_ge(s_sq, 4 * g + 4)
                for t in range(TT):
                    for q in range(4):
                        op = mm(ps[:, 4, t:t + 1], squares[q][:, t * P:(t + 1) * P], ones[:, 0:1], start=(q == 0), stop=(q == 3))
                op.then_inc(s_ms, 1)
                if not last:
                    for i in range(3, NT):
                        xbc_tile(g + 1, i)
                pe.wait_ge(s_yl, 4 * g + 5)
                for q in range(OU):
                    pe.wait_ge(s_ul, unit_o(g, q, last) + 1)
                    wh, wl = parts(None, q % 2, 4, 256)
                    for j in range(2):
                        if q:
                            pe.wait_ge(s_oacc, 8 * g + 2 * q + j)
                        for t in (2 * j, 2 * j + 1):
                            to, tt = ps[:, 6 + j, (t % 2) * 256:(t % 2 + 1) * 256], slice(t * P, (t + 1) * P)
                            for k in range(4):
                                mm(to, ysplit[:, 0, k, tt], wh[:, k, :], start=(k == 0), stop=False)
                                mm(to, ysplit[:, 0, k, tt], wl[:, k, :], start=False, stop=False)
                                op = mm(to, ysplit[:, 1, k, tt], wh[:, k, :], start=False, stop=(k == 3))
                        op.then_inc(s_unit if j else s_out, 1)

            pe.wait_ge(s_tok, 1)
            pe.wait_ge(s_el, 1)
            groups(pe, lambda g: turn(g, False), lambda g: turn(g, True))

            for t in range(TT):
                pe.wait_ge(s_h2f, t + 1)
                for j in range(2):
                    if t:
                        pe.wait_ge(s_h2tc, 2 * t - 1 + j)
                    for k in range(4):
                        op = nc.tensor.transpose(ps[:, 4 + j, k * P:(k + 1) * P], h2f[t][:, (4 * j + k) * P:(4 * j + k + 1) * P], ident)
                    op.then_inc(s_h2t, 1)
                if t == 0:
                    pe.wait_ge(ld_r, 32)
                pe.wait_ge(s_h2tc, 2 * t + 2)
                for k in range(DC):
                    op = mm(ps[:, 6, t * E:(t + 1) * E], h2T[t % 2][:, k, :], rw[:, k, :], start=(k == 0), stop=(k == DC - 1))
                op.then_inc(s_lg, 1)
            pe.wait_ge(s_mask, 1)
            mm(ps[:, 7, 0:(TT + 1) * E], ones, cum.rearrange("p t e -> p (t e)"), start=True, stop=False)
            mm(ps[:, 7, 0:TT * E], before, mask.rearrange("p t e -> p (t e)"), start=False, stop=True).then_inc(s_pos, 1)

            pe.sem_inc(s_xt, 1)

            def gather(b, j):
                if j == 0:
                    pe.wait_ge(s_sel, b + 1)
                for t in range(TT):
                    for part in range(2):
                        op = mm(bank(4 + j), sel[:, t, :], h2[:, part, t, j * 512:(j + 1) * 512], start=(t + part == 0), stop=(t == TT - 1 and part == 1))
                op.then_inc(s_ga, 1)

            def turn_rows(b, j):
                pe.wait_ge(s_xg, 2 * b + 2)
                for k in range(4):
                    d = 4 * j + k
                    op = nc.tensor.transpose(ps[:, 4 + j, k * P:(k + 1) * P], xg[:, d * P:(d + 1) * P], ident)
                op.then_inc(s_xt, 1)

            def scatter(b, j):
                if j == 0:
                    pe.wait_ge(s_ydl, b + 1)
                if j >= 2:
                    pe.wait_ge(s_acc, 8 * b + j - 1 + 1)
                t, n = j // 2, slice((j % 2) * 512, (j % 2 + 1) * 512)
                mm(bank(4 + j % 2), selT[:, t, :], yd[:, 0, n], start=True, stop=False)
                mm(bank(4 + j % 2), selT[:, t, :], yd[:, 1, n], start=False, stop=True).then_inc(s_sc, 1)

            def products(to, xh, xl, wh, wl, start, stop):
                n = range(len(to))
                for i in n:
                    mm(to[i], xh, wh[i], start=start, stop=False)
                for i in n:
                    mm(to[i], xh, wl[i], start=False, stop=False)
                for i in n:
                    op = mm(to[i], xl, wh[i], start=False, stop=stop)
                return op

            def moe(b, last):
                for i in range(DC):
                    if i % 4 == 0:
                        pe.wait_ge(s_xel, 2 * b + i // 4 + 1)
                    pe.wait_ge(s_wlv, MU * b + (i + 1))
                    pe.wait_ge(s_wlp, MU * b + (i + 1))
                    cols = [[wr[:, i % SPLIT, s, n * 512:(n + 1) * 512] for n in range(4)] for s in range(2)]
                    products([bank(n) for n in range(4)], xe[:, 0, i, :], xe[:, 1, i, :], cols[0], cols[1], i == 0, i == DC - 1).then_inc(s_wu, 1)
                    if i < 4:
                        if i == 0:
                            pe.wait_ge(s_xel, 2 * b + 2)
                        scatter(b, 2 * i)
                        scatter(b, 2 * i + 1)
                    if i == 4:
                        pe.wait_ge(s_acc, 8 * b + 7 + 1)
                        for t in range(TT):
                            op = nc.tensor.transpose(ps[:, 4, t * P:(t + 1) * P], sel[:, t, :].bitcast(F32), ident)
                        op.then_inc(s_selp, 1)
                pe.wait_ge(s_selT, b + 1)
                pe.wait_ge(s_acc, 8 * b + 8 + 1)
                if not last:
                    gather(b + 1, 0)
                    gather(b + 1, 1)
                pe.wait_ge(s_hid, b + 1)
                for j in range(2):
                    for k in range(4):
                        d = 4 * j + k
                        op = nc.tensor.transpose(ps[:, 7 - j, k * P:(k + 1) * P], hid[:, d * P:(d + 1) * P], ident)
                    op.then_inc(s_hp, 1)
                if not last:
                    turn_rows(b + 1, 0)
                pe.wait_ge(s_hTl, 2 * b + 2)
                for i in range(DC, MU):
                    pe.wait_ge(s_wlv, MU * b + (i + 1))
                    pe.wait_ge(s_wlp, MU * b + (i + 1))
                    for kk in range(2):
                        k = 2 * (i - DC) + kk
                        cols = [[wr[:, i % SPLIT, s, kk * D + n * 512:kk * D + (n + 1) * 512] for n in range(2)] for s in range(2)]
                        op = products([bank(6), bank(7)], hT[:, 0, k, :], hT[:, 1, k, :], cols[0], cols[1], k == 0, k == DC - 1)
                    op.then_inc(s_wu, 1)
                    if i == DC and not last:
                        turn_rows(b + 1, 1)

            pe.wait_ge(s_h2tc, 2 * TT)
            pe.wait_ge(s_h2l, TT)
            gather(0, 0)
            gather(0, 1)
            turn_rows(0, 0)
            turn_rows(0, 1)
            pe.wait_ge(s_zero, 1)
            pe.wait_ge(s_nblk, 1)
            final = pe.value_load(nblk_i[0:1, 1:2], min_val=E - 1, max_val=E * ROUNDS - 1)
            with pe.Fori(0, final) as b:
                moe(b, False)
            moe(final, True)
            for j in range(8):
                scatter(final + 1, j)


NAMES = ["x", "c", "ada_w", "ada_b", "ln1_g", "ln1_b", "ln2_g", "ln2_b", "ssd_w_in", "ssd_conv_w", "ssd_conv_b",
         "ssd_dt_bias", "ssd_a_log", "ssd_d", "ssd_norm_g", "ssd_w_out", "moe_w_up", "moe_w_down", "router_w", "router_b"]


def kernel(**inputs):
    import concourse.bacc as bacc
    from concourse.bass_utils import run_bass_kernel_spmd

    nc = bacc.Bacc("TRN2", target_bir_lowering=False, num_devices=1)
    arrays, args = {}, []
    for name in NAMES:
        a = np.ascontiguousarray(inputs[name])
        arrays[f"in_{name}"] = a
        args.append(nc.dram_tensor(f"in_{name}", a.shape, mybir.dt.from_np(a.dtype), kind="ExternalInput").ap())
    args.append(nc.dram_tensor("out_y", (1, T, D), F32, kind="ExternalOutput").ap())
    build(nc, *args)
    r = run_bass_kernel_spmd(nc, [arrays], core_ids=[0])
    return r.results[0]["out_y"]
```

```python
from contextlib import ExitStack

import numpy as np

import concourse.bass as bass
from concourse import mybir

F32 = mybir.dt.float32
F32R = mybir.dt.float32r
I32 = mybir.dt.int32
ALU = mybir.AluOpType
ACT = mybir.ActivationFunctionType
AX = mybir.AxisListType
ds = bass.ds

P = 128
D = 1024
T = 512
DC = D // P
TT = T // P
G = 4
HG = 8
HD = 64
NS = 128
DI = 2048
GW = DI // G
NTAP = 4
XBC = 2
NT = XBC + GW // P
ZT = GW // P
COL_X, COL_B, COL_C, COL_DT = DI, 2 * DI, 2 * DI + G * NS, 2 * DI + 2 * G * NS
E = 16
EG = 4
ROUNDS = T // P
ALPHA = 2.0 ** 0.25
EPS = 1e-5
MU = DC + DC // 2
CONSTS = 12
RING = SPLIT = 3
POOL_PART = 768


def build(nc, x, c, ada_w, ada_b, ln1_g, ln1_b, ln2_g, ln2_b, w_in, conv_w, conv_b, dt_bias, a_log,
          d_skip, norm_g, w_out, w_up, w_down, router_w, router_b, out):
    ctx = ExitStack()
    with ctx:
        def space(stack, name, words, dtype):
            whole = stack.enter_context(nc.sbuf_tensor(name, [P, words], dtype))
            top = [0]

            def place(n, at=None):
                if at is None:
                    at = top[0]
                    top[0] += n
                assert at + n <= words, (name, at + n)
                return whole[:, at:at + n]

            place.top = top
            return place

        def sem(name):
            return ctx.enter_context(nc.semaphore(name))

        place = space(ctx, "both", 10126, F32)
        ident = place(P)
        ones = place(P)
        causal = place(P)
        before = place(P)
        iota = place(P)
        taps = place(120).rearrange("p (k j) -> p k j", k=5)
        normg = place(16)
        dskip = place(16)
        ccol = place(DC)
        cact = place(DC)
        modc = place(16)
        onep = place(4)
        gmask = place(4)
        every8 = place(HG)
        earlier, later = (place(16).rearrange("p (e j) -> p e j", e=4) for _ in range(2))
        epsc = place(1)
        dtb = place(1)
        aneg = place(1)
        tok = place(TT * 96).rearrange("p (c s h) -> p c s h", c=TT, s=3)
        elast = place(HG * G * TT).rearrange("p (j n) -> p j n", j=HG)
        oacc = place(TT * D).rearrange("p (t n) -> p t n", t=TT)
        st6 = place(12 * TT).rearrange("p (t s n) -> p t s n", t=TT, s=2)
        mv = place(2 * TT).rearrange("p (t n) -> p t n", t=TT)
        rstd = place(TT)
        shift = place(TT)
        mod_at = place.top[0]
        modr = place(4 * D).rearrange("p (g n) -> p g n", g=4)
        both = place

        nblk_i = ctx.enter_context(nc.sbuf_tensor("nblk_i", [1, 2], I32))

        half = ExitStack()
        place = space(half, "ssd_r", 2 * DC * T + 4 * D + 2 * 4 * T + G * T + HG, F32R)
        hin = place(2 * DC * T).rearrange("p (s k t) -> p s k t", s=2, k=DC)
        wsplit = place(4 * D).rearrange("p (u s n) -> p u s n", u=2, s=2)
        ysplit = place(2 * 4 * T).rearrange("p (s k t) -> p s k t", s=2, k=4)
        acg = place(G * T).rearrange("p (g t) -> p g t", g=G)
        every8r = place(HG)
        place = space(half, "ssd", 23724, F32)
        stage = place(2 * D).rearrange("p (u n) -> p u n", u=2)
        adaA_at = place.top[0]
        xT = place(4 * T).rearrange("p (k t) -> p k t", k=4)
        bT = place(T)
        cT = place(T)
        conv = place(2 * T).rearrange("p (s t) -> p s t", s=2)
        yT = place(4 * T).rearrange("p (k t) -> p k t", k=4)
        btok = place(TT * NS).rearrange("p (c n) -> p c n", c=TT)
        xdt = place(TT * GW).rearrange("p (c n) -> p c n", c=TT)
        xw = place(3 * GW).rearrange("p (c n) -> p c n", c=3)
        adaA = place(4 * 2 * D, adaA_at).rearrange("p (s n) -> p s n", s=4)
        cbm = place(TT * P).rearrange("p (c t) -> p c t", c=TT)
        seg = place(2 * T).rearrange("p (s c t) -> p s c t", s=2, c=TT)
        ebc = place(2 * T).rearrange("p (s t) -> p s t", s=2)
        m_at = place.top[0]
        mh = place(4 * T).rearrange("p (h c t) -> p h c t", h=4, c=TT)
        ch = place(4 * 3 * P).rearrange("p (h t) -> p h t", h=4)
        state_at = place.top[0]
        state = place(3 * GW).rearrange("p (c n) -> p c n", c=3)
        stmp = place(GW)
        rstd4 = place(TT)
        gtok = place(TT * 24).rearrange("p (c s j) -> p c s j", c=TT, s=3)
        gel = place(HG * TT).rearrange("p (j n) -> p j n", j=HG)
        gtaps = place(5 * NT).rearrange("p (k j) -> p k j", k=5)
        gnd = place(8).rearrange("p (s j) -> p s j", s=2)
        acc = place(D)
        ada = place(2 * D).rearrange("p (s n) -> p s n", s=2)
        hraw = ada.rearrange("p s (h t) -> p (s h) t", h=2)
        squares = [ebc[:, 0, :], ebc[:, 1, :]] + [mh[:, i].rearrange("p c t -> p (c t)") for i in range(2)]
        accA = place(2 * D, state_at)
        wdt = place(DC * 32, m_at).rearrange("p (k n) -> p k n", k=DC)
        dtsplit = [ysplit[:, part, 0, 0:DC * 32].rearrange("p (k n) -> p k n", k=DC) for part in range(2)]
        rows = place(2 * P, m_at + 256).rearrange("p (s n) -> p s n", s=2)
        dtv = [place(T, m_at + 512 * (i + 1)) for i in range(5)]
        stk = place(T, m_at + 512 * 6)
        half.close()

        half = ExitStack()
        place = space(half, "moe", 19488 - 4096, F32)
        xt = place(TT * D).rearrange("p (t n) -> p t n", t=TT)
        lnr = place(2 * D).rearrange("p (a n) -> p a n", a=2)
        hid = lnr[:, 0, :]
        sgate = lnr[:, 1, :]
        ring = place(RING * 2 * D).rearrange("p (u n) -> p u n", u=RING)
        h2T = [ring[:, RING - 1, s * D:(s + 1) * D].rearrange("p (k s) -> p k s", k=DC) for s in range(2)]
        lnr2 = ring[:, 0, :].rearrange("p (a n) -> p a n", a=2)
        rowtmp = ring[:, 0, 0:D]
        h2f = [place(D), place(D), modr[:, 0, :]]
        h2f.append(h2f[0])
        xg = h2f[0]
        rw = place(DC * E).rearrange("p (k e) -> p k e", k=DC)
        rb = place(E)
        nbf = place(2)
        r3 = lambda w, n=E: place(w * n).rearrange("p (t e) -> p t e", e=n)
        prob, mask, wts, pm = r3(TT), r3(TT), r3(TT), r3(TT)
        pmx = place(TT * ROUNDS * E).rearrange("p (t r e) -> p t r e", t=TT, r=ROUNDS)
        wtb = place(TT * (1 + ROUNDS * E)).rearrange("p (t b) -> p t b", t=TT)
        m0 = [mod_at]

        def r4(w, n=E):
            m0[0] += w * n
            return both(w * n, m0[0] - w * n)

        selp, rank, tie = (r4(TT).rearrange("p (t e) -> p t e", e=E) for _ in range(3))
        gsum, grank = (r4(TT, EG).rearrange("p (t e) -> p t e", e=EG) for _ in range(2))
        pairs = [r4(TT * EG).rearrange("p (n e j) -> p n e j", e=4, j=4) for _ in range(2)]
        red, red2, cnt = r4(TT, 1), r4(TT, 1), r4(1)
        cum = r4(TT + 1).rearrange("p (t e) -> p t e", e=E)
        place = space(half, "moe_r", 23552 + 4096, F32R)
        wr = place(SPLIT * 4 * D).rearrange("p (u s n) -> p u s n", u=SPLIT, s=2)
        h2 = place(2 * TT * D).rearrange("p (s t n) -> p s t n", s=2, t=TT)
        xe = place(2 * DC * P).rearrange("p (s k t) -> p s k t", s=2, k=DC)
        hT = place(2 * DC * P).rearrange("p (s k t) -> p s k t", s=2, k=DC)
        yd = place(2 * D).rearrange("p (s n) -> p s n", s=2)
        sel = place(TT * P).rearrange("p (t s) -> p t s", t=TT)
        selT = place(TT * P).rearrange("p (t s) -> p t s", t=TT)
        half.close()

        ps = ctx.enter_context(nc.psum_tensor("ps", [P, 8, 512], F32))
        bank = lambda i: ps[:, i, :]
        bank4 = lambda i: ps[:, i, :].rearrange("p (c t) -> p c t", c=4)

        def sems(names):
            return [sem(n) for n in names.split()]

        ld_c, ld_small, ld_x, ld_wdt, ld_b0, ld_bg, ld_x2, ld_ln, ld_r, ld_out = sems("ld_c ld_small ld_x ld_wdt ld_b0 ld_bg ld_x2 ld_ln ld_r ld_out")
        s_const, s_cact, s_acc0, s_adaA, s_modp, s_modc, s_rowp, s_rowc = sems("s_const s_cact s_acc0 s_adaA s_modp s_modc s_rowp s_rowc")
        s_xtp, s_hraw, s_hinh, s_hinl, s_hinv = sems("s_xtp s_hraw s_hinh s_hinl s_hinv")
        s_dth, s_dtl, s_dtp, s_dtv, s_pre, s_prea = sems("s_dth s_dtl s_dtp s_dtv s_pre s_prea")
        s_tokp, s_tok, s_elp, s_el = sems("s_tokp s_tok s_elp s_el")
        s_uh, s_ul, s_unit = sems("s_uh s_ul s_unit")
        s_cv0, s_tap, s_cv, s_silu, s_gtap, s_zc, s_zs = sems("s_cv0 s_tap s_cv s_silu s_gtap s_zc s_zs")
        s_cb, s_cbm, s_btr, s_btok, s_xtr, s_xdt, s_xw, s_gc = sems("s_cb s_cbm s_btr s_btok s_xtr s_xdt s_xw s_gc")
        s_st, s_stu, s_stm = sems("s_st s_stu s_stm")
        s_abc, s_seg, s_dec, s_e, s_m, s_ch = sems("s_abc s_seg s_dec s_e s_m s_ch")
        s_y, s_y1, s_yz, s_sq, s_sqs, s_ms = sems("s_y s_y1 s_yz s_sq s_sqs s_ms")
        s_var, s_sqrt, s_rs, s_yh, s_yl = sems("s_var s_sqrt s_rs s_yh s_yl")
        s_out, s_oacc, s_adau, s_bc, s_bcu, s_accz = sems("s_out s_oacc s_adau s_bc s_bcu s_accz")
        s_n, s_fold, s_var1, s_sd1, s_shift, s_nrm, s_om, s_gain, s_done = sems("s_n s_fold s_var1 s_sd1 s_shift s_nrm s_om s_gain s_done")
        s_h2m, s_h2f, s_h2h, s_h2l, s_x1v, s_x1p, s_zero = sems("s_h2m s_h2f s_h2h s_h2l s_x1v s_x1p s_zero")
        s_h2t, s_h2tc, s_lg, s_mx, s_ex, s_mask, s_pos, s_nblk = sems("s_h2t s_h2tc s_lg s_mx s_ex s_mask s_pos s_nblk")
        s_wh, s_wlv, s_wlp, s_wu = sems("s_wh s_wlv s_wlp s_wu")
        s_sel, s_ga, s_xg, s_xt, s_xeh, s_xel, s_selp, s_selT = sems("s_sel s_ga s_xg s_xt s_xeh s_xel s_selp s_selT")
        s_gate, s_hid, s_hp, s_hTh, s_hTl, s_ydh, s_ydl, s_sc, s_acc = sems("s_gate s_hid s_hp s_hTh s_hTl s_ydh s_ydl s_sc s_acc")
        ld_adaA = [sem(f"ld_adaA{i}") for i in range(4)]
        ld_ada = [sem(f"ld_ada{i}") for i in range(2)]
        ld_u = [sem(f"ld_u{i}") for i in range(2)]
        ld_w = [sem(f"ld_w{i}") for i in range(RING)]

        rows_bank = lambda t: 4 - 2 * (t % 2)
        x_banks = (0, 6, 7, 1)
        ctx.enter_context(nc.allow_non_contiguous_dma("columns of a few constants"))
        block = ctx.enter_context(nc.Block())

        def groups(run, body, last):
            with run.Fori(0, G - 1) as g:
                body(g)
            last(G - 1)

        ZU, XU, OU = ZT, NT, 4
        TU = ZU + XU + OU
        assert XU % 2 == 0 and TU % 2 == 0 and ZU % 2 == 0

        def unit_z(g, i):
            return TU * g + (XU + i)

        def unit_x(g, i):
            return i if isinstance(g, int) and g == 0 else TU * g + (i - TU + XU + ZU)

        def unit_o(g, q, last):
            return TU * g + (XU + ZU + (0 if last else XU) + q)

        @block.sync
        def _(sp):
            sp.dma_start(ccol, c.rearrange("a (p k) -> p (a k)", k=DC)).then_inc(ld_c, 16)
            adaA_v = ada_w.rearrange("l (p k) n -> p (l k) n", k=DC)
            for k in range(4):
                if k == 2:
                    sp.wait_ge(s_acc0, 1)
                    sp.dma_start(accA[0:1, :], ada_b[0:1, 0:2 * D]).then_inc(ld_b0, 16)
                sp.dma_start(adaA[:, k, :], adaA_v[:, k, 0:2 * D]).then_inc(ld_adaA[k], 16)
            sp.dma_start(rows[0:96, 0, :], conv_w.rearrange("a k (j p) -> (a k j) p", p=P)).then_inc(ld_small, 16)
            sp.dma_start(rows[96:120, 0, :], conv_b.rearrange("a (j p) -> (a j) p", p=P)).then_inc(ld_small, 16)
            sp.dma_start(rows[0:16, 1, :], norm_g.rearrange("a (j p) -> (a j) p", p=P)).then_inc(ld_small, 16)
            for half in range(2):
                sp.dma_start(dskip[half * HD:(half + 1) * HD, :],
                             d_skip.rearrange("a (j two) -> two (a j)", two=2)[half:half + 1, :].broadcast_to([HD, 16])).then_inc(ld_small, 16)
            sp.dma_start(dtb[0:32, :], dt_bias.rearrange("a h -> h a")).then_inc(ld_small, 16)
            sp.dma_start(aneg[0:32, :], a_log.rearrange("a h -> h a")).then_inc(ld_small, 16)
            w_v = w_in.rearrange("l (k p) n -> p (l k) n", p=P)

            def load_tile(u, slot, col):
                if not (isinstance(u, int) and u < 2):
                    sp.wait_ge(s_ul, u - 1)
                sp.dma_start(stage[:, slot, :].rearrange("p (k n) -> p k n", k=DC), w_v[:, :, ds(col, P)]).then_inc(ld_u[slot], 16)

            def load_x(g, i):
                load_tile(unit_x(g, i), i % 2, g * NS + (COL_B, COL_C)[i] if i < XBC else g * GW + (COL_X + (i - XBC) * P))

            sp.dma_start(wdt, w_v[:, :, COL_DT:COL_DT + 32]).then_inc(ld_wdt, 16)
            for k in range(4, 8):
                sp.wait_ge(s_adaA, k - 3)
                sp.dma_start(adaA[:, k % 4, :], adaA_v[:, k, 0:2 * D]).then_inc(ld_adaA[k % 4], 16)
            for t in range(TT):
                sp.dma_start(oacc[:, t, :], x[0, t * P:(t + 1) * P, :]).then_inc(ld_x, 16)
            for i in range(NT):
                load_x(0, i)
            wo_v = w_out.rearrange("l (g k p) n -> p (l g) k n", p=P, k=4)

            def ada_piece(g, k):
                sp.wait_ge(s_adau, DC * g + max(k, 1))
                sp.dma_start(ada[:, k % 2, :], adaA_v[:, k, ds(g * D + 2 * D, D)]).then_inc(ld_ada[k % 2], 16)

            def turn(g, last):
                load_z = lambda i: load_tile(unit_z(g, i), i % 2, g * GW + i * P)
                load_z(0)
                load_z(1)
                sp.wait_ge(s_accz, g + 1)
                sp.dma_start(acc[0:1, :], ada_b[0:1, ds(g * D + 2 * D, D)]).then_inc(ld_bg, 16)
                ada_piece(g, 0)
                ada_piece(g, 1)
                load_z(2)
                ada_piece(g, 2)
                load_z(3)
                ada_piece(g, 3)
                def load_o(q):
                    sp.wait_ge(s_ul, unit_o(g, q, last) - 1)
                    sp.dma_start(stage[:, q % 2, :].rearrange("p (k n) -> p k n", k=4),
                                 wo_v[:, ds(g, 1), :, q * 256:(q + 1) * 256].rearrange("p a k n -> p (a k) n")).then_inc(ld_u[q % 2], 16)

                for i in range(2):
                    if last:
                        load_o(i)
                    else:
                        load_x(g + 1, i)
                    ada_piece(g, 2 * i + 4)
                    ada_piece(g, 2 * i + 5)
                if not last:
                    for i in range(2, NT):
                        load_x(g + 1, i)
                if last:
                    sp.wait_ge(s_unit, unit_z(G - 1, ZU))
                    for t in range(TT):
                        sp.dma_start(xt[:, t, :], x[0, t * P:(t + 1) * P, :]).then_inc(ld_x2, 16)
                for q in range(2 if last else 0, OU):
                    load_o(q)
                if last:
                    for i, row in enumerate((ln1_g, ln1_b)):
                        sp.dma_start(lnr[:, i, :], row[0:1, :].broadcast_to([P, D])).then_inc(ld_ln, 16)

            groups(sp, lambda g: turn(g, False), lambda g: turn(g, True))

            sp.wait_ge(s_oacc, 32 + 1)
            sp.wait_ge(s_fold, 3)
            sp.dma_start(rw, router_w.rearrange("(k p) e -> p k e", p=P)).then_inc(ld_r, 16)
            sp.dma_start(rb, router_b.rearrange("(a e) -> a e", a=1).broadcast_to([P, E])).then_inc(ld_r, 16)
            up_v = w_up.rearrange("l e (k p) n -> (l e) p k n", p=P)
            dn_v = w_down.rearrange("l e (k p) n -> (l e) p k n", p=P)

            def load_unit(e, i):
                if i < DC:
                    sp.dma_start(ring[:, i % RING, :], up_v[ds(e, 1), :, i, :].rearrange("a p n -> p (a n)")).then_inc(ld_w[i % RING], 16)
                else:
                    j = 2 * (i - DC)
                    sp.dma_start(ring[:, i % RING, :].rearrange("p (k n) -> p k n", k=2),
                                 dn_v[ds(e, 1), :, j:j + 2, :].rearrange("a p k n -> p (a k) n")).then_inc(ld_w[i % RING], 16)

            for i in range(RING - 1):
                load_unit(0, i)
            sp.wait_ge(s_lg, TT)
            load_unit(0, RING - 1)
            for i in range(RING, MU):
                sp.wait_ge(s_wlv, i - RING + 1)
                sp.wait_ge(s_wlp, i - RING + 1)
                load_unit(0, i)
            sp.wait_ge(s_nblk, 1)
            nblk = sp.value_load(nblk_i[0:1, 0:1], min_val=E, max_val=E * ROUNDS)
            with sp.Fori(1, nblk) as b:
                e = sp.snap(b % E)
                for i in range(MU):
                    sp.wait_ge(s_wlv, MU * b + (i - RING + 1))
                    sp.wait_ge(s_wlp, MU * b + (i - RING + 1))
                    load_unit(e, i)
            sp.wait_ge(s_wlv, MU * nblk)
            sp.wait_ge(s_wlp, MU * nblk)
            for i, row in enumerate((ln2_g, ln2_b)):
                sp.dma_start(lnr2[:, i, :], row[0:1, :].broadcast_to([P, D])).then_inc(ld_ln, 16)
            for n, t in enumerate((0, 1, 3, 2)):
                if t == 0:
                    sp.wait_ge(s_gain, 2)
                else:
                    sp.wait_ge(s_done, n)
                sp.dma_start(out[0, t * P:(t + 1) * P, :], xt[:, t, :]).then_inc(ld_out, 16)
            sp.wait_ge(ld_out, 16 * TT)

        @block.gpsimd
        def _(pool):
            pool.memset(ones, 1.0).then_inc(s_const, 1)
            pool.memset(epsc, EPS).then_inc(s_const, 1)
            pool.memset(onep, 1.0).then_inc(s_const, 1)
            pool.iota(iota, pattern=[[1, P]], base=0, channel_multiplier=0, allow_small_or_imprecise_dtypes=True).then_inc(s_const, 1)
            pool.wait_ge(s_const, 4)
            pool.memset(onep[:, 1:2], 0.0).then_inc(s_const, 1)
            sel_of = lambda out, op, base, pattern, cm: pool.affine_select(out=out, in_=ones[:, 0:out.free_size()], compare_op=op, fill=0.0, base=base, pattern=pattern, channel_multiplier=cm)
            sel_of(causal, ALU.is_ge, 0, [[1, P]], -1).then_inc(s_const, 1)
            sel_of(before, ALU.is_ge, -1, [[1, P]], -1).then_inc(s_const, 1)
            sel_of(ident, ALU.is_equal, 0, [[1, P]], -1).then_inc(s_const, 1)
            sel_of(gmask, ALU.is_ge, 0, [[-HG, G]], 1).then_inc(s_const, 1)
            sel_of(earlier, ALU.is_ge, -1, [[1, 4], [-1, 4]], 0).then_inc(s_const, 1)
            sel_of(later, ALU.is_ge, -1, [[-1, 4], [1, 4]], 0).then_inc(s_const, 1)
            pool.wait_ge(s_const, 9)
            pool.affine_select(out=gmask, in_=gmask, compare_op=ALU.is_ge, fill=0.0, base=HG - 1,
                               pattern=[[HG, G]], channel_multiplier=-1).then_inc(s_const, 1)

            def unit_low(u, slot):
                pool.wait_ge(s_uh, u + 1)
                pool.tensor_tensor(wsplit[:, slot, 1, :], stage[:, slot, :], wsplit[:, slot, 0, :].bitcast(F32), ALU.subtract).then_inc(s_ul, 1)

            pool.wait_ge(s_dth, 1)
            pool.tensor_tensor(dtsplit[1], wdt, dtsplit[0].bitcast(F32), ALU.subtract).then_inc(s_dtl, 1)
            for k in range(0, DC, 2):
                pool.wait_ge(s_hinh, k + 1)
                pool.tensor_tensor(hin[:, 1, k, :], hraw[:, k % 4, :], hin[:, 0, k, :].bitcast(F32), ALU.subtract).then_inc(s_hinl, 1)
            unit_low(0, 0)
            unit_low(1, 1)
            pool.wait_ge(s_xtp, DC)
            pool.memset(oacc, 0.0)
            pool.memset(acc, 0.0).then_inc(s_accz, 1)
            for i in range(2, XU):
                unit_low(i, i % 2)

            def decayed_c(g, h):
                pool.wait_ge(s_e, HG * g + h + 2)
                if h >= 4:
                    pool.wait_ge(s_y, 4 * g + (h - 4) // 2 + 1)
                pool.tensor_tensor(ch[:, h % 4, :], cT[:, P:], ebc[:, h % 2, P:], ALU.mult).then_inc(s_ch, 1)

            def turn(g, last):
                heads_after = {1: (0, 1), 2: (2,), 3: (3,), 4: (4, 5), 5: (6, 7)}
                for i in range(TU - (XU if last else 0)):
                    unit_low(TU * g + (XU + i), i % 2)
                    for h in heads_after.get(i, ()):
                        decayed_c(g, h)
                    if i == (5 if last else 7):
                        for q in (1, 2, 3):
                            pool.wait_ge(s_sq, 4 * g + q + 1)
                            if q > 1:
                                pool.wait_ge(s_sqs, 3 * g + q - 1)
                            pool.tensor_tensor(squares[0], squares[0], squares[q], ALU.add).then_inc(s_sqs, 1)
                    if last and i == TU - XU - 1:
                        fold_rows()

            def fold_rows():
                pool.wait_ge(ld_ln, 16 * 2)
                pool.wait_ge(s_bcu, 2 * 3 + 1)
                pool.tensor_tensor(rowtmp, lnr[:, 1, :], modr[:, 2, :], ALU.mult).then_inc(s_fold, 1)
                pool.wait_ge(s_fold, 1)
                pool.tensor_tensor(modr[:, 1, :], rowtmp, modr[:, 1, :], ALU.add).then_inc(s_fold, 1)
                pool.tensor_tensor(modr[:, 2, :], lnr[:, 0, :], modr[:, 2, :], ALU.mult).then_inc(s_fold, 1)

            groups(pool, lambda g: turn(g, False), lambda g: turn(g, True))

            pool.wait_ge(s_oacc, 32 + 1)
            pool.memset(yd.bitcast(F32), 0.0)
            pool.memset(selT.bitcast(F32), 0.0).then_inc(s_zero, 1)

            pool.wait_ge(s_fold, 3)
            pool.wait_ge(s_nrm, 2)
            pool.tensor_tensor(h2f[1], xt[:, 1, :], modr[:, 2, :], ALU.mult).then_inc(s_h2m, 1)
            for t in range(TT):
                pool.wait_ge(s_h2h, t + 1)
                pool.tensor_tensor(h2[:, 1, t, :], h2f[t], h2[:, 0, t, :].bitcast(F32), ALU.subtract).then_inc(s_h2l, 1)

            for i in range(3):
                pool.wait_ge(s_wh, i + 1)
                for part, done in ((slice(0, 2 * D - POOL_PART), s_wlv), (slice(2 * D - POOL_PART, 2 * D), s_wlp)):
                    pool.tensor_tensor(wr[:, i % SPLIT, 1, part], ring[:, i % RING, part], wr[:, i % SPLIT, 0, part].bitcast(F32), ALU.subtract).then_inc(done, 1)
            pool.memset(oacc, 0.0).then_inc(s_zero, 1)
            pool.wait_ge(s_h2f, TT)
            for n, t in enumerate((2, 3)):
                pool.tensor_tensor(xt[:, t, :], xt[:, t, :], lnr[:, 0, :], ALU.mult).then_inc(s_x1p, 1)
                pool.wait_ge(s_x1p, 2 * n + 1)
                pool.tensor_tensor(xt[:, t, :], xt[:, t, :], lnr[:, 1, :], ALU.add).then_inc(s_x1p, 1)

            def low(b, i):
                pool.wait_ge(s_wh, MU * b + (i + 1))
                part = slice(2 * D - POOL_PART, 2 * D)
                pool.tensor_tensor(wr[:, i % SPLIT, 1, part], ring[:, i % RING, part], wr[:, i % SPLIT, 0, part].bitcast(F32), ALU.subtract).then_inc(s_wlp, 1)

            for i in range(3, MU):
                low(0, i)
            pool.wait_ge(s_nblk, 1)
            nblk = pool.value_load(nblk_i[0:1, 0:1], min_val=E, max_val=E * ROUNDS)
            with pool.Fori(1, nblk) as b:
                for i in range(MU):
                    low(b, i)

            def gated(t):
                pool.wait_ge(s_acc, 8 * nblk + (2 * t + 3))
                pool.tensor_tensor(oacc[:, t, :], oacc[:, t, :], modr[:, 3, :], ALU.mult).then_inc(s_om, 1)

            def gain(t):
                pool.wait_ge(s_nrm, TT + t + 1)
                pool.tensor_tensor(xt[:, t, :], xt[:, t, :], lnr2[:, 0, :], ALU.mult).then_inc(s_gain, 1)

            gated(1)
            gated(3)
            pool.wait_ge(ld_ln, 16 * 4)
            gain(0)
            pool.wait_ge(s_gain, 1)
            pool.tensor_tensor(xt[:, 0, :], xt[:, 0, :], lnr2[:, 1, :], ALU.add).then_inc(s_gain, 1)
            gain(1)
            gain(2)

        @block.scalar
        def _(act):
            act.sem_inc(s_e, 1)
            act.wait_ge(ld_c, 16)
            act.activation(cact, ccol, ACT.Silu).then_inc(s_cact, 1)
            def unit_high(u, slot, nth):
                act.wait_ge(ld_u[slot], 16 * nth)
                if not (isinstance(u, int) and u < 2):
                    act.wait_ge(s_unit, u - 1)
                act.activation(wsplit[:, slot, 0, :], stage[:, slot, :], ACT.Identity).then_inc(s_uh, 1)
            act.wait_ge(ld_wdt, 16)
            act.activation(dtsplit[0], wdt, ACT.Identity).then_inc(s_dth, 1)
            act.wait_ge(ld_small, 16 * 7)
            act.activation(aneg[0:32, :], aneg[0:32, :], ACT.Exp).then_inc(s_prea, 1)
            for k in range(DC):
                act.wait_ge(s_hraw, k + 1)
                act.activation(hin[:, 0, k, :], hraw[:, k % 4, :], ACT.Identity).then_inc(s_hinh, 1)
            unit_high(0, 0, 1)
            unit_high(1, 1, 1)
            act.wait_ge(s_dtp, 1)
            act.activation(dtv[0][0:32], ps[0:32, 3, :], ACT.Identity, bias=dtb[0:32]).then_inc(s_prea, 1)
            act.wait_ge(s_pre, 1)
            act.activation(dtv[1][0:32], dtv[1][0:32], ACT.Exp, scale=-1.0).then_inc(s_prea, 1)
            act.wait_ge(s_pre, 2)
            act.activation(dtv[4][0:32], dtv[2][0:32], ACT.Ln).then_inc(s_prea, 1)

            def turn_unit(g, i):
                unit_high(TU * g + (XU + i), i % 2, TU // 2 * g + (XU // 2 + i // 2 + 1))

            def conv0(g, i):
                act.wait_ge(s_unit, unit_x(g, i) + 1)
                if i == 0:
                    act.wait_ge(s_gtap, 3 * g + 3)
                if i >= 2 or not (isinstance(g, int) and g == 0):
                    act.wait_ge(s_silu, NT * g + i - 1)
                act.activation(conv[:, i % 2, :], bank(i % 2), ACT.Identity, bias=gtaps[:, 4, i:i + 1],
                               scale=gtaps[:, 3, i:i + 1]).then_inc(s_cv0, 1)

            def silu(g, i):
                act.wait_ge(s_cv, NT * g + i + 1)
                to = bT if i == 0 else cT if i == 1 else xT[:, i - XBC, :]
                act.activation(to, conv[:, i % 2, :], ACT.Silu).then_inc(s_silu, 1)

            def zcopy(g, i):
                act.wait_ge(s_unit, unit_z(g, i) + 1)
                act.activation(yT[:, i, :], bank(i % 2), ACT.Identity).then_inc(s_zc, 1)

            def exps(g, h):
                act.wait_ge(s_seg, HG * g + h + 1)
                act.activation(seg[:, h % 2], seg[:, h % 2], ACT.Exp).then_inc(s_dec, 1)
                if h >= 2:
                    act.wait_ge(s_ch, HG * g + h - 1)
                act.activation(ebc[:, h % 2, :], bank(2 + h % 2), ACT.Exp).then_inc(s_e, 1)

            def square(g, q):
                act.wait_ge(s_yz, 4 * g + q + 1)
                if q == 0:
                    act.wait_ge(s_ch, HG * g + HG)
                act.activation(squares[q], yT[:, q, :], ACT.Square).then_inc(s_sq, 1)

            def turn(g, last):
                turn_unit(g, 1)
                act.wait_ge(s_btr, g + 1)
                act.activation(btok, bank4(5), ACT.Identity).then_inc(s_btok, 1)
                act.wait_ge(s_yl, 4 * g + 1)
                exps(g, 0)
                exps(g, 1)
                zcopy(g, 0)
                turn_unit(g, 2)
                exps(g, 2)
                zcopy(g, 1)
                turn_unit(g, 3)
                exps(g, 3)
                zcopy(g, 2)
                turn_unit(g, 4)
                exps(g, 4)
                exps(g, 5)
                zcopy(g, 3)
                turn_unit(g, 5)
                exps(g, 6)
                exps(g, 7)
                act.wait_ge(s_zc, ZT * (g + 1))
                act.activation(yT, yT, ACT.Silu).then_inc(s_zs, 1)
                if not last:
                    conv0(g + 1, 0)
                    turn_unit(g, 6)
                square(g, 0)
                square(g, 1)
                if not last:
                    silu(g + 1, 0)
                    conv0(g + 1, 1)
                    turn_unit(g, 7)
                    silu(g + 1, 1)
                square(g, 2)
                square(g, 3)
                for q in range(4):
                    act.activation(ysplit[:, 0, q, :], yT[:, q, :], ACT.Identity, scale=gnd[:, 0, q:q + 1]).then_inc(s_yh, 1)
                if not last:
                    conv0(g + 1, 2)
                    turn_unit(g, 8)
                act.wait_ge(s_var, g + 2)
                act.activation(rstd4, rstd4, ACT.Sqrt).then_inc(s_sqrt, 1)
                if not last:
                    conv0(g + 1, 3)
                    turn_unit(g, 9)
                if last:
                    turn_unit(g, 6)
                    turn_unit(g, 7)
                else:
                    for i in (4, 5):
                        silu(g + 1, i - 2)
                        conv0(g + 1, i)
                        turn_unit(g, i + 6)
                    silu(g + 1, 4)
                    silu(g + 1, 5)
                    turn_unit(g, 12)
                    turn_unit(g, 13)
                    turn_unit(g + 1, 0)

            for i in range(2):
                conv0(0, i)
                unit_high(i + 2, i % 2, 2)
            act.wait_ge(s_pre, 10)
            act.activation(dtv[1][0:32], dtv[1][0:32], ACT.Exp).then_inc(s_prea, 1)
            silu(0, 0)
            silu(0, 1)
            for i in range(2, 4):
                conv0(0, i)
                unit_high(i + 2, i % 2, 3)
            silu(0, 2)
            act.wait_ge(s_elp, 1)
            act.activation(elast, ps[:, 4, 0:P].rearrange("p (j n) -> p j n", j=HG), ACT.Exp).then_inc(s_el, 1)
            silu(0, 3)
            conv0(0, 4)
            turn_unit(0, 0)
            conv0(0, 5)
            silu(0, 4)
            silu(0, 5)
            groups(act, lambda g: turn(g, False), lambda g: turn(g, True))

            def router_rows(t):
                for j in range(2):
                    act.wait_ge(s_h2t, 2 * t + j + 1)
                    if t >= 2:
                        act.wait_ge(s_lg, t - 1)
                    act.activation(h2T[t % 2][:, 4 * j:4 * j + 4, :], bank4(rows_bank(t) + j), ACT.Identity).then_inc(s_h2tc, 1)

            def normalise(t, n):
                act.wait_ge(s_var1, n + 1)
                act.activation(rstd[:, t:t + 1], mv[:, t, 1:2], ACT.Sqrt, bias=epsc).then_inc(s_sd1, 1)
                act.wait_ge(s_shift, n + 1)
                act.activation(xt[:, t, :], xt[:, t, :], ACT.Identity, bias=shift[:, t:t + 1], scale=rstd[:, t:t + 1]).then_inc(s_nrm, 1)

            def h2_high(t):
                act.wait_ge(s_h2f, t + 1)
                act.activation(h2[:, 0, t, :], h2f[t], ACT.Identity).then_inc(s_h2h, 1)

            for t in range(3):
                normalise(t, t)
            h2_high(0)
            router_rows(0)
            normalise(3, 3)
            for t in range(1, TT):
                h2_high(t)
                router_rows(t)

            def high(b, i):
                act.wait_ge(ld_w[i % RING], 16 * (MU // RING) * b + 16 * (i // RING + 1))
                if not (isinstance(b, int) and i < SPLIT):
                    act.wait_ge(s_wu, MU * b + (i - SPLIT + 1))
                act.activation(wr[:, i % SPLIT, 0, :], ring[:, i % RING, :], ACT.Identity).then_inc(s_wh, 1)

            def gathered(b, j):
                act.wait_ge(s_ga, 2 * b + j + 1)
                if j == 0:
                    act.wait_ge(s_xt, 2 * b + 1)
                act.activation(xg[:, j * 512:(j + 1) * 512], bank(4 + j), ACT.Identity).then_inc(s_xg, 1)

            def rows_high(b, j):
                act.wait_ge(s_xt, 2 * b + j + 2)
                act.activation(xe[:, 0, 4 * j:4 * j + 4, :], bank4(4 + j), ACT.Identity).then_inc(s_xeh, 1)

            def moe(b, last):
                for i in range(3, DC):
                    high(b, i)
                act.wait_ge(s_selp, b + 1)
                act.activation(selT, bank4(4), ACT.Identity).then_inc(s_selT, 1)
                high(b, DC)
                high(b, DC + 1)
                act.wait_ge(s_wu, MU * b + DC)
                act.wait_ge(s_x1v, 4)
                act.wait_ge(s_x1p, 4)
                for j in range(2):
                    act.activation(sgate[:, j * 512:(j + 1) * 512], bank(j), ACT.Silu).then_inc(s_gate, 1)
                if not last:
                    gathered(b + 1, 0)
                for j in range(2):
                    act.wait_ge(s_hp, 2 * b + j + 1)
                    act.activation(hT[:, 0, 4 * j:4 * j + 4, :], bank4(7 - j), ACT.Identity).then_inc(s_hTh, 1)
                if not last:
                    gathered(b + 1, 1)
                high(b, DC + 2)
                if not last:
                    rows_high(b + 1, 0)
                high(b, DC + 3)
                if not last:
                    rows_high(b + 1, 1)
                    high(b + 1, 0)
                    high(b + 1, 1)
                act.wait_ge(s_wu, MU * b + MU)
                act.activation(yd[:, 0, :].rearrange("p (n f) -> p n f", n=2), ps[:, 6:8, :], ACT.Identity).then_inc(s_ydh, 1)
                if not last:
                    high(b + 1, 2)

            high(0, 0)
            high(0, 1)
            act.wait_ge(s_mx, 1)
            act.activation(prob, prob, ACT.Exp).then_inc(s_ex, 1)
            high(0, 2)
            act.activation(rstd, rstd, ACT.Silu)
            gathered(0, 0)
            gathered(0, 1)
            rows_high(0, 0)
            rows_high(0, 1)
            act.wait_ge(s_nblk, 1)
            final = act.value_load(nblk_i[0:1, 1:2], min_val=E - 1, max_val=E * ROUNDS - 1)
            with act.Fori(0, final) as b:
                moe(b, False)
            moe(final, True)

            for t in range(TT):
                normalise(t, TT + t)

        @block.vector
        def _(dve):
            for s in (s_oacc, s_var, s_stu, s_adau, s_yl, s_acc, s_ydl, s_bcu):
                dve.sem_inc(s, 1)
            dve.memset(accA, 0.0).then_inc(s_acc0, 1)
            dve.memset(acg.bitcast(F32), 0.0)
            dve.wait_ge(s_cact, 1)
            dve.wait_ge(ld_b0, 16)
            for k in range(DC):
                dve.wait_ge(ld_adaA[k % 4], 16 * (k // 4 + 1))
                if k:
                    dve.wait_ge(s_adaA, k)
                dve.scalar_tensor_tensor(accA, adaA[:, k % 4, :], cact[:, k:k + 1], accA, ALU.mult, ALU.add).then_inc(s_adaA, 1)
            dve.wait_ge(s_rowp, 2)
            dve.tensor_copy(taps, ps[:, 0, 0:120].rearrange("p (k j) -> p k j", k=5)).then_inc(s_rowc, 1)
            dve.tensor_copy(normg, ps[:, 0, 128:144]).then_inc(s_rowc, 1)
            dve.wait_ge(s_modp, 1)
            dve.tensor_copy(modc[:, 0:DC], ps[:, 0, 160:160 + DC]).then_inc(s_modc, 1)
            dve.tensor_scalar(modc[:, DC:], ps[:, 0, 160 + DC:160 + 2 * DC], 1.0, None, ALU.add).then_inc(s_modc, 1)
            dve.wait_ge(s_modc, 2)

            def hin_low(k):
                dve.wait_ge(s_hinh, k + 1)
                dve.tensor_tensor(hin[:, 1, k, :], hraw[:, k % 4, :], hin[:, 0, k, :].bitcast(F32), ALU.subtract).then_inc(s_hinv, 1)

            for k in range(DC):
                dve.wait_ge(s_xtp, k + 1)
                if k >= 4:
                    dve.wait_ge(s_hinv if k % 2 else s_hinl, k // 2 - 1)
                dve.tensor_scalar(hraw[:, k % 4, :], bank(1 + k % 7), modc[:, DC + k:DC + k + 1], modc[:, k:k + 1],
                                  ALU.mult, ALU.add).then_inc(s_hraw, 1)
                if k >= 2 and k % 2 == 0:
                    hin_low(k - 1)
            hin_low(DC - 1)
            def xbc_taps(g):
                dve.tensor_copy(gtaps[:, :, 0:1], taps[:, :, ds(g + 16, 1)]).then_inc(s_gtap, 1)
                dve.tensor_copy(gtaps[:, :, 1:2], taps[:, :, ds(g + 20, 1)]).then_inc(s_gtap, 1)
                dve.tensor_copy(gtaps[:, :, 2:NT], taps[:, :, ds(4 * g, 4)]).then_inc(s_gtap, 1)
                dve.wait_ge(s_gtap, 3 * g + 3)

            def xbc_tile(g, i):
                dve.wait_ge(s_cv0, NT * g + i + 1)
                for n, k in enumerate((2, 1, 0)):
                    s = NTAP - 1 - k
                    if n:
                        dve.wait_ge(s_tap, 2 * (NT * g + i) + n)
                    op = dve.scalar_tensor_tensor(conv[:, i % 2, s:], ps[:, i % 2, 0:T - s], gtaps[:, k, i:i + 1],
                                                  conv[:, i % 2, s:], ALU.mult, ALU.add)
                    op.then_inc(s_cv if n == 2 else s_tap, 1)

            def seg_head(g, h):
                dve.wait_ge(s_abc, HG * g + h + 1)
                if h >= 2:
                    dve.wait_ge(s_m, HG * g + h - 1)
                for k in range(TT):
                    a = gtok[:, k, 0, h:h + 1]
                    op = dve.tensor_scalar(seg[:, h % 2, k, :], ps[:, 2 + h % 2, k * P:(k + 1) * P], a, a, ALU.min, ALU.subtract)
                op.then_inc(s_seg, 1)

            def mix_head(g, h):
                dve.wait_ge(s_dec, HG * g + h + 1)
                if h == 0:
                    dve.wait_ge(s_cbm, g + 1)
                if h >= 4:
                    dve.wait_ge(s_y, 4 * g + (h - 4) // 2 + 1)
                dve.tensor_tensor(mh[:, h % 4], seg[:, h % 2], cbm, ALU.mult).then_inc(s_m, 1)

            def ada_piece(g, k):
                dve.wait_ge(ld_ada[k % 2], 16 * (4 * g + k // 2 + 1))
                if k == 0:
                    dve.wait_ge(ld_bg, 16 * (g + 1))
                else:
                    dve.wait_ge(s_adau, DC * g + k + 1)
                dve.scalar_tensor_tensor(acc, ada[:, k % 2, :], cact[:, k:k + 1], acc, ALU.mult, ALU.add).then_inc(s_adau, 1)

            def state_step(g, k):
                dve.wait_ge(s_st, 3 * g + k + 1)
                if k == 0:
                    dve.tensor_copy(state[:, 0, :], bank(5)).then_inc(s_stu, 1)
                else:
                    dve.wait_ge(s_stu, 3 * g + k + 1)
                    el = gel[:, :, k].unsqueeze(2).broadcast_to([P, HG, HD])
                    dve.tensor_tensor(stmp.rearrange("p (h n) -> p h n", h=HG), state[:, k - 1, :].rearrange("p (h n) -> p h n", h=HG), el, ALU.mult).then_inc(s_stm, 1)
                    dve.wait_ge(s_stm, 2 * g + k)
                    dve.tensor_tensor(state[:, k, :], stmp, bank(5), ALU.add).then_inc(s_stu, 1)

            steps = [0]

            def link(op):
                steps[0] += 1
                op.then_inc(s_n, 1)
                dve.wait_ge(s_n, steps[0])

            def residual(q):
                if q == 0:
                    dve.wait_ge(ld_x2, 16 * TT)
                dve.wait_ge(s_oacc, 8 * (G - 1) + 2 * q + 3)
                cols = slice(q * 256, (q + 1) * 256)
                if q < 3:
                    link(dve.tensor_tensor(oacc[:, :, cols], oacc[:, :, cols], modr[:, 0, cols].unsqueeze(1).broadcast_to([P, TT, 256]), ALU.mult))
                    link(dve.scalar_tensor_tensor(xt[:, :, cols], xt[:, :, cols], ALPHA, oacc[:, :, cols], ALU.mult, ALU.add))
                for t in {1: (0, 1), 2: (2, 3)}.get(q, ()):
                    dve.bn_stats(st6[:, t, 0, :], xt[:, t, 0:512])

            def gate(g, q):
                dve.wait_ge(s_y, 4 * g + q + 1)
                if q >= 2:
                    dve.wait_ge(s_yz, 4 * g + q - 1)
                yt = seg[:, q % 2].rearrange("p c t -> p (c t)")
                dve.scalar_tensor_tensor(yt, xT[:, q, :], gnd[:, 1, q:q + 1], bank(6 + q % 2), ALU.mult, ALU.add).then_inc(s_y1, 1)
                dve.wait_ge(s_y1, 4 * g + q + 1)
                dve.tensor_tensor(yT[:, q, :], yt, yT[:, q, :], ALU.mult).then_inc(s_yz, 1)

            def turn(g, last):
                dve.tensor_copy(gtok, tok[:, :, :, ds(HG * g, HG)]).then_inc(s_gc, 1)
                dve.tensor_copy(gel, elast[:, :, ds(TT * g, TT)]).then_inc(s_gc, 1)
                dve.tensor_copy(gnd[:, 0, :], normg[:, ds(4 * g, 4)]).then_inc(s_gc, 1)
                dve.tensor_copy(gnd[:, 1, :], dskip[:, ds(4 * g, 4)]).then_inc(s_gc, 1)
                dve.wait_ge(s_gc, 4 * g + 4)
                dve.wait_ge(s_cb, g + 1)
                dve.tensor_tensor(cbm, bank4(4), causal.unsqueeze(1).broadcast_to([P, TT, P]), ALU.mult).then_inc(s_cbm, 1)
                for k in range(TT):
                    dve.wait_ge(s_xtr, TT * g + k + 1)
                    src = bank(x_banks[k]).rearrange("p (h n) -> p h n", h=HG)
                    col = lambda n: gtok[:, k, n, :].unsqueeze(2).broadcast_to([P, HG, HD])
                    dve.tensor_tensor(xdt[:, k, :].rearrange("p (h n) -> p h n", h=HG), src, col(1), ALU.mult).then_inc(s_xdt, 1)
                    if k < 3:
                        dve.tensor_tensor(xw[:, k, :].rearrange("p (h n) -> p h n", h=HG), src, col(2), ALU.mult).then_inc(s_xw, 1)
                for h in range(HG):
                    seg_head(g, h)
                    ada_piece(g, h)
                    if h < 3:
                        state_step(g, h)
                    if h:
                        mix_head(g, h - 1)
                if not last:
                    xbc_taps(g + 1)
                mix_head(g, HG - 1)
                dve.wait_ge(s_m, HG * g + HG)
                dve.wait_ge(s_zs, g + 1)
                gate(g, 0)
                gate(g, 1)
                if not last:
                    xbc_tile(g + 1, 0)
                for n in range(2):
                    dve.wait_ge(s_bc, 2 * g + n + 1)
                    dve.tensor_scalar(modr[:, ds(g, 1), n * 512:(n + 1) * 512].rearrange("p a n -> p (a n)"), bank(2 + n),
                                      onep[:, ds(g, 1)], None, ALU.add).then_inc(s_bcu, 1)
                if not last:
                    dve.memset(acc, 0.0).then_inc(s_accz, 1)
                    xbc_tile(g + 1, 1)
                gate(g, 2)
                gate(g, 3)
                for q in range(4):
                    dve.wait_ge(s_yh, 4 * g + q + 1)
                    dve.scalar_tensor_tensor(ysplit[:, 1, q, :], yT[:, q, :], gnd[:, 0, q:q + 1], ysplit[:, 0, q, :].bitcast(F32), ALU.mult, ALU.subtract).then_inc(s_yl, 1)
                if not last:
                    xbc_tile(g + 1, 2)
                dve.wait_ge(s_oacc, 8 * g + 1)
                dve.wait_ge(s_ms, g + 1)
                dve.tensor_scalar(rstd4, ps[:, 4, 0:TT], 1.0 / GW, EPS, ALU.mult, ALU.add).then_inc(s_var, 1)
                if not last:
                    xbc_tile(g + 1, 3)
                dve.wait_ge(s_sqrt, g + 1)
                dve.reciprocal(rstd4, rstd4).then_inc(s_rs, 1)
                if not last:
                    xbc_tile(g + 1, 4)
                    xbc_tile(g + 1, 5)
                dve.wait_ge(s_rs, g + 1)
                for q in range(OU):
                    for j in range(2):
                        if j:
                            dve.wait_ge(s_unit, unit_o(g, q, last) + 1)
                        else:
                            dve.wait_ge(s_out, OU * g + q + 1)
                        for t in (2 * j, 2 * j + 1):
                            o = oacc[:, t, q * 256:(q + 1) * 256]
                            op = dve.scalar_tensor_tensor(o, ps[:, 6 + j, (t % 2) * 256:(t % 2 + 1) * 256], rstd4[:, t:t + 1], o, ALU.mult, ALU.add)
                        op.then_inc(s_oacc, 1)
                    if last:
                        residual(q)

            dve.wait_ge(s_rowc, 2)
            xbc_taps(0)

            dve.wait_ge(s_const, CONSTS)
            dve.wait_ge(s_prea, 2)
            dve.tensor_scalar(aneg[0:32, :], aneg[0:32, :], -1.0, None, ALU.mult).then_inc(s_dtv, 1)
            v, ev, uv, cv, lv = (a[0:32] for a in dtv)
            pre = [0]

            def step(op):
                pre[0] += 1
                op.then_inc(s_pre, 1)
                dve.wait_ge(s_pre, pre[0])

            step(dve.scalar_tensor_tensor(ev, v, -1.0, v, ALU.mult, ALU.max))
            dve.wait_ge(s_prea, 3)
            step(dve.tensor_scalar(uv, ev, 1.0, None, ALU.add))
            step(dve.tensor_scalar(cv, uv, -1.0, None, ALU.add))
            step(dve.tensor_tensor(cv, ev, cv, ALU.subtract))
            dve.wait_ge(s_prea, 4)
            step(dve.reciprocal(uv, uv))
            step(dve.tensor_tensor(cv, cv, uv, ALU.mult))
            step(dve.tensor_tensor(cv, cv, lv, ALU.add))
            step(dve.scalar_tensor_tensor(v, v, 0.0, cv, ALU.max, ALU.add))
            xbc_tile(0, 0)
            dve.wait_ge(s_dtv, 1)
            dve.tensor_scalar(cv, v, aneg[0:32, :], None, ALU.mult).then_inc(s_dtv, 1)
            dve.wait_ge(s_dtv, 2)
            dve.tensor_copy(stk[32:64], v)
            for k in range(TT):
                op = dve.tensor_tensor_scan(stk[0:32, k * P:(k + 1) * P], ones[0:32, :],
                                            cv[:, k * P:(k + 1) * P], 0.0, ALU.mult, ALU.add)
            step(op)
            acum3 = stk[0:32].rearrange("p (c t) -> p c t", t=P)
            step(dve.tensor_tensor(ev.rearrange("p (c t) -> p c t", t=P), acum3[:, :, P - 1:P].broadcast_to([32, TT, P]), acum3, ALU.subtract))
            xbc_tile(0, 1)
            for g in range(G):
                dve.tensor_scalar(acg[0:32, g, :], stk[0:32], gmask[0:32, g:g + 1], None, ALU.mult).then_inc(s_dtv, 1)
            dve.wait_ge(s_dtv, 2 + G)
            for g in range(G):
                dve.scalar_tensor_tensor(acg[32:64, g, :], stk[0:32], gmask[0:32, g:g + 1], acg[0:32, g, :].bitcast(F32), ALU.mult, ALU.subtract).then_inc(s_dtv, 1)
            dve.tensor_reduce(every8, ident.rearrange("p (a j) -> p j a", j=HG), AX.X, ALU.add).then_inc(s_dtv, 1)
            dve.wait_ge(s_dtv, 3 + 2 * G)
            dve.tensor_copy(every8r, every8).then_inc(s_dtv, 1)
            dve.wait_ge(s_prea, 5)
            step(dve.tensor_tensor(stk[64:96], ev, v, ALU.mult))
            xbc_tile(0, 2)
            xbc_tile(0, 3)
            dve.wait_ge(s_tokp, 1)
            dve.tensor_copy(tok, ps[:, 5, 0:TT * 96].rearrange("p (c s h) -> p c s h", c=TT, s=3)).then_inc(s_tok, 1)
            xbc_tile(0, 4)
            xbc_tile(0, 5)
            dve.wait_ge(s_tok, 1)
            dve.wait_ge(s_el, 1)
            groups(dve, lambda g: turn(g, False), lambda g: turn(g, True))

            def scale(t, n):
                dve.wait_ge(s_var1, n + 1)
                dve.wait_ge(s_sd1, n + 1)
                link(dve.reciprocal(rstd[:, t:t + 1], rstd[:, t:t + 1]))
                dve.scalar_tensor_tensor(shift[:, t:t + 1], mv[:, t, 0:1], -1.0, rstd[:, t:t + 1], ALU.mult, ALU.mult).then_inc(s_shift, 1)

            def last_quarter(t):
                cols = slice(3 * 256, D)
                link(dve.tensor_tensor(oacc[:, t, cols], oacc[:, t, cols], modr[:, 0, cols], ALU.mult))
                link(dve.scalar_tensor_tensor(xt[:, t, cols], xt[:, t, cols], ALPHA, oacc[:, t, cols], ALU.mult, ALU.add))
                link(dve.bn_stats(st6[:, t, 1, :], xt[:, t, 512:]))
                dve.bn_aggr(mv[:, t, :], st6[:, t].rearrange("p s n -> p (s n)")).then_inc(s_var1, 1)

            def modulate(t):
                if t == 1:
                    dve.wait_ge(s_h2m, 1)
                else:
                    dve.wait_ge(s_nrm, t + 1)
                    if t == 3:
                        dve.wait_ge(s_h2l, 1)
                        dve.wait_ge(s_h2t, 2)
                    link(dve.tensor_tensor(h2f[t], xt[:, t, :], modr[:, 2, :], ALU.mult))
                dve.tensor_tensor(h2f[t], h2f[t], modr[:, 1, :], ALU.add).then_inc(s_h2f, 1)

            last_quarter(0)
            last_quarter(1)
            scale(0, 0)
            last_quarter(2)
            scale(1, 1)
            dve.wait_ge(s_fold, 3)
            modulate(0)
            last_quarter(3)
            scale(2, 2)
            modulate(1)
            scale(3, 3)
            modulate(2)
            modulate(3)
            for t in range(2):
                dve.tensor_tensor(xt[:, t, :], xt[:, t, :], lnr[:, 0, :], ALU.mult).then_inc(s_x1v, 1)
                dve.wait_ge(s_x1v, 2 * t + 1)
                dve.tensor_tensor(xt[:, t, :], xt[:, t, :], lnr[:, 1, :], ALU.add).then_inc(s_x1v, 1)

            dve.wait_ge(s_lg, TT)
            dve.wait_ge(ld_r, 32)
            dve.wait_ge(s_h2l, 3)
            b3 = lambda a, n=E: a.unsqueeze(2).broadcast_to([P, TT, n])
            link(dve.tensor_copy(prob, ps[:, 6, 0:TT * E].rearrange("p (t e) -> p t e", e=E)))
            link(dve.tensor_reduce(red, prob, AX.X, ALU.max))
            dve.tensor_tensor(prob, prob, b3(red), ALU.subtract).then_inc(s_mx, 1)
            dve.wait_ge(s_ex, 1)
            link(dve.tensor_reduce(red, prob, AX.X, ALU.add))
            link(dve.reciprocal(red2, red))
            link(dve.tensor_tensor(prob, prob, b3(red2), ALU.mult))
            link(dve.tensor_tensor(selp, prob, rb.unsqueeze(1).broadcast_to([P, TT, E]), ALU.add))

            def ranks(val, rank):
                this = val.unsqueeze(3).broadcast_to([P, val.shape[1], 4, 4])
                other = val.unsqueeze(2).broadcast_to([P, val.shape[1], 4, 4])
                ge, gt = (c[:, 0:val.shape[1]] for c in pairs)
                of = lambda m: m.unsqueeze(1).broadcast_to([P, val.shape[1], 4, 4])
                dve.tensor_tensor(ge, other, this, ALU.is_ge)
                link(dve.tensor_tensor(gt, other, this, ALU.is_gt))
                dve.tensor_tensor(ge, ge, of(earlier), ALU.mult)
                link(dve.tensor_tensor(gt, gt, of(later), ALU.mult))
                link(dve.tensor_tensor(ge, ge, gt, ALU.add))
                link(dve.tensor_reduce(rank, ge, AX.X, ALU.add))

            quad = lambda a: a.rearrange("p t (g e) -> p (t g) e", e=E // EG)
            ranks(quad(selp), quad(rank))
            link(dve.tensor_scalar(rank, rank, 2.0, None, ALU.is_lt))
            link(dve.tensor_tensor(tie, selp, rank, ALU.mult))
            link(dve.tensor_reduce(gsum.rearrange("p t g -> p (t g)"), quad(tie), AX.X, ALU.add))
            ranks(gsum, grank)
            link(dve.tensor_scalar(grank, grank, 1.0, None, ALU.is_lt))
            link(dve.tensor_tensor(quad(mask), quad(rank), grank.rearrange("p t g -> p (t g)").unsqueeze(2).broadcast_to([P, TT * EG, E // EG]), ALU.mult))
            dve.memset(cum[:, 0, :], 0.0)
            link(dve.tensor_copy(cum[:, 1, :], mask[:, 0, :]))
            for t in range(1, TT):
                op = dve.tensor_tensor(cum[:, t + 1, :], cum[:, t, :], mask[:, t, :], ALU.add)
                if t < TT - 1:
                    link(op)
            op.then_inc(s_mask, 1)
            link(dve.tensor_tensor(wts, prob, mask, ALU.mult))
            link(dve.tensor_reduce(red, wts, AX.X, ALU.add))
            link(dve.reciprocal(red2, red))
            link(dve.tensor_tensor(wts, wts, b3(red2), ALU.mult))
            dve.wait_ge(s_pos, 1)
            link(dve.scalar_tensor_tensor(pm, ps[:, 7, 0:TT * E].rearrange("p (t e) -> p t e", e=E), 1.0, mask, ALU.add, ALU.mult))
            link(dve.tensor_scalar(pmx[:, :, 0, :], pm, -1.0, None, ALU.add))
            pmb = pmx.rearrange("p t r e -> p t (r e)")

            def select(b):
                for t in range(TT):
                    op = dve.tensor_scalar(sel[:, t, :], iota, pmb[:, t, ds(b, 1)], None, ALU.is_equal)
                op.then_inc(s_sel, 1)

            select(0)
            link(dve.tensor_reduce(nbf[:, 0:1], ps[:, 7, TT * E:TT * E + E], AX.X, ALU.max))
            link(dve.tensor_scalar(cnt[:, 0:1], nbf[:, 0:1], float(P), float(E), ALU.is_gt, ALU.mult))
            link(dve.tensor_scalar(cnt[:, 1:2], nbf[:, 0:1], float(2 * P), float(E), ALU.is_gt, ALU.mult))
            link(dve.tensor_scalar(cnt[:, 2:3], nbf[:, 0:1], float(3 * P), float(E), ALU.is_gt, ALU.mult))
            link(dve.tensor_reduce(nbf[:, 1:2], cnt[:, 0:3], AX.X, ALU.add))
            dve.tensor_scalar(nblk_i[0:1, 0:1], nbf[0:1, 1:2], float(E), None, ALU.add)
            dve.tensor_scalar(nblk_i[0:1, 1:2], nbf[0:1, 1:2], float(E - 1), None, ALU.add).then_inc(s_nblk, 1)
            for r in range(1, ROUNDS):
                dve.tensor_scalar(pmx[:, :, r, :], pm, float(-1 - P * r), None, ALU.add)
            for r in range(ROUNDS):
                dve.tensor_copy(wtb[:, :, 1 + r * E:1 + (r + 1) * E], wts)
            link(dve.memset(wtb[:, :, 0:1], 0.0))
            dve.wait_ge(s_nblk, 1)
            final = dve.value_load(nblk_i[0:1, 1:2], min_val=E - 1, max_val=E * ROUNDS - 1)

            def low(b, i):
                dve.wait_ge(s_wh, MU * b + (i + 1))
                part = slice(0, 2 * D - POOL_PART)
                dve.tensor_tensor(wr[:, i % SPLIT, 1, part], ring[:, i % RING, part], wr[:, i % SPLIT, 0, part].bitcast(F32), ALU.subtract).then_inc(s_wlv, 1)

            def add(b, js):
                for j in js:
                    dve.wait_ge(s_sc, 8 * b + j + 1)
                    t = j // 2
                    o = oacc[:, t, (j % 2) * 512:(j % 2 + 1) * 512]
                    dve.scalar_tensor_tensor(o, bank(4 + j % 2), wtb[:, t, ds(b, 1)], o, ALU.mult, ALU.add).then_inc(s_acc, 1)

            def rows_low(b, j):
                dve.wait_ge(s_xeh, 2 * b + j + 1)
                h = slice(4 * j, 4 * j + 4)
                dve.tensor_tensor(xe[:, 1, h, :], bank4(4 + j), xe[:, 0, h, :].bitcast(F32), ALU.subtract).then_inc(s_xel, 1)

            def moe(b, last):
                dve.wait_ge(s_acc, 8 * b + 1)
                add(b, (0,))
                low(b, 3)
                add(b, (1,))
                low(b, 4)
                for i in range(5, 8):
                    add(b, (2 * i - 8, 2 * i - 7))
                    low(b, i)
                if not last:
                    dve.wait_ge(s_selp, b + 1)
                    select(b + 1)
                low(b, DC)
                low(b, DC + 1)
                for j in range(2):
                    half = slice(j * 512, (j + 1) * 512)
                    dve.wait_ge(s_gate, 2 * b + j + 1)
                    dve.tensor_tensor(hid[:, half], sgate[:, half], bank(2 + j), ALU.mult).then_inc(s_hid, 1)
                for j in range(2):
                    dve.wait_ge(s_hTh, 2 * b + j + 1)
                    h = slice(4 * j, 4 * j + 4)
                    dve.tensor_tensor(hT[:, 1, h, :], bank4(7 - j), hT[:, 0, h, :].bitcast(F32), ALU.subtract).then_inc(s_hTl, 1)
                low(b, DC + 2)
                if not last:
                    rows_low(b + 1, 0)
                low(b, DC + 3)
                if not last:
                    rows_low(b + 1, 1)
                    low(b + 1, 0)
                    low(b + 1, 1)
                dve.wait_ge(s_ydh, b + 1)
                two = lambda a: a.rearrange("p (n f) -> p n f", n=2)
                dve.tensor_tensor(two(yd[:, 1, :]), ps[:, 6:8, :], two(yd[:, 0, :].bitcast(F32)), ALU.subtract).then_inc(s_ydl, 1)
                if not last:
                    low(b + 1, 2)

            rows_low(0, 0)
            rows_low(0, 1)
            dve.wait_ge(s_zero, 2)
            with dve.Fori(0, final) as b:
                moe(b, False)
            moe(final, True)

            def gated(t):
                link(dve.tensor_tensor(oacc[:, t, :], oacc[:, t, :], modr[:, 3, :], ALU.mult))

            def sums(t):
                if t % 2:
                    dve.wait_ge(s_om, t // 2 + 1)
                link(dve.scalar_tensor_tensor(xt[:, t, :], xt[:, t, :], ALPHA, oacc[:, t, :], ALU.mult, ALU.add))
                dve.bn_stats(st6[:, t, 0, :], xt[:, t, 0:512])
                link(dve.bn_stats(st6[:, t, 1, :], xt[:, t, 512:]))
                dve.bn_aggr(mv[:, t, :], st6[:, t].rearrange("p s n -> p (s n)")).then_inc(s_var1, 1)

            def finish(t):
                if t < 3:
                    dve.wait_ge(s_gain, t + 2)
                else:
                    dve.wait_ge(s_nrm, TT + t + 1)
                    link(dve.tensor_tensor(xt[:, t, :], xt[:, t, :], lnr2[:, 0, :], ALU.mult))
                dve.tensor_tensor(xt[:, t, :], xt[:, t, :], lnr2[:, 1, :], ALU.add).then_inc(s_done, 1)

            dve.wait_ge(s_x1p, 4)
            dve.wait_ge(ld_ln, 16 * 4)
            add(final + 1, (0, 1))
            dve.wait_ge(s_acc, 8 * final + 11)
            gated(0)
            add(final + 1, (2, 3))
            sums(0)
            add(final + 1, (4, 5))
            scale(0, TT)
            dve.wait_ge(s_acc, 8 * final + 15)
            gated(2)
            add(final + 1, (6, 7))
            sums(1)
            sums(2)
            scale(1, TT + 1)
            sums(3)
            scale(2, TT + 2)
            scale(3, TT + 3)
            finish(1)
            finish(3)
            finish(2)

        @block.tensor
        def _(pe):
            mm = nc.tensor.matmul
            pe.wait_ge(s_const, CONSTS)

            def x_chunk(k):
                for t in range(TT):
                    op = nc.tensor.transpose(ps[:, 1 + k % 7, t * P:(t + 1) * P], oacc[:, t, k * P:(k + 1) * P], ident)
                op.then_inc(s_xtp, 1)

            pe.wait_ge(ld_small, 16 * 7)
            nc.tensor.transpose(ps[:, 0, 0:120], rows[0:120, 0, :], ident[0:120, 0:120]).then_inc(s_rowp, 1)
            nc.tensor.transpose(ps[:, 0, 128:144], rows[0:16, 1, :], ident[0:16, 0:16]).then_inc(s_rowp, 1)
            pe.wait_ge(s_rowc, 2)
            pe.wait_ge(s_adaA, DC)
            for j in range(16):
                op = mm(ps[:, 0, 160 + j:161 + j], accA[:, j * P:(j + 1) * P], ones[:, 0:1], start=True, stop=True)
            op.then_inc(s_modp, 1)
            pe.wait_ge(ld_x, 16 * TT)
            for k in range(DC):
                if k == 7:
                    pe.wait_ge(s_hraw, 1)
                x_chunk(k)

            def parts(slot, k, n):
                return wsplit[:, slot, 0, :].rearrange("p (k n) -> p k n", k=k), wsplit[:, slot, 1, :].rearrange("p (k n) -> p k n", k=k)

            def tile(u, slot, to):
                pe.wait_ge(s_ul, u + 1)
                wh, wl = parts(slot, DC, P)
                for k in range(DC):
                    mm(to, wh[:, k, :], hin[:, 0, k, :], start=(k == 0), stop=False)
                    mm(to, wh[:, k, :], hin[:, 1, k, :], start=False, stop=False)
                    op = mm(to, wl[:, k, :], hin[:, 0, k, :], start=False, stop=(k == DC - 1))
                op.then_inc(s_unit, 1)

            def xbc_tile(g, i):
                if i >= 2:
                    pe.wait_ge(s_cv, NT * g + i - 1)
                elif not isinstance(g, int):
                    pe.wait_ge(s_zc, ZT * (g - 1) + i + 3)
                tile(unit_x(g, i), i % 2, bank(i % 2))

            def z_tile(g, i):
                if i >= 2:
                    pe.wait_ge(s_zc, ZT * g + i - 1)
                elif i == 0:
                    pe.wait_ge(s_xw, 3 * g + 1)
                else:
                    pe.wait_ge(s_xdt, TT * g + 4)
                tile(unit_z(g, i), i % 2, bank(i % 2))

            pe.wait_ge(s_dtl, 1)
            pe.wait_ge(s_hraw, 3)
            for k in range(DC):
                pe.wait_ge(s_hinv if k % 2 else s_hinl, k // 2 + 1)
                mm(ps[0:32, 3, :], dtsplit[0][:, k, :], hin[:, 0, k, :], start=(k == 0), stop=False)
                mm(ps[0:32, 3, :], dtsplit[0][:, k, :], hin[:, 1, k, :], start=False, stop=False)
                op = mm(ps[0:32, 3, :], dtsplit[1][:, k, :], hin[:, 0, k, :], start=False, stop=(k == DC - 1))
            op.then_inc(s_dtp, 1)
            for i in range(4):
                xbc_tile(0, i)
            pe.wait_ge(s_dtv, 4 + 2 * G)
            acl = acg.rearrange("p g (c t) -> p (g c) t", t=P)
            for j in range(HG):
                op = mm(ps[:, 4, j * 16:(j + 1) * 16], every8r[:, j:j + 1].broadcast_to([P, P]), acl[:, :, P - 1], start=True, stop=True)
            op.then_inc(s_elp, 1)
            pe.wait_ge(s_pre, 11)
            for k in range(TT):
                op = nc.tensor.transpose(ps[:, 5, k * 96:(k + 1) * 96], stk[0:96, k * P:(k + 1) * P], ident[0:96, 0:96])
            op.then_inc(s_tokp, 1)
            xbc_tile(0, 4)
            xbc_tile(0, 5)

            def acum_rows(g, h):
                if h < 2:
                    pe.wait_ge(s_bcu, 2 * g + 1)
                else:
                    pe.wait_ge(s_e, HG * g + h - 1 + 1)
                mm(bank(2 + h % 2), every8r[:, h:h + 1].broadcast_to([P, P]),
                   acg[:, ds(g, 1), :].rearrange("p a t -> p (a t)"), start=True, stop=True).then_inc(s_abc, 1)

            def state_sum(g, k):
                pe.wait_ge(s_xw, 3 * g + k + 1)
                if k == 0:
                    pe.wait_ge(s_btok, g + 1)
                else:
                    pe.wait_ge(s_stu, 3 * g + k + 1)
                mm(bank(5), btok[:, k, :], xw[:, k, :], start=True, stop=True).then_inc(s_st, 1)

            def y_pair(g, q):
                pe.wait_ge(s_m, HG * g + 2 * q + 2)
                pe.wait_ge(s_ch, HG * g + 2 * q + 2)
                if q == 0:
                    pe.wait_ge(s_stu, 3 * g + 4)
                    pe.wait_ge(s_oacc, 8 * g + 1)
                if q >= 2:
                    pe.wait_ge(s_y1, 4 * g + q - 1)
                for k in range(TT):
                    for hh in range(2):
                        h = 2 * q + hh
                        o = ps[hh * HD:(hh + 1) * HD, 6 + q % 2, k * P:(k + 1) * P]
                        op = mm(o, xdt[:, k, h * HD:(h + 1) * HD], mh[:, h % 4, k, :], start=True, stop=(k == 0))
                        if k:
                            op = mm(o, state[:, k - 1, h * HD:(h + 1) * HD], ch[:, h % 4, (k - 1) * P:k * P], start=False, stop=True)
                op.then_inc(s_y, 1)

            def turn(g, last):
                pe.wait_ge(s_silu, NT * (g + 1))
                pe.wait_ge(s_var, g + 1)
                for k in range(TT):
                    t = slice(k * P, (k + 1) * P)
                    op = mm(ps[:, 4, t], bT[:, t], cT[:, t], start=True, stop=True)
                op.then_inc(s_cb, 1)
                pe.wait_ge(s_stu, 3 * g + 1)
                for k in range(TT):
                    t = slice(k * P, (k + 1) * P)
                    op = nc.tensor.transpose(ps[:, 5, t], bT[:, t], ident)
                op.then_inc(s_btr, 1)
                for k in range(TT):
                    if k == 0:
                        pe.wait_ge(s_cv, NT * g + NT)
                    if k == 1:
                        pe.wait_ge(s_oacc, 8 * g + 1)
                    for j in range(4):
                        op = nc.tensor.transpose(ps[:, x_banks[k], j * P:(j + 1) * P], xT[:, j, k * P:(k + 1) * P], ident)
                    op.then_inc(s_xtr, 1)
                acum_rows(g, 0)
                acum_rows(g, 1)
                state_sum(g, 0)
                z_tile(g, 0)
                state_sum(g, 1)
                acum_rows(g, 2)
                z_tile(g, 1)
                state_sum(g, 2)
                acum_rows(g, 3)
                acum_rows(g, 4)
                z_tile(g, 2)
                acum_rows(g, 5)
                y_pair(g, 0)
                acum_rows(g, 6)
                z_tile(g, 3)
                acum_rows(g, 7)
                y_pair(g, 1)
                if not last:
                    xbc_tile(g + 1, 0)
                pe.wait_ge(s_adau, DC * g + DC + 1)
                pe.wait_ge(s_e, HG * g + HG + 1)
                for n in range(2):
                    mm(bank(2 + n), ones, acc[:, n * 512:(n + 1) * 512], start=True, stop=True).then_inc(s_bc, 1)
                if not last:
                    xbc_tile(g + 1, 1)
                y_pair(g, 2)
                y_pair(g, 3)
                if not last:
                    xbc_tile(g + 1, 2)
                    xbc_tile(g + 1, 3)
                pe.wait_ge(s_cbm, g + 1)
                pe.wait_ge(s_sqs, 3 * g + 3)
                for t in range(TT):
                    op = mm(ps[:, 4, t:t + 1], squares[0][:, t * P:(t + 1) * P], ones[:, 0:1], start=True, stop=True)
                op.then_inc(s_ms, 1)
                if not last:
                    for i in range(4, NT):
                        xbc_tile(g + 1, i)
                pe.wait_ge(s_yl, 4 * g + 5)
                for q in range(OU):
                    pe.wait_ge(s_ul, unit_o(g, q, last) + 1)
                    wh, wl = parts(q % 2, 4, 256)
                    for j in range(2):
                        if q:
                            pe.wait_ge(s_oacc, 8 * g + 2 * q + j)
                        for t in (2 * j, 2 * j + 1):
                            to, tt = ps[:, 6 + j, (t % 2) * 256:(t % 2 + 1) * 256], slice(t * P, (t + 1) * P)
                            for k in range(4):
                                mm(to, ysplit[:, 0, k, tt], wh[:, k, :], start=(k == 0), stop=False)
                                mm(to, ysplit[:, 0, k, tt], wl[:, k, :], start=False, stop=False)
                                op = mm(to, ysplit[:, 1, k, tt], wh[:, k, :], start=False, stop=(k == 3))
                        op.then_inc(s_unit if j else s_out, 1)

            pe.wait_ge(s_tok, 1)
            pe.wait_ge(s_el, 1)
            groups(pe, lambda g: turn(g, False), lambda g: turn(g, True))

            def rows_turned(t):
                pe.wait_ge(s_h2f, t + 1)
                for j in range(2):
                    if t >= 2:
                        pe.wait_ge(s_h2tc, 2 * t - 3 + j)
                    for k in range(4):
                        op = nc.tensor.transpose(ps[:, rows_bank(t) + j, k * P:(k + 1) * P], h2f[t][:, (4 * j + k) * P:(4 * j + k + 1) * P], ident)
                    op.then_inc(s_h2t, 1)

            def logits(t):
                if t == 0:
                    pe.wait_ge(ld_r, 32)
                pe.wait_ge(s_h2tc, 2 * t + 2)
                for k in range(DC):
                    op = mm(ps[:, 6, t * E:(t + 1) * E], h2T[t % 2][:, k, :], rw[:, k, :], start=(k == 0), stop=(k == DC - 1))
                op.then_inc(s_lg, 1)

            rows_turned(0)
            for t in range(1, TT):
                rows_turned(t)
                logits(t - 1)
            logits(TT - 1)
            pe.wait_ge(s_mask, 1)
            mm(ps[:, 7, 0:(TT + 1) * E], ones, cum.rearrange("p t e -> p (t e)"), start=True, stop=False)
            mm(ps[:, 7, 0:TT * E], before, mask.rearrange("p t e -> p (t e)"), start=False, stop=True).then_inc(s_pos, 1)

            pe.sem_inc(s_xt, 1)

            def gather(b, j):
                if j == 0:
                    pe.wait_ge(s_sel, b + 1)
                for t in range(TT):
                    for part in range(2):
                        op = mm(bank(4 + j), sel[:, t, :], h2[:, part, t, j * 512:(j + 1) * 512], start=(t + part == 0), stop=(t == TT - 1 and part == 1))
                op.then_inc(s_ga, 1)

            def turn_rows(b, j):
                pe.wait_ge(s_xg, 2 * b + 2)
                for k in range(4):
                    d = 4 * j + k
                    op = nc.tensor.transpose(ps[:, 4 + j, k * P:(k + 1) * P], xg[:, d * P:(d + 1) * P], ident)
                op.then_inc(s_xt, 1)

            def scatter(b, j):
                if j == 0:
                    pe.wait_ge(s_ydl, b + 1)
                if j >= 2:
                    pe.wait_ge(s_acc, 8 * b + j - 1 + 1)
                t, n = j // 2, slice((j % 2) * 512, (j % 2 + 1) * 512)
                mm(bank(4 + j % 2), selT[:, t, :], yd[:, 0, n], start=True, stop=False)
                mm(bank(4 + j % 2), selT[:, t, :], yd[:, 1, n], start=False, stop=True).then_inc(s_sc, 1)

            def products(to, xh, xl, wh, wl, start, stop):
                n = range(len(to))
                for i in n:
                    mm(to[i], xh, wh[i], start=start, stop=False)
                for i in n:
                    mm(to[i], xh, wl[i], start=False, stop=False)
                for i in n:
                    op = mm(to[i], xl, wh[i], start=False, stop=stop)
                return op

            def moe(b, last):
                for i in range(DC):
                    if i % 4 == 0:
                        pe.wait_ge(s_xel, 2 * b + i // 4 + 1)
                    pe.wait_ge(s_wlv, MU * b + (i + 1))
                    pe.wait_ge(s_wlp, MU * b + (i + 1))
                    cols = [[wr[:, i % SPLIT, s, n * 512:(n + 1) * 512] for n in range(4)] for s in range(2)]
                    products([bank(n) for n in range(4)], xe[:, 0, i, :], xe[:, 1, i, :], cols[0], cols[1], i == 0, i == DC - 1).then_inc(s_wu, 1)
                    if 1 <= i < 5:
                        if i == 1:
                            pe.wait_ge(s_xel, 2 * b + 2)
                        scatter(b, 2 * i - 2)
                        scatter(b, 2 * i - 1)
                    if i == 5:
                        pe.wait_ge(s_acc, 8 * b + 7 + 1)
                        for t in range(TT):
                            op = nc.tensor.transpose(ps[:, 4, t * P:(t + 1) * P], sel[:, t, :].bitcast(F32), ident)
                        op.then_inc(s_selp, 1)
                pe.wait_ge(s_selT, b + 1)
                pe.wait_ge(s_acc, 8 * b + 8 + 1)
                if not last:
                    gather(b + 1, 0)
                for j in range(2):
                    pe.wait_ge(s_hid, 2 * b + j + 1)
                    for k in range(4):
                        d = 4 * j + k
                        op = nc.tensor.transpose(ps[:, 7 - j, k * P:(k + 1) * P], hid[:, d * P:(d + 1) * P], ident)
                    op.then_inc(s_hp, 1)
                if not last:
                    gather(b + 1, 1)
                pe.wait_ge(s_hTl, 2 * b + 2)
                for i in range(DC, MU):
                    pe.wait_ge(s_wlv, MU * b + (i + 1))
                    pe.wait_ge(s_wlp, MU * b + (i + 1))
                    for kk in range(2):
                        k = 2 * (i - DC) + kk
                        cols = [[wr[:, i % SPLIT, s, kk * D + n * 512:kk * D + (n + 1) * 512] for n in range(2)] for s in range(2)]
                        op = products([bank(6), bank(7)], hT[:, 0, k, :], hT[:, 1, k, :], cols[0], cols[1], k == 0, k == DC - 1)
                    op.then_inc(s_wu, 1)
                    if i < DC + 2 and not last:
                        turn_rows(b + 1, i - DC)

            pe.wait_ge(s_h2tc, 2 * TT)
            pe.wait_ge(s_h2l, TT)
            gather(0, 0)
            gather(0, 1)
            turn_rows(0, 0)
            turn_rows(0, 1)
            pe.wait_ge(s_zero, 1)
            pe.wait_ge(s_nblk, 1)
            final = pe.value_load(nblk_i[0:1, 1:2], min_val=E - 1, max_val=E * ROUNDS - 1)
            with pe.Fori(0, final) as b:
                moe(b, False)
            moe(final, True)
            for j in range(8):
                scatter(final + 1, j)


NAMES = ["x", "c", "ada_w", "ada_b", "ln1_g", "ln1_b", "ln2_g", "ln2_b", "ssd_w_in", "ssd_conv_w", "ssd_conv_b",
         "ssd_dt_bias", "ssd_a_log", "ssd_d", "ssd_norm_g", "ssd_w_out", "moe_w_up", "moe_w_down", "router_w", "router_b"]


def kernel(**inputs):
    import concourse.bacc as bacc
    from concourse.bass_utils import run_bass_kernel_spmd

    nc = bacc.Bacc("TRN2", target_bir_lowering=False, num_devices=1)
    arrays, args = {}, []
    for name in NAMES:
        a = np.ascontiguousarray(inputs[name])
        arrays[f"in_{name}"] = a
        args.append(nc.dram_tensor(f"in_{name}", a.shape, mybir.dt.from_np(a.dtype), kind="ExternalInput").ap())
    args.append(nc.dram_tensor("out_y", (1, T, D), F32, kind="ExternalOutput").ap())
    build(nc, *args)
    r = run_bass_kernel_spmd(nc, [arrays], core_ids=[0])
    return r.results[0]["out_y"]
```
